# Optimizing a Trainium2 kernel written in Bass

```python
import jax, jax.numpy as jnp
from jax import lax
import numpy as np

D_MODEL = 1024
BATCH = 1
SEQ = 256
DEPTH = 2

N_MIXERS = 2
HEAD_DIM = 64
ROPE_THETA = 10000.0
NORM_EPS = 1e-6

NSA_HEADS = 16
NSA_KV_HEADS = 4
CMP_LEN = 32
CMP_STRIDE = 16
CMP_HIDDEN = 256
SLC_LEN = 64
SLC_TOPK = 16
WIN_LEN = 512
FORCE_BONUS = 1e4
SLC_Q_CHUNK = 16
NSA_IN_DIM = NSA_HEADS * HEAD_DIM + 6 * NSA_KV_HEADS * HEAD_DIM + 3 * NSA_HEADS

SWA_HEADS = 16
SWA_KV_HEADS = 2
SWA_WINDOW = 128
SWA_IN_DIM = SWA_HEADS * HEAD_DIM + 2 * SWA_KV_HEADS * HEAD_DIM

Q_BLOCK = 128

D_FF = 2816
CONV_WIDTH = 3

N_A = (DEPTH + 1) // 2
N_B = DEPTH // 2


def rms_norm(x, gain):
    xf = x.astype(jnp.float32)
    y = xf * lax.rsqrt(jnp.mean(xf * xf, axis=-1, keepdims=True) + NORM_EPS)
    return (y * gain.astype(jnp.float32)).astype(x.dtype)

def rope_tables(seq):
    pos = jnp.arange(seq, dtype=jnp.float32)
    inv = ROPE_THETA ** (-jnp.arange(0, HEAD_DIM, 2, dtype=jnp.float32) / HEAD_DIM)
    ang = pos[:, None] * inv[None, :]
    return jnp.cos(ang), jnp.sin(ang)

def apply_rope(x, cos, sin):
    c = cos[None, :, None, :].astype(x.dtype)
    s = sin[None, :, None, :].astype(x.dtype)
    x1, x2 = jnp.split(x, 2, axis=-1)
    return jnp.concatenate([x1 * c - x2 * s, x2 * c + x1 * s], axis=-1)

def to_q_groups(q, n_groups):
    b, s, h, d = q.shape
    return q.reshape(b, s, n_groups, h // n_groups, d).transpose(0, 2, 3, 1, 4)

def from_q_groups(o):
    b, g, r, s, d = o.shape
    return o.transpose(0, 3, 1, 2, 4).reshape(b, s, g * r * d)

def masked_softmax(s, mask):
    s = jnp.where(mask, s, -jnp.inf)
    m = jnp.max(s, axis=-1, keepdims=True)
    m = jnp.where(jnp.isfinite(m), m, 0.0)
    p = jnp.exp(s - m)
    d = jnp.sum(p, axis=-1, keepdims=True)
    return p / jnp.where(d > 0.0, d, 1.0)

def banded_attention(q, k, v, window, sinks=None):
    b, g, r, seq, hd = q.shape
    nqb = seq // Q_BLOCK
    span = Q_BLOCK + window
    pad = ((0, 0), (0, 0), (window, 0), (0, 0))
    k_pad = jnp.pad(k, pad)
    v_pad = jnp.pad(v, pad)
    qb = q.reshape(b, g, r, nqb, Q_BLOCK, hd).transpose(3, 0, 1, 2, 4, 5)
    scale = hd ** -0.5

    def block(args):
        blk, q_blk = args
        start = blk * Q_BLOCK
        kb = lax.dynamic_slice_in_dim(k_pad, start, span, axis=2)
        vb = lax.dynamic_slice_in_dim(v_pad, start, span, axis=2)
        qpos = start + jnp.arange(Q_BLOCK)
        kpos = start - window + jnp.arange(span)
        rel = qpos[:, None] - kpos[None, :]
        mask = (rel >= 0) & (rel < window) & (kpos[None, :] >= 0)
        s = jnp.einsum('bgrqd,bgkd->bgrqk', q_blk, kb).astype(jnp.float32) * scale
        if sinks is None:
            p = masked_softmax(s, mask)
        else:
            s = jnp.where(mask, s, -jnp.inf)
            sink = sinks.astype(jnp.float32)[None, :, :, None, None]
            m = jnp.maximum(jnp.max(s, axis=-1, keepdims=True), sink)
            p = jnp.exp(s - m)
            p = p / (jnp.sum(p, axis=-1, keepdims=True) + jnp.exp(sink - m))
        return jnp.einsum('bgrqk,bgkd->bgrqd', p.astype(vb.dtype), vb)

    o = lax.map(block, (jnp.arange(nqb), qb))
    return o.transpose(1, 2, 3, 0, 4, 5).reshape(b, g, r, seq, hd)

def nsa_mixer(h, cos, sin, w_in, cmp_pe, cmp_w1, cmp_w2, gate_b, w_o):
    b, seq, _ = h.shape
    g, r, hd = NSA_KV_HEADS, NSA_HEADS // NSA_KV_HEADS, HEAD_DIM
    sizes = [NSA_HEADS * hd] + [g * hd] * 6 + [3 * NSA_HEADS]
    splits = np.cumsum(sizes)[:-1].tolist()
    q, kc, vc, ks, vs, kw, vw, gt = jnp.split(h @ w_in, splits, axis=-1)

    q = to_q_groups(apply_rope(q.reshape(b, seq, NSA_HEADS, hd), cos, sin), g)

    def kv(t, rotate):
        t = t.reshape(b, seq, g, hd)
        if rotate:
            t = apply_rope(t, cos, sin)
        return t.transpose(0, 2, 1, 3)

    kc, ks, kw = kv(kc, True), kv(ks, True), kv(kw, True)
    vc, vs, vw = kv(vc, False), kv(vs, False), kv(vw, False)
    pos = jnp.arange(seq)
    scale = hd ** -0.5

    n_cmp = (seq - CMP_LEN) // CMP_STRIDE + 1
    cstart = jnp.arange(n_cmp) * CMP_STRIDE
    cidx = cstart[:, None] + jnp.arange(CMP_LEN)[None, :]

    def compress(t, pe, w1, w2):
        blk = (t[:, :, cidx] + pe).reshape(b, g, n_cmp, CMP_LEN * hd)
        return jax.nn.gelu(blk @ w1) @ w2

    kc = compress(kc, cmp_pe[0], cmp_w1[0], cmp_w2[0])
    vc = compress(vc, cmp_pe[1], cmp_w1[1], cmp_w2[1])
    s_cmp = jnp.einsum('bgrqd,bgcd->bgrqc', q, kc).astype(jnp.float32) * scale
    cmask = (cstart + CMP_LEN - 1)[None, :] <= pos[:, None]
    p_cmp = masked_softmax(s_cmp, cmask)
    o_cmp = jnp.einsum('bgrqc,bgcd->bgrqd', p_cmp.astype(vc.dtype), vc)

    n_slc = seq // SLC_LEN
    top_n = min(SLC_TOPK, n_slc)
    sstart = jnp.arange(n_slc) * SLC_LEN
    overlap = ((cstart[:, None] <= sstart[None, :] + SLC_LEN - 1)
               & (cstart[:, None] + CMP_LEN - 1 >= sstart[None, :])).astype(jnp.float32)
    imp = jnp.einsum('bgrqc,cn->bgqn', p_cmp, overlap)
    cur = pos // SLC_LEN
    blk = jnp.arange(n_slc)
    forced = (blk[None, :] == 0) | (blk[None, :] == cur[:, None]) | (blk[None, :] == cur[:, None] - 1)
    causal = blk[None, :] <= cur[:, None]
    score = jnp.where(causal, imp + jnp.where(forced, FORCE_BONUS, 0.0), -1.0)
    top_score, sel = lax.top_k(score, top_n)
    sel_valid = top_score >= 0.0

    nqc = seq // SLC_Q_CHUNK
    q_ch = q.reshape(b, g, r, nqc, SLC_Q_CHUNK, hd).transpose(3, 0, 1, 2, 4, 5)
    sel_ch = sel.reshape(b, g, nqc, SLC_Q_CHUNK, top_n).transpose(2, 0, 1, 3, 4)
    val_ch = sel_valid.reshape(b, g, nqc, SLC_Q_CHUNK, top_n).transpose(2, 0, 1, 3, 4)
    pos_ch = pos.reshape(nqc, SLC_Q_CHUNK)
    gather_rows = jax.vmap(jax.vmap(lambda t, i: t[i]))
    n_keys = top_n * SLC_LEN

    def slc_block(args):
        q_c, sel_c, val_c, qpos = args
        tok = sel_c[..., None] * SLC_LEN + jnp.arange(SLC_LEN)
        tmask = val_c[..., None] & (tok <= qpos[None, None, :, None, None])
        tok = tok.reshape(b, g, SLC_Q_CHUNK, n_keys)
        tmask = tmask.reshape(b, g, SLC_Q_CHUNK, n_keys)
        kg = gather_rows(ks, tok)
        vg = gather_rows(vs, tok)
        s = jnp.einsum('bgrqd,bgqkd->bgrqk', q_c, kg).astype(jnp.float32) * scale
        p = masked_softmax(s, tmask[:, :, None])
        return jnp.einsum('bgrqk,bgqkd->bgrqd', p.astype(vg.dtype), vg)

    o_slc = lax.map(slc_block, (q_ch, sel_ch, val_ch, pos_ch))
    o_slc = o_slc.transpose(1, 2, 3, 0, 4, 5).reshape(b, g, r, seq, hd)

    o_win = banded_attention(q, kw, vw, WIN_LEN)

    gates = jax.nn.sigmoid((gt + gate_b).astype(jnp.float32))
    gates = gates.reshape(b, seq, g, r, 3).transpose(0, 2, 3, 1, 4).astype(q.dtype)
    o = gates[..., 0, None] * o_cmp + gates[..., 1, None] * o_slc + gates[..., 2, None] * o_win
    return from_q_groups(o) @ w_o

def swa_mixer(h, cos, sin, w_qkv, b_qkv, sinks, w_o, b_o):
    b, seq, _ = h.shape
    g, r, hd = SWA_KV_HEADS, SWA_HEADS // SWA_KV_HEADS, HEAD_DIM
    q, k, v = jnp.split(h @ w_qkv + b_qkv, [SWA_HEADS * hd, SWA_HEADS * hd + g * hd], axis=-1)
    q = to_q_groups(apply_rope(q.reshape(b, seq, SWA_HEADS, hd), cos, sin), g)
    k = apply_rope(k.reshape(b, seq, g, hd), cos, sin).transpose(0, 2, 1, 3)
    v = v.reshape(b, seq, g, hd).transpose(0, 2, 1, 3)
    o = banded_attention(q, k, v, SWA_WINDOW, sinks.reshape(g, r))
    return from_q_groups(o) @ w_o + b_o

def causal_depthwise_conv(a, w, bias):
    f = a.shape[-1]
    y = lax.conv_general_dilated(a, w.astype(a.dtype)[:, None, :], window_strides=(1,),
                                 padding=[(CONV_WIDTH - 1, 0)],
                                 dimension_numbers=('NWC', 'WIO', 'NWC'),
                                 feature_group_count=f)
    return y + bias.astype(a.dtype)

def conv_ffn(h, w_gu, conv_w, conv_b, w_down):
    a, u = jnp.split(h @ w_gu, 2, axis=-1)
    a = causal_depthwise_conv(a, conv_w, conv_b)
    return (jax.nn.silu(a) * u) @ w_down

def first_inputs(seed: int = 0) -> dict:
    key = jax.random.key(seed)
    ks = jax.random.split(key, 20)
    f32 = jnp.float32

    def nrm(k, shape, scale):
        return jax.random.normal(k, shape, f32) * scale

    att_w = NSA_HEADS * HEAD_DIM
    swa_w = SWA_HEADS * HEAD_DIM
    return {
        'x': nrm(ks[0], (BATCH, SEQ, D_MODEL), 1.0),
        'nsa_w_in': nrm(ks[1], (N_A, D_MODEL, NSA_IN_DIM), D_MODEL ** -0.5),
        'nsa_cmp_pe': nrm(ks[2], (N_A, 2, CMP_LEN, HEAD_DIM), 0.02),
        'nsa_cmp_w1': nrm(ks[3], (N_A, 2, CMP_LEN * HEAD_DIM, CMP_HIDDEN), (CMP_LEN * HEAD_DIM) ** -0.5),
        'nsa_cmp_w2': nrm(ks[4], (N_A, 2, CMP_HIDDEN, HEAD_DIM), CMP_HIDDEN ** -0.5),
        'nsa_gate_b': nrm(ks[5], (N_A, 3 * NSA_HEADS), 0.1),
        'nsa_w_o': nrm(ks[6], (N_A, att_w, D_MODEL), att_w ** -0.5),
        'swa_w_qkv': nrm(ks[7], (N_B, D_MODEL, SWA_IN_DIM), D_MODEL ** -0.5),
        'swa_b_qkv': nrm(ks[8], (N_B, SWA_IN_DIM), 0.02),
        'swa_sinks': nrm(ks[9], (N_B, SWA_HEADS), 1.0),
        'swa_w_o': nrm(ks[10], (N_B, swa_w, D_MODEL), swa_w ** -0.5),
        'swa_b_o': nrm(ks[11], (N_B, D_MODEL), 0.02),
        'ffn_w_gu': nrm(ks[12], (DEPTH, D_MODEL, 2 * D_FF), D_MODEL ** -0.5),
        'ffn_conv_w': nrm(ks[13], (DEPTH, CONV_WIDTH, D_FF), CONV_WIDTH ** -0.5),
        'ffn_conv_b': nrm(ks[14], (DEPTH, D_FF), 0.02),
        'ffn_w_down': nrm(ks[15], (DEPTH, D_FF, D_MODEL), D_FF ** -0.5),
        'norm_mix': 1.0 + nrm(ks[16], (DEPTH, D_MODEL), 0.02),
        'norm_ffn': 1.0 + nrm(ks[17], (DEPTH, D_MODEL), 0.02),
        'norm_final': 1.0 + nrm(ks[18], (D_MODEL,), 0.02),
    }

def first_block(x, nsa_w_in, nsa_cmp_pe, nsa_cmp_w1, nsa_cmp_w2, nsa_gate_b, nsa_w_o,
              swa_w_qkv, swa_b_qkv, swa_sinks, swa_w_o, swa_b_o,
              ffn_w_gu, ffn_conv_w, ffn_conv_b, ffn_w_down,
              norm_mix, norm_ffn, norm_final):
    cos, sin = rope_tables(x.shape[1])
    for i in range(DEPTH):
        j = i // N_MIXERS
        h = rms_norm(x, norm_mix[i])
        if i % N_MIXERS == 0:
            x = x + nsa_mixer(h, cos, sin, nsa_w_in[j], nsa_cmp_pe[j], nsa_cmp_w1[j],
                              nsa_cmp_w2[j], nsa_gate_b[j], nsa_w_o[j])
        else:
            x = x + swa_mixer(h, cos, sin, swa_w_qkv[j], swa_b_qkv[j], swa_sinks[j],
                              swa_w_o[j], swa_b_o[j])
        h = rms_norm(x, norm_ffn[i])
        x = x + conv_ffn(h, ffn_w_gu[i], ffn_conv_w[i], ffn_conv_b[i], ffn_w_down[i])
    return rms_norm(x, norm_final)


DEPTH_2 = 1

CHUNK = 64
N_META = 16
SB_HEADS = 8
SB_HEAD_DIM = 64
GLA_HEADS = 4
GLA_HEAD_DK = 128
GLA_HEAD_DV = 256
GATE_RANK = 16
GATE_TAU = 16.0
CONV_W = 3
N_BRANCHES = 2
EPS = 1e-6

SB_WIDTH = SB_HEADS * SB_HEAD_DIM
GLA_K_WIDTH = GLA_HEADS * GLA_HEAD_DK
GLA_V_WIDTH = GLA_HEADS * GLA_HEAD_DV
IN_WIDTHS = (SB_WIDTH, SB_WIDTH, SB_WIDTH, GLA_K_WIDTH, GLA_K_WIDTH, GLA_V_WIDTH, GLA_V_WIDTH, GATE_RANK, N_BRANCHES * D_MODEL)
IN_TOTAL = 3 * SB_WIDTH + 2 * GLA_K_WIDTH + 2 * GLA_V_WIDTH + GATE_RANK + N_BRANCHES * D_MODEL


def _rmsnorm(x, g):
    xf = x.astype(jnp.float32)
    y = xf * lax.rsqrt(jnp.mean(xf * xf, axis=-1, keepdims=True) + EPS)
    return (y * g.astype(jnp.float32)).astype(x.dtype)

def _split_cols(a, widths):
    outs, start = [], 0
    for w in widths:
        outs.append(a[..., start:start + w])
        start += w
    return outs

def _heads(a, n_heads):
    b, l, _ = a.shape
    return a.reshape(b, l, n_heads, -1).transpose(0, 2, 1, 3)

def _stick_breaking(q, k, v):
    b, h, lp, dh = q.shape
    nb = lp // Q_BLOCK
    scale = dh ** -0.5
    kpos = jnp.arange(lp)
    qb = q.reshape(b, h, nb, Q_BLOCK, dh).transpose(2, 0, 1, 3, 4)

    def block(args):
        qi, i = args
        z = jnp.einsum('bhqd,bhkd->bhqk', qi, k).astype(jnp.float32) * scale
        qpos = i * Q_BLOCK + jnp.arange(Q_BLOCK)
        strict = kpos[None, :] < qpos[:, None]
        u = jnp.where(strict, jax.nn.log_sigmoid(-z), 0.0)
        tail = lax.cumsum(u, axis=3, reverse=True) - u
        w = jnp.where(strict, jnp.exp(jax.nn.log_sigmoid(z) + tail), 0.0)
        return jnp.einsum('bhqk,bhkd->bhqd', w.astype(v.dtype), v)

    out = lax.map(block, (qb, jnp.arange(nb)))
    return out.transpose(1, 2, 0, 3, 4).reshape(b, h, lp, dh)

def _gla(q, k, v, g):
    b, h, lp, dk = q.shape
    dv = v.shape[-1]
    nc = lp // CHUNK

    def to_chunks(a):
        return a.reshape(b, h, nc, CHUNK, a.shape[-1]).transpose(2, 0, 1, 3, 4)

    qc, kc, vc, gc = to_chunks(q), to_chunks(k), to_chunks(v), to_chunks(g)
    causal = jnp.tril(jnp.ones((CHUNK, CHUNK), dtype=bool))

    def step(state, inp):
        qi, ki, vi, gi = inp
        cum = jnp.cumsum(gi, axis=2)
        diff = cum[:, :, :, None, :] - cum[:, :, None, :, :]
        decay = jnp.exp(jnp.where(causal[None, None, :, :, None], diff, -jnp.inf))
        att = jnp.einsum('bhtd,bhsd,bhtsd->bhts', qi, ki, decay)
        o = jnp.einsum('bhts,bhsv->bhtv', att, vi) + jnp.einsum('bhtd,bhdv->bhtv', qi * jnp.exp(cum), state)
        last = cum[:, :, -1:, :]
        state = jnp.exp(last[:, :, 0, :])[..., None] * state + jnp.einsum('bhsd,bhsv->bhdv', ki * jnp.exp(last - cum), vi)
        return state, o

    state0 = jnp.zeros((b, h, dk, dv), jnp.float32)
    _, oc = lax.scan(step, state0, (qc, kc, vc, gc))
    return oc.transpose(1, 2, 0, 3, 4).reshape(b, h, lp, dv)

def _causal_dwconv(a, w, bias):
    a_p = jnp.pad(a, ((0, 0), (CONV_W - 1, 0), (0, 0)))
    y = lax.conv_general_dilated(a_p, w[:, None, :].astype(a.dtype), window_strides=(1,), padding='VALID',
                                 dimension_numbers=('NWC', 'WIO', 'NWC'), feature_group_count=a.shape[-1])
    return y + bias.astype(a.dtype)

def second_inputs(seed: int = 0) -> dict:
    key = jax.random.key(seed)
    ks = jax.random.split(key, 20)
    f32 = jnp.float32

    def nrm(k, shape, scale):
        return jax.random.normal(k, shape, f32) * scale

    def gain(k, n):
        return 1.0 + 0.02 * jax.random.normal(k, (DEPTH_2, n), f32)

    return {
        "x": nrm(ks[0], (BATCH, SEQ, D_MODEL), 1.0),
        "meta_tokens": nrm(ks[1], (N_META, D_MODEL), 1.0),
        "norm_mix_pre": gain(ks[2], D_MODEL),
        "w_in": nrm(ks[3], (DEPTH_2, D_MODEL, IN_TOTAL), D_MODEL ** -0.5),
        "w_gk_up": nrm(ks[4], (DEPTH_2, GATE_RANK, GLA_K_WIDTH), GATE_RANK ** -0.5),
        "b_gk": nrm(ks[5], (DEPTH_2, GLA_K_WIDTH), 0.1),
        "gla_head_norm": gain(ks[6], GLA_HEAD_DV),
        "w_sb_out": nrm(ks[7], (DEPTH_2, SB_WIDTH, D_MODEL), SB_WIDTH ** -0.5),
        "w_gla_out": nrm(ks[8], (DEPTH_2, GLA_V_WIDTH, D_MODEL), GLA_V_WIDTH ** -0.5),
        "w_o": nrm(ks[9], (DEPTH_2, D_MODEL, D_MODEL), D_MODEL ** -0.5),
        "norm_mix_post": gain(ks[10], D_MODEL),
        "norm_ffn_pre": gain(ks[11], D_MODEL),
        "w_ffn_up": nrm(ks[12], (DEPTH_2, D_MODEL, D_FF), D_MODEL ** -0.5),
        "w_ffn_gate": nrm(ks[13], (DEPTH_2, D_MODEL, D_FF), D_MODEL ** -0.5),
        "conv_w": nrm(ks[14], (DEPTH_2, CONV_W, D_FF), CONV_W ** -0.5),
        "conv_b": nrm(ks[15], (DEPTH_2, D_FF), 0.02),
        "w_ffn_down": nrm(ks[16], (DEPTH_2, D_FF, D_MODEL), D_FF ** -0.5),
        "norm_ffn_post": gain(ks[17], D_MODEL),
    }

def second_block(x, meta_tokens, norm_mix_pre, w_in, w_gk_up, b_gk, gla_head_norm, w_sb_out, w_gla_out, w_o,
              norm_mix_post, norm_ffn_pre, w_ffn_up, w_ffn_gate, conv_w, conv_b, w_ffn_down, norm_ffn_post):
    b, s, _ = x.shape
    L = s + N_META
    Lp = -(-L // Q_BLOCK) * Q_BLOCK
    meta = jnp.broadcast_to(meta_tokens[None].astype(x.dtype), (b, N_META, D_MODEL))
    h = jnp.concatenate([meta, x], axis=1)

    for l in range(DEPTH_2):
        hn = _rmsnorm(h, norm_mix_pre[l])
        hn_p = jnp.pad(hn, ((0, 0), (0, Lp - L), (0, 0)))
        proj = hn_p @ w_in[l]
        sb_q, sb_k, sb_v, g_q, g_k, g_v, g_r, g_lr, merge = _split_cols(proj, IN_WIDTHS)

        sb = _stick_breaking(_heads(sb_q, SB_HEADS), _heads(sb_k, SB_HEADS), _heads(sb_v, SB_HEADS))
        sb = sb.transpose(0, 2, 1, 3).reshape(b, Lp, SB_WIDTH)[:, :L]

        glog = jax.nn.log_sigmoid((g_lr @ w_gk_up[l] + b_gk[l]).astype(jnp.float32)) / GATE_TAU
        gq = _heads(g_q, GLA_HEADS).astype(jnp.float32) * (GLA_HEAD_DK ** -0.5)
        gk = _heads(g_k, GLA_HEADS).astype(jnp.float32)
        gv = _heads(g_v, GLA_HEADS).astype(jnp.float32)
        o = _gla(gq, gk, gv, _heads(glog, GLA_HEADS))
        o = _rmsnorm(o, gla_head_norm[l])
        o = o.transpose(0, 2, 1, 3).reshape(b, Lp, GLA_V_WIDTH)[:, :L].astype(h.dtype)
        o = o * jax.nn.silu(g_r[:, :L])

        gates = jax.nn.sigmoid(merge[:, :L])
        gate_sb, gate_gla = gates[..., :D_MODEL], gates[..., D_MODEL:]
        mix = (gate_sb * (sb @ w_sb_out[l]) + gate_gla * (o @ w_gla_out[l])) @ w_o[l]
        h = h + _rmsnorm(mix, norm_mix_post[l])

        hn = _rmsnorm(h, norm_ffn_pre[l])
        up = hn @ w_ffn_up[l]
        act = jax.nn.gelu(_causal_dwconv(up, conv_w[l], conv_b[l]), approximate=True)
        ffn = (act * (hn @ w_ffn_gate[l])) @ w_ffn_down[l]
        h = h + _rmsnorm(ffn, norm_ffn_post[l])

    return h[:, N_META:]


def setup_inputs(seed=0):
    out = dict(first_inputs(seed))
    for name, value in second_inputs(seed + 1).items():
        if name != "x":
            out[name + "_2"] = value
    return out


def reference(
    x, nsa_w_in, nsa_cmp_pe, nsa_cmp_w1, nsa_cmp_w2, nsa_gate_b, nsa_w_o, swa_w_qkv, swa_b_qkv,
    swa_sinks, swa_w_o, swa_b_o, ffn_w_gu, ffn_conv_w, ffn_conv_b, ffn_w_down, norm_mix,
    norm_ffn, norm_final, meta_tokens_2, norm_mix_pre_2, w_in_2, w_gk_up_2, b_gk_2,
    gla_head_norm_2, w_sb_out_2, w_gla_out_2, w_o_2, norm_mix_post_2, norm_ffn_pre_2,
    w_ffn_up_2, w_ffn_gate_2, conv_w_2, conv_b_2, w_ffn_down_2, norm_ffn_post_2,
):
    x = first_block(
        x, nsa_w_in, nsa_cmp_pe, nsa_cmp_w1, nsa_cmp_w2, nsa_gate_b, nsa_w_o, swa_w_qkv,
        swa_b_qkv, swa_sinks, swa_w_o, swa_b_o, ffn_w_gu, ffn_conv_w, ffn_conv_b, ffn_w_down,
        norm_mix, norm_ffn, norm_final,
    )
    return second_block(
        x, meta_tokens_2, norm_mix_pre_2, w_in_2, w_gk_up_2, b_gk_2, gla_head_norm_2,
        w_sb_out_2, w_gla_out_2, w_o_2, norm_mix_post_2, norm_ffn_pre_2, w_ffn_up_2,
        w_ffn_gate_2, conv_w_2, conv_b_2, w_ffn_down_2, norm_ffn_post_2,
    )


_drawn_inputs = setup_inputs


def setup_inputs(seed=0):
    import zlib

    import numpy as np

    out = dict(_drawn_inputs(seed))
    spreads = {}
    factors = {'nsa_cmp_pe': 4.558,
     'norm_mix': 3.288,
     'gla_head_norm_2': 5.003,
     'norm_mix_post_2': 3.481,
     'norm_ffn_pre_2': 3.195,
     'conv_b_2': 5.111,
     'norm_ffn_post_2': 17.368,
     'swa_b_o': 3.485}
    for name, (base, spread) in spreads.items():
        noise = np.random.default_rng([zlib.crc32(name.encode()), seed]).standard_normal(out[name].shape)
        drawn = base * np.exp(spread * noise) if base else spread * noise
        out[name] = __import__('jax').numpy.asarray(drawn.astype(out[name].dtype))
    for name, factor in factors.items():
        out[name] = (out[name] * factor).astype(out[name].dtype)
    return out
```

```python
import concourse.bass as bass
from concourse import mybir
from contextlib import ExitStack
import numpy as np

F32 = mybir.dt.float32
BF16 = mybir.dt.bfloat16
U32 = mybir.dt.uint32
ALU = mybir.AluOpType
ACT = mybir.ActivationFunctionType
AX = mybir.AxisListType

D, SEQ, META = 1024, 256, 16
T1, T2 = SEQ, SEQ + META
KC = D // 128
DFF = 2816
FC = DFF // 128
HD = 64
EPS = 1e-6
SCALE = HD ** -0.5
NEG = -1e30
NCMP, CSTR, CLEN = 15, 16, 32
GN, GDK = 4, 128
LEVELS = 7
ZW = 272 + 144 + 16

EARLY = {"ident": 128, "ones": 128, "rot": 128, "cos": T1, "sin": T1, "causal": 128, "before": 128, "cmpneg": 2 * NCMP}
LATE = {"sbvalid": ZW, "sbneg": ZW, "tri": 128, "all": 128, "gla": (LEVELS + 1) * 128}


def columns(parts):
    at, out = 0, {}
    for name, width in parts.items():
        out[name] = (at, at + width)
        at += width
    return out, at


def constants():
    p = np.arange(128)
    q = np.arange(128)
    early, n = columns(EARLY)
    e = np.zeros((128, n), np.float32)

    def put(a, cols, name, v):
        a[:, cols[name][0]:cols[name][1]] = v

    put(e, early, "ident", np.eye(128))
    put(e, early, "ones", 1.0 / D)
    rot = np.zeros((128, 128), np.float32)
    for m in range(128):
        if m % 64 < 32:
            rot[m + 32, m] = -1.0
        else:
            rot[m - 32, m] = 1.0
    put(e, early, "rot", rot)
    inv = (np.float32(10000.0) ** (-np.arange(0, HD, 2, dtype=np.float32) / np.float32(HD))).astype(np.float32)
    ang = inv[p % 32][:, None] * np.arange(T1, dtype=np.float32)[None, :]
    put(e, early, "cos", np.cos(ang.astype(np.float32)))
    put(e, early, "sin", np.sin(ang.astype(np.float32)))
    put(e, early, "causal", np.where(q[None, :] <= p[:, None], 0.0, NEG))
    put(e, early, "before", np.where(q[None, :] > p[:, None], 0.0, NEG))
    c = np.arange(NCMP)
    cm = [np.where(c[None, :] * CSTR + CLEN - 1 <= (p + 128 * b)[:, None], 0.0, NEG) for b in range(2)]
    put(e, early, "cmpneg", np.concatenate(cm, 1))

    late, n = columns(LATE)
    l = np.zeros((128, n), np.float32)
    valid = []
    for b in range(3):
        t = np.arange(128 * b, T2)
        s = p + 128 * b
        valid.append((s[:, None] < t[None, :]) & (s[:, None] < T2))
    valid = np.concatenate(valid, 1)
    put(l, late, "sbvalid", valid)
    put(l, late, "sbneg", np.where(valid, 0.0, NEG))
    put(l, late, "tri", np.where(p[:, None] >= q[None, :], -1.0 / SCALE, 0.0))
    put(l, late, "all", -1.0 / SCALE)
    g = [p[:, None] == q[None, :]]
    for i in range(LEVELS):
        b = 1 << i
        g.append((p[:, None] // (2 * b) == q[None, :] // (2 * b)) & (p[:, None] % (2 * b) < b) & (q[None, :] % (2 * b) >= b))
    put(l, late, "gla", np.concatenate(g, 1))
    return e, l


VEC0 = {"g": 9 * KC, "bo": KC, "hn": 2, "bgk": 4, "bqkv": 10, "gb": 1}
VEC_CONV = {"w0": FC, "w1": FC, "w2": FC, "b": FC}


def vector_loads(vec_in, pe_in, meta_in, A):
    at, _ = columns(VEC0)
    loads = []

    def rows(table, r, vector):
        n = vector.shape[0] // 128
        loads.append((vec_in[r:r + n, table, :], vector.rearrange("(c p) -> c p", p=128)))

    gains = [A["norm_mix"][0], A["norm_ffn"][0], A["norm_mix"][1], A["norm_ffn"][1], A["norm_final"],
             A["norm_mix_pre_2"][0], A["norm_mix_post_2"][0], A["norm_ffn_pre_2"][0], A["norm_ffn_post_2"][0]]
    for i, g in enumerate(gains):
        rows(0, at["g"][0] + KC * i, g)
    rows(0, at["bo"][0], A["swa_b_o"][0])
    rows(0, at["hn"][0], A["gla_head_norm_2"][0])
    rows(0, at["bgk"][0], A["b_gk_2"][0])
    rows(0, at["bqkv"][0], A["swa_b_qkv"][0])
    r = at["gb"][0]
    loads.append((vec_in[r:r + 1, 0, 0:48], A["nsa_gate_b"]))
    for table, w, b in ((1, A["ffn_conv_w"][0], A["ffn_conv_b"][0]), (2, A["ffn_conv_w"][1], A["ffn_conv_b"][1]),
                        (3, A["conv_w_2"][0], A["conv_b_2"][0])):
        for k in range(3):
            rows(table, FC * k, w[k])
        rows(table, FC * 3, b)
    for kv in range(2):
        for twice in range(2):
            loads.append((pe_in[:, kv, twice, :], A["nsa_cmp_pe"][0][kv]))
    loads.append((meta_in, A["meta_tokens_2"]))
    return loads


def build(nc, A, out):
    ctx = ExitStack()
    with ctx:
        def sb(name, shape, dt=F32):
            return ctx.enter_context(nc.sbuf_tensor(name, shape, dt))

        def sem(name):
            return ctx.enter_context(nc.semaphore(name))

        ecol, en = columns(EARLY)
        lcol, ln = columns(LATE)
        early = sb("early", [128, en])
        late = sb("late", [128, ln])

        def E(name):
            return early[:, ecol[name][0]:ecol[name][1]]

        def L(name):
            return late[:, lcol[name][0]:lcol[name][1]]

        ident, ones = E("ident"), E("ones")
        ident_b = sb("ident_b", [128, 128], BF16)
        mask_b = sb("mask_b", [128, 256], BF16)
        sbneg_b = sb("sbneg_b", [128, ZW], BF16)
        vcol0, _ = columns(VEC0)
        vcolc, vcn = columns(VEC_CONV)
        vecs = sb("vecs", [128, 4, 128])

        def vec(name, i):
            at = vcol0[name][0] + i
            return vecs[:, 0, at:at + 1]

        ring = sb("ring", [128, 2, 4096])
        xT = sb("xT", [128, KC, T2])
        h2 = sb("h2", [128, KC, T2])
        xg = sb("xg", [128, KC, T2])
        sq = sb("sq", [128, KC, T2])
        rstd = sb("rstd", [128, T2])
        root = sb("root", [128, T2])
        eps_col = sb("eps_col", [128, 1])
        big = sb("big", [128, 52 * T2])
        NW = 14600
        work = sb("work", [128, NW])

        def chunks(T):
            return big[:, 0:(52 * T2 // T) * T].rearrange("p (c t) -> p c t", t=T)

        big1, big2 = chunks(T1), chunks(T2)

        class Carver:
            def __init__(self):
                self.at = 0

            def __call__(self, *shape):
                n = int(np.prod(shape))
                v = work[:, self.at:self.at + n]
                self.at += n
                assert self.at <= NW, self.at
                if len(shape) == 2:
                    return v.rearrange("p (a b) -> p a b", b=shape[1])
                if len(shape) == 3:
                    return v.rearrange("p (a b c) -> p a b c", b=shape[1], c=shape[2])
                return v

        bank = [ctx.enter_context(nc.psum_tensor(f"bank{i}", [128, 512], F32)) for i in range(8)]

        x_in = big[:, 0:2048].rearrange("p (b n) -> p b n", b=2)
        vec_in = big[:, 2048:2560].rearrange("p (v n) -> p v n", v=4)
        pe_in = big[0:32, 2560:2816].rearrange("p (k u d) -> p k u d", k=2, u=2)
        meta_in = big[0:META, 2816:3840]

        vec_loads = vector_loads(vec_in, pe_in, meta_in, A)
        VEC_DMAS, SMALL_DMAS = len(vec_loads), 4

        cv = Carver()
        xs, tcos, tsin = cv(2, T1), cv(2, T1), cv(2, T1)
        vtok = cv(2, 2, 256)
        S_p, S_pt = cv(2, 512), cv(2, 512)
        st_mx, st_neg, st_den, st_r, st_es = cv(2, 4), cv(2, 4), cv(2, 4), cv(2, 4), cv(2, 4)
        sinks, nsinks = cv(16), cv(16)
        pe_dup = cv(2, CLEN)
        w2k_sb, w2v_sb = cv(2, 128), cv(2, HD)
        gates = cv(2, 48)
        egate = cv(2, 48)
        blkT = cv(2, 16, 60)
        hidT = cv(2, 2, 60)
        kcT = cv(2, 60)
        vc_rep = cv(256)
        c_s, c_e = cv(32, NCMP), cv(32, NCMP)
        c_mx, c_den = cv(32), cv(32)
        c_p = cv(32, 32)
        c_pt = cv(2, 4, 128)
        f_a, f_u, f_c1, f_c2, f_c3, f_s = cv(2, T2 + 2), cv(2, T2), cv(2, T2), cv(2, T2), cv(2, T2), cv(2, T2)
        cv = Carver()
        glr = cv(T2)
        up_sb = cv(512)
        sv_tok = cv(3, 512)
        kpad = cv(4, 128)
        sb_end = cv.at
        z_a, z_r, z_l, z_u, z_w = cv(2, ZW), cv(2, ZW), cv(2, ZW), cv(2, ZW), cv(2, ZW)
        cv.at = sb_end - 512 - 1536
        gv_tok = cv(3, 1024)
        cum = cv(GN, T2)
        g_d, g_q, g_k = cv(2, GN * T2), cv(2, GN * T2), cv(2, GN * T2)
        att = cv(2, GN, 128)
        att2 = cv(GN, 16)
        g_tmp = cv(2, T2)
        kdT = g_q[:, 1, 0:1024].rearrange("p (c k) -> p c k", c=2)
        s1 = g_k[:, 1, 0:1024].rearrange("p (n v) -> p n v", n=GN)
        s2 = g_d[:, 0, 0:1024].rearrange("p (n v) -> p n v", n=GN)

        early_loaded, x_loaded, vec_loaded, small_loaded, late_loaded = map(sem, (
            "early_loaded", "x_loaded", "vec_loaded", "small_loaded", "late_loaded"))
        ring_loaded = [sem("ring_loaded0"), sem("ring_loaded1")]
        out_stored = sem("out_stored")
        proj_done, proj_taken, down_part = map(sem, ("proj_done", "proj_taken", "down_part"))
        xg_ready, sq_ready, ss_done, root_ready = map(sem, ("xg_ready", "sq_ready", "ss_done", "root_ready"))
        turn_done, turn_taken = sem("turn_done"), sem("turn_taken")
        prepared = sem("prepared")
        biased = sem("biased")
        perm_done, cos_done, sin_done, roped = map(sem, ("perm_done", "cos_done", "sin_done", "roped"))
        vt_done, vt_taken = sem("vt_done"), sem("vt_taken")
        gate_moved, gate_exp, gates_ready = map(sem, ("gate_moved", "gate_exp", "gates_ready"))
        blk_ready, cmp_hid, cmp_act, cmp_kv, cmp_kv_taken = map(sem, (
            "blk_ready", "cmp_hid", "cmp_act", "cmp_kv", "cmp_kv_taken"))
        cmp_scores, cmp_centered, cmp_exp, cmp_probs, cmp_turned, cmp_pt = map(sem, (
            "cmp_scores", "cmp_centered", "cmp_exp", "cmp_probs", "cmp_turned", "cmp_pt"))
        at_scores, at_neg, at_exp, at_r, at_probs, at_turned, at_pt, at_pv, at_out = map(sem, (
            "at_scores", "at_neg", "at_exp", "at_r", "at_probs", "at_turned", "at_pt", "at_pv", "at_out"))
        at_sink, at_sinkexp = sem("at_sink"), sem("at_sinkexp")
        c1_ready, conv_mid, conv_ready, act_ready, hidden_ready = map(sem, (
            "c1_ready", "conv_mid", "conv_ready", "act_ready", "hidden_ready"))
        h2_ready = sem("h2_ready")
        kpad_ready, up_loaded, state2 = sem("kpad_ready"), sem("up_loaded"), sem("state2")
        z_scores, z_abs, z_relu, z_ln, z_soft, z_tri, z_weights, z_pv, z_out = map(sem, (
            "z_scores", "z_abs", "z_relu", "z_ln", "z_soft", "z_tri", "z_weights", "z_pv", "z_out"))
        g_log, g_x, g_abs, g_ln, g_cum = map(sem, ("g_log", "g_x", "g_abs", "g_ln", "g_cum"))
        g_dist, g_decay, g_qk, g_att, g_sel = map(sem, ("g_dist", "g_decay", "g_qk", "g_att", "g_sel"))
        k_dist, k_decay, k_dec, k_turned, k_tok, q_decay, q_dec = map(sem, (
            "k_dist", "k_decay", "k_dec", "k_turned", "k_tok", "q_decay", "q_dec"))
        s_done, s_taken, go_done, go_taken, go_sq, go_ss, go_root, go_ready = map(sem, (
            "s_done", "s_taken", "go_done", "go_taken", "go_sq", "go_ss", "go_root", "go_ready"))
        mix_ready, y_turned, y_taken = sem("mix_ready"), sem("y_turned"), sem("y_taken")

        def rows(w):
            return w.rearrange("(k p) n -> p k n", p=128)

        def slot(s, k, n):
            return ring[:, s, 0:k * n].rearrange("p (k n) -> p k n", n=n)

        slabs, release, loaded = [], [], []
        per_slot = [0, 0]
        tally = {"chunk": 0, "part": 0, "hid": 0}

        def slab(parts, chunks_after=0, part=False, hid=False):
            s = len(slabs) % 2
            slabs.append([(dst(s), src) for dst, src in parts])
            per_slot[s] += 16 * len(parts)
            loaded.append(per_slot[s])
            tally["chunk"] += chunks_after
            if part:
                tally["part"] += 1
                release.append((down_part, tally["part"]))
            elif hid:
                tally["hid"] += 1
                release.append((cmp_hid, tally["hid"]))
            else:
                release.append((proj_done, tally["chunk"]))

        def plain(w, c0, c1, k=KC):
            return [(lambda s: slot(s, k, c1 - c0), rows(w)[:, :, c0:c1])]

        def down_slabs(w):
            for g in range(2):
                for k0, k1 in ((0, 8), (8, 16), (16, 22)):
                    src = rows(w)[:, k0:k1, g * 512:(g + 1) * 512]
                    slab([(lambda s, k=k1 - k0: slot(s, k, 512), src)], 4 if k1 == 22 else 0, part=k1 != 22)

        def updown(wg, wu, wd):
            at = len(slabs)
            for m in range(FC // 2):
                cols = slice(256 * m, 256 * m + 256)
                slab([(lambda s: slot(s, KC, 512)[:, :, 0:256], rows(wg)[:, :, cols]),
                      (lambda s: slot(s, KC, 512)[:, :, 256:512], rows(wu)[:, :, cols])], 4)
            down_slabs(wd)
            return at

        w_in = A["nsa_w_in"][0]
        for c0 in (1024, 1536, 2048):
            slab(plain(w_in, c0, c0 + 512), 4)
        slab(plain(w_in, 2560, 2608), 1)
        for c0 in (0, 512):
            slab(plain(w_in, c0, c0 + 512), 4)
        for kv in range(2):
            slab([(lambda s: slot(s, 16, 256), A["nsa_cmp_w1"][0][kv].rearrange("(k p) n -> p k n", p=128))], hid=True)
        for c0 in (0, 512):
            slab(plain(A["nsa_w_o"][0], c0, c0 + 512), 4)
        gu = A["ffn_w_gu"]
        ffn_at = [updown(gu[0][:, 0:DFF], gu[0][:, DFF:2 * DFF], A["ffn_w_down"][0])]
        w_qkv = A["swa_w_qkv"][0]
        slab(plain(w_qkv, 1024, 1280), 2)
        for c0 in (0, 512):
            slab(plain(w_qkv, c0, c0 + 512), 4)
        for c0 in (0, 512):
            slab(plain(A["swa_w_o"][0], c0, c0 + 512), 4)
        ffn_at.append(updown(gu[1][:, 0:DFF], gu[1][:, DFF:2 * DFF], A["ffn_w_down"][1]))
        w2_in = A["w_in_2"][0]
        for c0 in range(0, 4608, 512):
            slab(plain(w2_in, c0, c0 + 512), 4)
        slab(plain(w2_in, 4608, 4624), 1)
        for c0 in range(4624, 6672, 512):
            slab(plain(w2_in, c0, c0 + 512), 4)
        slab([(lambda s: slot(s, 4, 1024), rows(A["w_sb_out_2"][0]))], 8)
        for w in (A["w_gla_out_2"][0], A["w_o_2"][0]):
            for c0 in (0, 512):
                slab(plain(w, c0, c0 + 512), 4)
        ffn_at.append(updown(A["w_ffn_up_2"][0], A["w_ffn_gate_2"][0], A["w_ffn_down_2"][0]))
        ups = [(gu[0][:, 0:DFF], gu[0][:, DFF:2 * DFF]), (gu[1][:, 0:DFF], gu[1][:, DFF:2 * DFF]),
               (A["w_ffn_up_2"][0], A["w_ffn_gate_2"][0])]
        N_NSA = 0
        N_NSA_O = 21
        N_FFN = [29, 29 + 52 + 10 + 8, 0]
        N_SWA = N_FFN[0] + 52
        N_SWA_O = N_SWA + 10
        N_IN2 = N_FFN[1] + 52
        N_SBO = N_IN2 + 36 + 1 + 16
        N_GLO = N_SBO + 8
        N_WO2 = N_GLO + 8
        N_FFN[2] = N_WO2 + 8

        class Line:
            def __init__(self, eng, own):
                self.eng, self.own, self.count, self.last = eng, own, {}, None

            def put(self, ins, signal=None):
                s = self.own if signal is None else signal
                self.count[id(s)] = self.count.get(id(s), 0) + 1
                ins.then_inc(s, 1)
                self.last = (s, self.count[id(s)])

            def skip(self, signal, n):
                self.count[id(signal)] = self.count.get(id(signal), 0) + n
                self.last = (signal, self.count[id(signal)])

            def settle(self):
                self.eng.wait_ge(*self.last)

        act_step, dve_step, pool_step = sem("act_step"), sem("dve_step"), sem("pool_step")

        def each(ap, n, axis=1):
            v = ap.unsqueeze(axis)
            return v.broadcast_to([*v.shape[:axis], n, *v.shape[axis + 1:]])

        NSA = [(8, 1), (9, 1), (10, 0), (11, 0), (12, 1), (13, 1), (14, 0), (15, 0), (16, 1), (17, 1), (18, 0), (19, 0),
               (20, 0)] + [(i, 1) for i in range(8)]
        SWA = [(12, 1), (9, 0)] + [(i, 1) for i in range(8)]
        NSA_OUT, SWA_OUT, K_AT = 22, 10, 30
        KEYS = {12: 0, 13: 2, 16: 4, 17: 6}
        NSA_ROPED, SWA_ROPED = 14, 9
        NSA_UNITS = [(ci, kind) for ci in range(8) for kind in ("first", "second0", "second1")]
        SWA_UNITS = [(ci, kind) for ci in range(8) for kind in ("first", "second")]
        V_SWA = len(NSA_UNITS)

        block = ctx.enter_context(nc.Block())

        @block.sync
        def _(sp):
            def issue(n):
                if n >= 2:
                    sp.wait_ge(*release[n - 2])
                for dst, src in slabs[n]:
                    sp.dma_start(dst, src).then_inc(ring_loaded[n % 2], 16)

            def issue_ffn(l):
                at = ffn_at[l]
                a, u = ups[l]
                issue_up(at, a, u, 0, static=True)
                with sp.Fori(0, (FC // 2 - 1) // 2) as i:
                    for j in (1, 2):
                        sp.wait_ge(proj_done, i * 8 + (N_FFN[l] + 4 * (j - 1)))
                        for half, w in enumerate((a, u)):
                            sp.dma_start(slot((at + j) % 2, KC, 512)[:, :, 256 * half:256 * half + 256],
                                         rows(w)[:, :, bass.ds(i * 512 + 256 * j, 256)])\
                              .then_inc(ring_loaded[(at + j) % 2], 16)
                for n in range(at + FC // 2, at + FC // 2 + 6):
                    issue(n)

            def issue_up(at, a, u, m, static):
                sp.wait_ge(*release[at - 2])
                for half, w in enumerate((a, u)):
                    sp.dma_start(slot(at % 2, KC, 512)[:, :, 256 * half:256 * half + 256],
                                 rows(w)[:, :, 0:256]).then_inc(ring_loaded[at % 2], 16)

            n = 0
            for l in range(3):
                while n < ffn_at[l]:
                    issue(n)
                    n += 1
                issue_ffn(l)
                n = ffn_at[l] + FC // 2 + 6
            assert n == len(slabs)
            o_sb = big[:, 0:2048].rearrange("p (b n) -> p b n", b=2)
            for tb in range(2):
                sp.wait_ge(y_taken, 2 * tb + 2)
                sp.dma_start(out[0][128 * tb:128 * tb + 128, :], o_sb[:, tb, :]).then_inc(out_stored, 16)
            sp.wait_ge(out_stored, 32)

        @block.tensor
        def _(pe):
            mm = nc.tensor.matmul
            line = {"n": 0, "slab": 0}

            def arrived(n):
                pe.wait_ge(ring_loaded[n % 2], loaded[n])

            def chunk(pairs, M, T, b=None):
                n = line["n"]
                b = n % 4 if b is None else b
                if n >= 4:
                    pe.wait_ge(proj_taken, n - 3)
                for i, (w, x) in enumerate(pairs):
                    last = mm(bank[b][0:M, 0:T], w, x, start=i == 0, stop=i == len(pairs) - 1)
                last.then_inc(proj_done, 1)
                line["n"] += 1

            def turn(ins, signal):
                for dst, src in ins:
                    k = src.shape[0]
                    last = nc.tensor.transpose(dst, src, ident[0:k, 0:k])
                last.then_inc(signal, 1)

            def sum_squares(i, T, c0, c1):
                for c in range(c0, c1):
                    pe.wait_ge(sq_ready, 8 * i + c + 1)
                    last = mm(bank[7][:, 0:T], ones, sq[:, c, 0:T], start=c == 0, stop=c == 7)
                if c1 == 8:
                    last.then_inc(ss_done, 1)

            def xg_all(i):
                pe.wait_ge(xg_ready, 8 * (i + 1))

            pe.wait_ge(early_loaded, 16)
            pe.wait_ge(vec_loaded, 16 * VEC_DMAS)
            pe.wait_ge(prepared, 2)
            turn([(bank[4][:, 128 * v:128 * v + 128], vec_in[:, v, :]) for v in range(4)], turn_done)
            turn([(bank[5][:, 32 * k:32 * k + 32], pe_in[:, k, :, :].rearrange("p u d -> p (u d)")) for k in range(2)],
                 turn_done)
            turn([(bank[6][:, 16 * c:16 * c + 16], meta_in[:, 128 * c:128 * c + 128]) for c in range(8)], turn_done)
            pe.wait_ge(x_loaded, 32)
            for b in range(4):
                turn([(bank[b][:, 256 * c + 128 * tb:256 * c + 128 * tb + 128],
                          x_in[:, tb, 128 * (2 * b + c):128 * (2 * b + c) + 128]) for c in range(2) for tb in range(2)],
                     turn_done)
            sum_squares(0, T1, 0, 8)
            xg_all(0)
            pe.wait_ge(turn_taken, 7)

            rope = {"k": 0}

            def permute(after):
                k = rope["k"]
                pe.wait_ge(*after)
                if k >= 2:
                    pe.wait_ge(sin_done, k - 1)
                mm(bank[4 + k % 2][:, 0:T1], E("rot"), xs[:, k % 2, :], start=True, stop=True).then_inc(perm_done, 1)
                rope["k"] += 1

            def nsa_pairs(n, s):
                w = slot(s % 2, KC, 48 if n == 12 else 512)
                if n == 12:
                    return [(w[:, k, :], xg[:, k, 0:T1]) for k in range(KC)], 48
                c = 128 * ((n if n < 12 else n - 13) % 4)
                return [(w[:, k, c:c + 128], xg[:, k, 0:T1]) for k in range(KC)], 128

            for n in range(21):
                s = n // 4 if n < 13 else 4 + (n - 13) // 4
                if n in (0, 4, 8, 12, 13, 17):
                    arrived(s)
                pairs, M = nsa_pairs(n, s)
                chunk(pairs, M, T1)
                if n >= 1 and NSA[n - 1][1]:
                    permute((proj_taken, n))
                if n == 13:
                    pe.wait_ge(proj_taken, 12)
                    for w in range(2):
                        turn([(bank[6 + w][:, 256 * kb + 128 * j:256 * kb + 128 * j + 128],
                                      big1[:, 14 + 4 * w + j, 128 * kb:128 * kb + 128]) for kb in range(2) for j in range(2)],
                             vt_done)
                if n == 15:
                    pe.wait_ge(gate_moved, 1)
                    pe.wait_ge(vt_taken, 1)
                    turn([(bank[6][:, 48 * qb:48 * qb + 48], big1[0:48, 20, 128 * qb:128 * qb + 128]) for qb in range(2)],
                         vt_done)
            permute((proj_taken, 21))

            pe.wait_ge(proj_taken, 21)
            for kv in range(2):
                arrived(6 + kv)
                pe.wait_ge(blk_ready, 8 * kv + 8)
                w1 = slot(kv % 2, 16, 256)
                for hc in range(2):
                    for p in range(16):
                        last = mm(bank[2][:, 120 * kv + 60 * hc:120 * kv + 60 * hc + 60], w1[:, p, 128 * hc:128 * hc + 128],
                                  blkT[:, kv, p, :], start=p == 0, stop=p == 15)
                last.then_inc(cmp_hid, 1)
            pe.wait_ge(cmp_act, 1)
            pe.wait_ge(small_loaded, 16 * SMALL_DMAS)
            for hc in range(2):
                mm(bank[3][:, 0:60], w2k_sb[:, hc, :], hidT[:, 0, hc, :], start=hc == 0, stop=hc == 1)
            for g in range(4):
                for hc in range(2):
                    last = mm(bank[3][0:NCMP, 64 + 64 * g:128 + 64 * g], hidT[:, 1, hc, NCMP * g:NCMP * g + NCMP],
                              w2v_sb[:, hc, :], start=hc == 0, stop=hc == 1)
            last.then_inc(cmp_kv, 1)
            pe.wait_ge(cmp_kv_taken, 6)
            pe.wait_ge(roped, NSA_ROPED)

            def q_of(ci, qb):
                return big1[:, ci, 128 * qb:128 * qb + 128]

            for qb in range(2):
                for h in range(16):
                    g, a = h // 4, h % 2
                    c = NCMP * (16 * qb + h)
                    last = mm(bank[2][:, c:c + NCMP], q_of(h // 2, qb), kcT[:, a, NCMP * g:NCMP * g + NCMP],
                              start=True, stop=True, skip_group_check=True)
            last.then_inc(cmp_scores, 1)

            def cmp_turn():
                pe.wait_ge(cmp_probs, 1)
                pe.wait_ge(vt_taken, 3)
                for qb in range(2):
                    turn([(bank[6 + qb][:, 128 * hg:128 * hg + 128],
                                   c_p[:, 16 * qb + 4 * hg:16 * qb + 4 * hg + 4, :].rearrange("p h c -> p (h c)"))
                                  for hg in range(4)], cmp_turned)

            def unit_scores(v, u, nsa):
                ci, kind = u
                if v >= 2:
                    pe.wait_ge(at_exp, v - 1)
                S = bank[4 + v % 2]
                causal, before = mask_b[:, 128:256], mask_b[:, 0:128]
                if nsa:
                    ks = [[big1[:, K_AT + 2 * (4 * b + ci // 2) + a, :] for a in range(2)] for b in range(2)]
                    if kind == "first":
                        mm(S[:, :], ident_b[:, :], each(causal, 4), start=True, stop=False, skip_group_check=True)
                        for a in range(2):
                            for b in range(2):
                                o = 256 * a + 128 * b
                                last = mm(S[:, o:o + 128], q_of(ci, 0), ks[b][a][:, 0:128],
                                          start=False, stop=True, skip_group_check=True)
                    else:
                        a = int(kind[-1])
                        mm(S[:, :].rearrange("p (b k) -> p b k", b=2)[:, :, 128:256], ident_b[:, :], each(causal, 2),
                           start=True, stop=False, skip_group_check=True)
                        for b in range(2):
                            last = mm(S[:, 256 * b:256 * b + 256], q_of(ci, 1), ks[b][a],
                                      start=False, stop=True, skip_group_check=True)
                else:
                    k = [big1[:, K_AT + 2 * (ci // 4) + a, :] for a in range(2)]
                    if kind == "first":
                        mm(S[:, 0:256], ident_b[:, :], each(causal, 2), start=True, stop=False, skip_group_check=True)
                        for a in range(2):
                            last = mm(S[:, 128 * a:128 * a + 128], q_of(ci, 0), k[a][:, 0:128],
                                      start=False, stop=True, skip_group_check=True)
                    else:
                        mm(S[:, :], ident_b[:, :], each(mask_b[:, :], 2), start=True, stop=False, skip_group_check=True)
                        for a in range(2):
                            last = mm(S[:, 256 * a:256 * a + 256], q_of(ci, 1), k[a],
                                      start=False, stop=True, skip_group_check=True)
                last.then_inc(at_scores, 1)

            def unit_turn(v, u, nsa):
                pe.wait_ge(at_probs, v + 1)
                if v >= 2:
                    pe.wait_ge(at_pt, v - 1)
                n = 2 if not nsa and u[1] == "first" else 4
                turn([(bank[6 + v % 2][:, 128 * i:128 * i + 128], S_p[:, v % 2, 128 * i:128 * i + 128])
                         for i in range(n)], at_turned)

            def unit_pv(v, u, nsa, c0):
                ci, kind = u
                pe.wait_ge(at_pt, v + 1)
                if kind == "first" and c0 + ci >= 2:
                    pe.wait_ge(at_out, c0 + ci - 1)
                O = bank[ci % 2]

                def piece(a, qb, i, w, kb, g, first=False):
                    return mm(O[64 * a:64 * a + 64, 128 * qb:128 * qb + 128], vtok[:, w, kb, 64 * g:64 * g + 64],
                              S_pt[:, v % 2, 128 * i:128 * i + 128], start=first, stop=True, skip_group_check=True)

                if nsa:
                    g = ci // 2
                    if kind == "first":
                        for a in range(2):
                            r = (2 * ci + a) % 4
                            mm(O[64 * a:64 * a + 64, 0:256], vc_rep[32 * r:32 * r + NCMP, 64 * g:64 * g + 64],
                               c_pt[32 * r:32 * r + NCMP, :, g, :], start=True, stop=False, skip_group_check=True)
                            for b in range(2):
                                last = piece(a, 0, 2 * a + b, b, 0, g)
                    else:
                        a = int(kind[-1])
                        for b in range(2):
                            for kb in range(2):
                                last = piece(a, 1, 2 * b + kb, b, kb, g)
                elif kind == "first":
                    for a in range(2):
                        last = piece(a, 0, a, 0, 0, ci // 4, first=True)
                else:
                    for a in range(2):
                        for kb in range(2):
                            last = piece(a, 1, 2 * a + kb, 0, kb, ci // 4)
                last.then_inc(at_pv, 1)

            def attention(units, v0, nsa, c0):
                for i in range(len(units) + 2):
                    if i < len(units):
                        unit_scores(v0 + i, units[i], nsa)
                    if nsa and i == 1:
                        cmp_turn()
                        pe.wait_ge(cmp_pt, 2)
                    if 1 <= i <= len(units):
                        unit_turn(v0 + i - 1, units[i - 1], nsa)
                    if i >= 2:
                        unit_pv(v0 + i - 2, units[i - 2], nsa, c0)

            attention(NSA_UNITS, 0, True, 0)

            def out_proj(slab0, src, ready, T, norm, K=KC):
                pe.wait_ge(*ready)
                for c in range(8):
                    if c % 4 == 0:
                        arrived(slab0 + c // 4)
                    w = slot((slab0 + c // 4) % 2, K, 512)
                    chunk([(w[:, k, 128 * (c % 4):128 * (c % 4) + 128], src[:, k, 0:T]) for k in range(K)], 128, T)
                    if norm is not None and c >= 2:
                        sum_squares(norm, T, c - 2, c - 1)
                if norm is not None:
                    sum_squares(norm, T, 6, 8)

            def ffn(l, T, norm):
                at, n0 = ffn_at[l], N_FFN[l]
                assert line["n"] == n0, (line["n"], n0)
                pe.wait_ge(proj_taken, n0)

                def up(s, target, n):
                    pe.wait_ge(ring_loaded[s], target)
                    for q in range(4):
                        pe.wait_ge(proj_taken, n + q - 3)
                        c = 256 * (q % 2) + 128 * (q // 2)
                        for k in range(KC):
                            last = mm(bank[q][:, 0:T], slot(s, KC, 512)[:, k, c:c + 128], xg[:, k, 0:T],
                                      start=k == 0, stop=k == KC - 1)
                        last.then_inc(proj_done, 1)

                up(at % 2, loaded[at], n0)
                with pe.Fori(0, (FC // 2 - 1) // 2) as i:
                    for j in (1, 2):
                        up((at + j) % 2, i * 32 + loaded[at + j], i * 8 + (n0 + 4 * j))
                line["n"] += 4 * (FC // 2)
                for g in range(2):
                    for part, (k0, k1) in enumerate(((0, 8), (8, 16), (16, 22))):
                        s = at + FC // 2 + 3 * g + part
                        arrived(s)
                        pe.wait_ge(hidden_ready, FC * l + k1)
                        w = slot(s % 2, k1 - k0, 512)
                        for c in range(4):
                            n = line["n"] + c
                            if part == 0:
                                pe.wait_ge(proj_taken, n - 3)
                            for k in range(k0, k1):
                                last = mm(bank[c][:, 0:T], w[:, k - k0, 128 * c:128 * c + 128],
                                          (big2 if T == T2 else big1)[:, k, :], start=k == 0, stop=k == FC - 1)
                            if part == 2:
                                last.then_inc(proj_done, 1)
                                if g and c == 0:
                                    sum_squares(norm, T, 0, 4)
                        if part < 2:
                            last.then_inc(down_part, 1)
                    line["n"] += 4
                sum_squares(norm, T, 4, 8)

            out_proj(8, big1[:, NSA_OUT:NSA_OUT + 8, :], (at_out, 8), T1, 1)
            xg_all(1)
            ffn(0, T1, 2)

            xg_all(2)
            s0 = ffn_at[0] + 17
            for n in range(10):
                if n in (0, 2, 6):
                    arrived(s0 + (n + 2) // 4)
                if n < 2:
                    w = slot(s0 % 2, KC, 256)
                    pairs = [(w[:, k, 128 * n:128 * n + 128], xg[:, k, 0:T1]) for k in range(KC)]
                else:
                    w = slot((s0 + (n + 2) // 4) % 2, KC, 512)
                    c = 128 * ((n - 2) % 4)
                    pairs = [(w[:, k, c:c + 128], xg[:, k, 0:T1]) for k in range(KC)]
                chunk(pairs, 128, T1)
                if n >= 1 and SWA[n - 1][1]:
                    permute((biased, n))
                if n == 3:
                    pe.wait_ge(biased, 2)
                    turn([(bank[6][:, 128 * kb:128 * kb + 128], big1[:, 9, 128 * kb:128 * kb + 128]) for kb in range(2)],
                         vt_done)
            permute((biased, 10))
            pe.wait_ge(roped, NSA_ROPED + SWA_ROPED)
            pe.wait_ge(vt_taken, 4)
            pe.wait_ge(proj_taken, N_SWA + 10)
            attention(SWA_UNITS, V_SWA, False, 8)
            out_proj(s0 + 3, big1[:, SWA_OUT:SWA_OUT + 8, :], (at_out, 16), T1, 3)
            xg_all(3)
            ffn(1, T1, 4)

            sum_squares(5, T2, 0, 8)
            xg_all(5)
            s0 = ffn_at[1] + 17
            for n in range(53):
                s = s0 + (n // 4 if n < 36 else 9 if n == 36 else 10 + (n - 37) // 4)
                c = n % 4 if n < 36 else (n - 37) % 4
                if n == 36 or c == 0:
                    arrived(s)
                w = slot(s % 2, KC, 16 if n == 36 else 512)
                if n == 36:
                    chunk([(w[:, k, :], xg[:, k, :]) for k in range(KC)], 16, T2)
                else:
                    chunk([(w[:, k, 128 * c:128 * c + 128], xg[:, k, :]) for k in range(KC)], 128, T2)

            pe.wait_ge(proj_taken, N_IN2 + 53)
            for tb in range(3):
                w = min(128, T2 - 128 * tb)
                turn([(bank[4 + tb][0:w, 128 * c:128 * c + 128], big2[:, 8 + c, 128 * tb:128 * tb + w])
                              for c in range(4)], vt_done)
            pe.wait_ge(vt_taken, 4 + 3)
            pe.wait_ge(kpad_ready, 1)
            Z = [bank[0], bank[1], bank[4], bank[5]]
            parts = [(0, 0, T2), (1, 272, 144), (2, 416, 16)]

            def z_score(i):
                if i >= 4:
                    pe.wait_ge(z_weights, i - 3)
                c, a = i // 2, i % 2
                for b, at, w in parts:
                    k = kpad[64 * a:64 * a + 64, c, :] if b == 2 else big2[64 * a:64 * a + 64, 4 + c, 128 * b:128 * b + 128]
                    last = mm(Z[i % 4][:, at:at + w], k, big2[64 * a:64 * a + 64, c, T2 - w:T2], start=b == 0, stop=True,
                              skip_group_check=True)
                last.then_inc(z_scores, 1)

            def z_sum(i):
                pe.wait_ge(z_soft, i + 1)
                for b, at, w in parts:
                    for b2, at2, w2 in parts[b:]:
                        last = mm(Z[i % 4][:, at + w - w2:at + w], L("tri") if b2 == b else L("all"),
                                  z_u[:, i % 2, at2:at2 + w2], start=False, stop=True, skip_group_check=True)
                mm(Z[i % 4][:, 0:ZW], ident_b[:, :], sbneg_b[:, :], start=False, stop=True, skip_group_check=True)\
                    .then_inc(z_tri, 1)

            def z_value(i):
                pe.wait_ge(z_weights, i + 1)
                c, a = i // 2, i % 2
                if a == 0 and c >= 2:
                    pe.wait_ge(z_out, c - 1)
                for b, at, w in parts:
                    n = 16 if b == 2 else 128
                    last = mm(bank[2 + c % 2][64 * a:64 * a + 64, T2 - w:T2], sv_tok[0:n, b, 64 * i:64 * i + 64],
                              z_w[0:n, i % 2, at:at + w], start=b == 0, stop=True, skip_group_check=True)
                last.then_inc(z_pv, 1)

            for i in range(8 + 2):
                if i < 8:
                    z_score(i)
                if 1 <= i <= 8:
                    z_sum(i - 1)
                if i >= 2:
                    z_value(i - 2)

            pe.wait_ge(z_weights, 8)
            pe.wait_ge(z_out, 4)
            pe.wait_ge(up_loaded, 16)
            for n in range(GN):
                last = mm(bank[n][:, 0:T2], up_sb[0:16, 128 * n:128 * n + 128], glr[0:16, :], start=True, stop=True)
            last.then_inc(g_log, 1)
            for tb in range(3):
                w = min(128, T2 - 128 * tb)
                for half in range(2):
                    i = 2 * tb + half
                    if i >= 4:
                        pe.wait_ge(vt_taken, 7 + i - 3)
                    turn([(bank[4 + i % 4][0:w, 128 * c:128 * c + 128], big2[:, 20 + 4 * half + c, 128 * tb:128 * tb + w])
                             for c in range(4)], vt_done)

            def level(lv):
                if lv == 0:
                    pe.wait_ge(g_x, GN)
                    pe.wait_ge(vt_taken, 7 + 6)
                    q, k = big2[:, 12:16, :], big2[:, 16:20, :]
                else:
                    pe.wait_ge(g_qk, lv)
                    q = g_q[:, lv % 2, :].rearrange("p (n t) -> p n t", n=GN)
                    k = g_k[:, lv % 2, :].rearrange("p (n t) -> p n t", n=GN)
                if lv >= 2:
                    pe.wait_ge(g_sel, lv - 1)
                for ck in range(2):
                    for n in range(GN):
                        last = mm(bank[2 * (lv % 2) + ck][:, 128 * n:128 * n + 128], k[:, n, 128 * ck:128 * ck + 128],
                                  q[:, n, 128 * ck:128 * ck + 128], start=True, stop=True, skip_group_check=True)
                if lv <= 4:
                    for n in range(GN):
                        last = mm(bank[4 + lv % 2][0:16, 16 * n:16 * n + 16], k[:, n, 256:T2], q[:, n, 256:T2],
                                  start=True, stop=True, skip_group_check=True)
                last.then_inc(g_att, 1)

            for lv in range(LEVELS + 1):
                level(lv)
            pe.wait_ge(k_dec, 1)
            for ck in range(2):
                turn([(bank[6 + ck][:, 128 * n:128 * n + 128],
                          g_k[:, 0, :].rearrange("p (n t) -> p n t", n=GN)[:, n, 128 * ck:128 * ck + 128])
                         for n in range(GN)], k_turned)
            pe.wait_ge(g_sel, LEVELS + 1)
            for ck in range(2):
                pe.wait_ge(k_tok, ck + 1)
                for n in range(GN):
                    last = mm(bank[2 * ck + 4 * (1 - ck) + n // 2][:, 256 * (n % 2):256 * (n % 2) + 256],
                              kdT[:, ck, 128 * n:128 * n + 128], gv_tok[:, ck, 256 * n:256 * n + 256],
                              start=True, stop=True, skip_group_check=True)
                last.then_inc(s_done, 1)
            pe.wait_ge(state2, GN)
            pe.wait_ge(q_dec, 1)
            for o in range(8):
                n, dv = o // 2, o % 2
                b = bank[o % 4]
                if o >= 4:
                    pe.wait_ge(go_taken, o - 3)
                cols = slice(256 * n + 128 * dv, 256 * n + 128 * dv + 128)
                qt = g_q[:, 0, :].rearrange("p (n t) -> p n t", n=GN)
                mm(b[:, 0:128], gv_tok[:, 0, cols], att[:, 0, n, :], start=True, stop=True, skip_group_check=True)
                mm(b[:, 128:256], gv_tok[:, 1, cols], att[:, 1, n, :], start=False, stop=True, skip_group_check=True)
                mm(b[:, 128:256], s1[:, n, 128 * dv:128 * dv + 128], qt[:, n, 128:256], start=False, stop=True,
                   skip_group_check=True)
                mm(b[:, 256:T2], gv_tok[0:16, 2, cols], att2[0:16, n, :], start=False, stop=True, skip_group_check=True)
                mm(b[:, 256:T2], s2[:, n, 128 * dv:128 * dv + 128], qt[:, n, 256:T2], start=False, stop=True,
                   skip_group_check=True).then_inc(go_done, 1)
            for n in range(GN):
                for dv in range(2):
                    pe.wait_ge(go_sq, 2 * n + dv + 1)
                    last = mm(bank[4 + n][:, 0:T2], ones, sq[:, 2 * n + dv, :], start=dv == 0, stop=dv == 1)
                last.then_inc(go_ss, 1)

            s0 = s0 + 14
            arrived(s0)
            pe.wait_ge(z_out, 4)
            w = slot(s0 % 2, 4, 1024)
            for c in range(8):
                chunk([(w[:, k, 128 * c:128 * c + 128], big2[:, 8 + k, :]) for k in range(4)], 128, T2)
            out_proj(s0 + 1, big2[:, 0:8, :], (go_ready, 8), T2, None)
            out_proj(s0 + 3, big2[:, 12:20, :], (mix_ready, 8), T2, 6)
            sum_squares(7, T2, 0, 8)
            xg_all(7)
            ffn(2, T2, 8)
            for tb in range(2):
                for half in range(2):
                    pe.wait_ge(h2_ready, 24 if half else 20)
                    i = 2 * tb + half
                    turn([(bank[i][:, 128 * c:128 * c + 128],
                              h2[:, 4 * half + c, META + 128 * tb:META + 128 * tb + 128]) for c in range(4)], y_turned)

        @block.scalar
        def _(act):
            line = Line(act, act_step)
            fn = nc.scalar.activation
            act.dma_start(early[:, :], A["early_c"]).then_inc(early_loaded, 16)
            for tb in range(2):
                act.dma_start(x_in[:, tb, :], A["x"][0][128 * tb:128 * tb + 128, :]).then_inc(x_loaded, 16)
            act.wait_ge(prepared, 1)
            for dst, src in vec_loads:
                act.dma_start(dst, src).then_inc(vec_loaded, 16)
            w2 = [A["nsa_cmp_w2"][0][kv].rearrange("(c p) d -> p c d", p=128) for kv in range(2)]
            for dst, src in ((w2k_sb[:, :, 0:64], w2[0]), (w2k_sb[:, :, 64:128], w2[0]), (w2v_sb, w2[1])):
                act.dma_start(dst, src).then_inc(small_loaded, 16)
            act.dma_start(sinks, A["swa_sinks"][0].unsqueeze(0).broadcast_to([128, 16])).then_inc(small_loaded, 16)
            act.dma_start(late[:, :], A["late_c"]).then_inc(late_loaded, 16)

            def squares(i, T, src, ready):
                for c in range(8):
                    act.wait_ge(*ready(c))
                    line.put(fn(sq[:, c, 0:T], src[:, c, 0:T], ACT.Square), sq_ready)
                act.wait_ge(ss_done, i + 1)
                line.put(fn(root[:, 0:T], bank[7][:, 0:T], ACT.Sqrt, bias=eps_col[:, 0:1]), root_ready)

            def taken(n0):
                return lambda c: (proj_taken, n0 + c + 1)

            squares(0, T1, xT, lambda c: (turn_taken, 4 + c // 2))
            for w in range(2):
                act.wait_ge(vt_done, w + 1)
                line.put(fn(vtok[:, w, :, :].rearrange("p a b -> p (a b)"), bank[6 + w][:, :], ACT.Copy), vt_taken)
            act.wait_ge(vt_done, 3)
            line.put(fn(egate.rearrange("p a b -> p (a b)"), bank[6][:, 0:96], ACT.Exp, scale=-1.0), vt_taken)
            act.wait_ge(cmp_hid, 2)
            line.put(fn(hidT.rearrange("p a b c -> p (a b c)"), bank[2][:, 0:240], ACT.Gelu_apprx_tanh), cmp_act)
            act.wait_ge(cmp_kv, 1)
            act.wait_ge(prepared, 5)
            for a in range(2):
                half = slice(64 * a, 64 * a + 64)
                line.put(fn(kcT[half, a, :], bank[3][half, 0:60], ACT.Copy), cmp_kv_taken)
            for r in range(4):
                line.put(fn(vc_rep[32 * r:32 * r + NCMP, :], bank[3][0:NCMP, 64:320], ACT.Copy), cmp_kv_taken)

            def attention(units, v0, nsa, c0, dst):
                for i in range(len(units) + 3):
                    if i < len(units):
                        v = v0 + i
                        first = units[i][1] == "first"
                        act.wait_ge(at_neg, v + 1)
                        if v >= 2:
                            act.wait_ge(at_turned, v - 1)
                        n, w = (4 if nsa else 2, 128) if first else (2, 256)
                        for k in range(n):
                            ins = fn(S_p[:, v % 2, w * k:w * k + w], bank[4 + v % 2][:, w * k:w * k + w], ACT.Exp,
                                     scale=SCALE, bias=st_neg[:, v % 2, k:k + 1], accum_out=st_den[:, v % 2, k:k + 1])
                        line.put(ins, at_exp)
                        if not nsa:
                            act.wait_ge(at_sink, v - v0 + 1)
                            line.put(fn(st_es[:, v % 2, 0:2], st_es[:, v % 2, 0:2], ACT.Exp), at_sinkexp)
                    if nsa and i == 0:
                        act.wait_ge(cmp_centered, 1)
                        line.put(fn(c_e, c_s, ACT.Exp, scale=SCALE), cmp_exp)
                    if nsa and i == 1:
                        for qb in range(2):
                            act.wait_ge(cmp_turned, qb + 1)
                            line.put(fn(c_pt[:, qb, :, :].rearrange("p a b -> p (a b)"), bank[6 + qb][:, :], ACT.Copy), cmp_pt)
                    j = i - 3
                    if j >= 0 and units[j][1] in ("second", "second1"):
                        act.wait_ge(at_pv, v0 + j + 1)
                        ci = units[j][0]
                        line.put(fn(big1[:, dst + ci, :], bank[ci % 2][:, 0:256], ACT.Copy), at_out)

            attention(NSA_UNITS, 0, True, 0, NSA_OUT)
            squares(1, T1, xT, taken(N_NSA_O))

            def ffn(l, T, func):
                def step(k, n, p, w0, b, first):
                    act.wait_ge(proj_taken, n + 1)
                    if not first:
                        act.wait_ge(conv_mid, k - 1)
                    fn(f_c1[:, p, 0:T], f_a[:, p, 0:T], ACT.Identity, scale=w0, bias=b).then_inc(c1_ready, 1)
                    act.wait_ge(conv_ready, k + 1)
                    if not first:
                        act.wait_ge(hidden_ready, k - 1)
                    fn(f_s[:, p, 0:T], f_c3[:, p, 0:T], func).then_inc(act_ready, 1)

                def tap(name, f):
                    at = vcolc[name][0]
                    if isinstance(f, int):
                        return vecs[:, 1 + l, at + f:at + f + 1]
                    return vecs[:, 1 + l, bass.ds(f + at, 1)]

                for f in range(2):
                    step(FC * l + f, N_FFN[l] + 2 * f, f, tap("w0", f), tap("b", f), l == 0)
                with act.Fori(0, (FC // 2 - 1) // 2) as i:
                    for j in range(4):
                        step(i * 4 + (FC * l + 2 + j), i * 8 + (N_FFN[l] + 4 + 2 * j), j % 2,
                             tap("w0", i * 4 + (2 + j)), tap("b", i * 4 + (2 + j)), False)

            ffn(0, T1, ACT.Silu)
            squares(2, T1, xT, taken(N_FFN[0] + 44))
            rope = 0
            for n in range(10):
                place, r = SWA[n]
                act.wait_ge(proj_taken, N_SWA + n + 1)
                t = xs[:, (NSA_ROPED + rope) % 2, :] if r else big1[:, place, :]
                line.put(fn(t, t, ACT.Identity, bias=vec("bqkv", 8 if n == 0 else 9 if n == 1 else n - 2)), biased)
                rope += r
                if n == 3:
                    act.wait_ge(vt_done, 4)
                    line.put(fn(vtok[:, 0, :, 0:128], bank[6][:, 0:256].rearrange("p (a b) -> p a b", a=2), ACT.Copy),
                             vt_taken)
            attention(SWA_UNITS, V_SWA, False, 8, SWA_OUT)
            squares(3, T1, xT, taken(N_SWA_O))
            ffn(1, T1, ACT.Silu)
            squares(4, T1, xT, taken(N_FFN[1] + 44))
            squares(5, T2, h2, lambda c: (h2_ready, c + 1))
            for c in range(8):
                act.wait_ge(proj_taken, N_IN2 + 28 + c + 1)
                t = big2[:, 28 + c, :]
                line.put(fn(t, t, ACT.Silu))
            for c in range(16):
                act.wait_ge(proj_taken, N_IN2 + 37 + c + 1)
                t = big2[:, 36 + c, :]
                line.put(fn(t, t, ACT.Sigmoid))
            for tb in range(3):
                w = min(128, T2 - 128 * tb)
                act.wait_ge(vt_done, 5 + tb)
                line.put(fn(sv_tok[0:w, tb, :], bank[4 + tb][0:w, :], ACT.Copy), vt_taken)
            Z = [bank[0], bank[1], bank[4], bank[5]]

            def z_final(i):
                act.wait_ge(z_tri, i + 1)
                if i >= 2:
                    act.wait_ge(z_pv, i - 1)
                line.put(fn(z_w[:, i % 2, :], Z[i % 4][:, 0:ZW], ACT.Exp, scale=SCALE), z_weights)

            def z_evac(i):
                if i % 2:
                    act.wait_ge(z_pv, i + 1)
                    line.put(fn(big2[:, 8 + i // 2, :], bank[2 + (i // 2) % 2][:, 0:T2], ACT.Copy), z_out)

            for i in range(8):
                act.wait_ge(z_abs, i + 1)
                if i >= 2:
                    act.wait_ge(z_soft, i - 1)
                line.put(fn(z_l[:, i % 2, :], z_a[:, i % 2, :], ACT.Exp, scale=-SCALE))
                line.settle()
                line.put(fn(z_l[:, i % 2, :], z_l[:, i % 2, :], ACT.Ln, bias=1.0), z_ln)
                if i >= 1:
                    z_final(i - 1)
                if i >= 2:
                    z_evac(i - 2)
            z_final(7)
            z_evac(6)
            z_evac(7)
            act.wait_ge(g_abs, 1)
            ga = g_d[:, 1, :]
            line.put(fn(ga, ga, ACT.Exp, scale=-1.0))
            line.settle()
            line.put(fn(ga, ga, ACT.Ln, bias=1.0), g_ln)
            for i in range(6):
                tb, half = i // 2, i % 2
                w = min(128, T2 - 128 * tb)
                act.wait_ge(vt_done, 8 + i)
                line.put(fn(gv_tok[0:w, tb, 512 * half:512 * half + 512], bank[4 + i % 4][0:w, :], ACT.Copy), vt_taken)
            for lv in range(1, LEVELS + 1):
                act.wait_ge(g_dist, lv)
                line.put(fn(g_d[:, lv % 2, :], g_d[:, lv % 2, :], ACT.Exp, scale=-1.0 / 16), g_decay)
            act.wait_ge(k_dist, 1)
            line.put(fn(g_d[:, 0, :], g_d[:, 0, :], ACT.Exp, scale=-1.0 / 16), k_decay)
            line.put(fn(cum, cum, ACT.Exp, scale=-1.0 / 16), q_decay)
            for ck in range(2):
                act.wait_ge(k_turned, ck + 1)
                line.put(fn(kdT[:, ck, :], bank[6 + ck][:, :], ACT.Copy), k_tok)
            act.wait_ge(s_done, 1)
            for half in range(2):
                ins = fn(s1[:, 2 * half:2 * half + 2, :].rearrange("p a b -> p (a b)"), bank[4 + half][:, :], ACT.Copy)
                if half:
                    line.put(ins, s_taken)
            for o in range(8):
                act.wait_ge(go_taken, o + 1)
                line.put(fn(sq[:, o, :], big2[:, o, :], ACT.Square), go_sq)
            rs = g_d[:, 1, :].rearrange("p (n t) -> p n t", n=GN)
            for n in range(GN):
                act.wait_ge(go_ss, n + 1)
                line.put(fn(rs[:, n, :], bank[4 + n][:, 0:T2], ACT.Sqrt, scale=float(D // 256), bias=eps_col[:, 0:1]), go_root)
            squares(6, T2, xT, taken(N_WO2))
            squares(7, T2, h2, lambda c: (h2_ready, 8 + c + 1))
            ffn(2, T2, ACT.Gelu_apprx_tanh)
            squares(8, T2, xT, taken(N_FFN[2] + 44))
            o_sb = big[:, 0:2048].rearrange("p (b n) -> p b n", b=2)
            for i in range(4):
                act.wait_ge(y_turned, i + 1)
                line.put(fn(o_sb[:, i // 2, 512 * (i % 2):512 * (i % 2) + 512], bank[i][:, :], ACT.Copy), y_taken)

        @block.vector
        def _(dve):
            line = Line(dve, dve_step)
            V = nc.vector

            def factor(i, T):
                dve.wait_ge(root_ready, i + 1)
                line.put(V.reciprocal(rstd[:, 0:T], root[:, 0:T]))
                line.settle()

            def take(n, dst, M, T, signal=proj_taken):
                dve.wait_ge(proj_done, n + 1)
                line.put(V.tensor_tensor(dst, bank[n % 4][0:M, 0:T], rstd[0:M, 0:T], ALU.mult), signal)

            V.memset(f_a[:, :, 0:2], 0.0)
            dve.wait_ge(turn_done, 1)
            line.put(V.tensor_copy(vecs[:, :, :],
                                   bank[4][:, :].rearrange("p (a b) -> p a b", a=4)), turn_taken)
            dve.wait_ge(turn_done, 2)
            line.put(V.tensor_copy(pe_dup, bank[5][:, 0:64].rearrange("p (a b) -> p a b", a=2)), turn_taken)
            dve.wait_ge(turn_done, 3)
            line.put(V.tensor_copy(h2[:, :, 0:META], bank[6][:, 0:128].rearrange("p (a b) -> p a b", a=8)), turn_taken)
            for b in range(4):
                dve.wait_ge(turn_done, 4 + b)
                line.put(V.tensor_copy(xT[:, 2 * b:2 * b + 2, 0:T1], bank[b][:, :].rearrange("p (a b) -> p a b", a=2)),
                         turn_taken)
            factor(0, T1)

            rope = {"k": 0}

            def rope_sin():
                k = rope["k"]
                dve.wait_ge(perm_done, k + 1)
                if k >= 2:
                    dve.wait_ge(roped, k - 1)
                line.put(V.tensor_tensor(tsin[:, k % 2, :], bank[4 + k % 2][:, 0:T1], E("sin"), ALU.mult), sin_done)
                rope["k"] += 1

            def projections(n0, table, each_after):
                k0 = rope["k"]
                seen = 0
                for i, (place, r) in enumerate(table):
                    if r:
                        k = k0 + seen
                        if k >= 2:
                            dve.wait_ge(perm_done, k - 1)
                            dve.wait_ge(cos_done, k - 1)
                        dst, seen = xs[:, k % 2, :], seen + 1
                    else:
                        dst = big1[:, place, :]
                    if n0 == 0 and i == 12:
                        take(n0 + i, dst[0:48], 48, T1)
                    else:
                        take(n0 + i, dst, 128, T1)
                    if i >= 1 and table[i - 1][1]:
                        rope_sin()
                    each_after(i)
                rope_sin()

            def nsa_extra(i):
                if i == 12:
                    line.settle()
                    line.put(V.tensor_scalar(big1[0:48, 20, :], big1[0:48, 20, :],
                                             vecs[0:48, 0, vcol0["gb"][0]:vcol0["gb"][0] + 1], None, ALU.add), gate_moved)
                if i in (14, 16):
                    kv = (i - 14) // 2
                    dve.wait_ge(roped, 2)
                    for a in range(2):
                        for par in range(2):
                            for lh in range(2):
                                src = big1[64 * a:64 * a + 64, 8 + 2 * kv:10 + 2 * kv, :]\
                                    .rearrange("p j (c l s) -> p j c l s", l=8, s=2)[:, :, lh:lh + NCMP, :, par]
                                dst = blkT[64 * par:64 * par + 64, kv, 8 * lh:8 * lh + 8, :]\
                                    .rearrange("p l (j a c) -> p a j c l", j=2, a=2)[:, a]
                                pos = pe_dup[64 * a:64 * a + 64, kv, 16 * lh:16 * lh + 16]\
                                    .rearrange("p (l s) -> p l s", s=2)[:, :, par]
                                pos = each(each(pos, NCMP), 2)
                                line.put(V.tensor_tensor(dst, src, pos, ALU.add), blk_ready)
                if i == 18:
                    dve.wait_ge(vt_taken, 3)
                    e = egate.rearrange("p a b -> p (a b)")
                    line.put(V.tensor_scalar(e, e, 1.0, None, ALU.add))
                    line.settle()
                    line.put(V.reciprocal(gates.rearrange("p a b -> p (a b)"), e), gates_ready)

            projections(0, NSA, nsa_extra)

            gate_of = gates.rearrange("p q (c a b) -> p q c a b", c=8, a=2)

            def cmp_softmax():
                dve.wait_ge(cmp_scores, 1)
                neg = E("cmpneg").rearrange("p (q c) -> p q c", q=2)
                line.put(V.tensor_tensor(c_s.rearrange("p (q h) c -> p q h c", q=2),
                                         bank[2][:, 0:480].rearrange("p (q h c) -> p q h c", q=2, h=16),
                                         each(neg, 16, axis=2), ALU.add))
                line.settle()
                line.put(V.tensor_reduce(c_mx, c_s, AX.X, ALU.max))
                line.settle()
                line.put(V.tensor_scalar(c_mx, c_mx, -1e20, None, ALU.max))
                line.settle()
                line.put(V.tensor_tensor(c_s, c_s, each(c_mx, NCMP, axis=2), ALU.subtract), cmp_centered)

            def cmp_norm():
                dve.wait_ge(cmp_exp, 1)
                dve.wait_ge(prepared, 3)
                line.put(V.tensor_reduce(c_den, c_e, AX.X, ALU.add))
                line.settle()
                line.put(V.tensor_scalar(c_den, c_den, 1e-6, None, ALU.max))
                line.settle()
                line.put(V.reciprocal(c_mx, c_den))
                line.settle()
                line.put(V.tensor_tensor(c_den.rearrange("p (q h) -> p q h", q=2), c_mx.rearrange("p (q h) -> p q h", q=2),
                                         gates.rearrange("p q (h b) -> p q h b", b=3)[:, :, :, 0], ALU.mult))
                line.settle()
                line.put(V.tensor_tensor(c_p[:, :, 0:NCMP], c_e, each(c_den, NCMP, axis=2), ALU.mult), cmp_probs)

            def attention(units, v0, nsa):
                for i in range(len(units) + 2):
                    if i < len(units):
                        v = v0 + i
                        ci, kind = units[i]
                        first = kind == "first"
                        n, w = (4 if nsa else 2, 128) if first else (2, 256)
                        dve.wait_ge(at_scores, v + 1)
                        line.put(V.tensor_reduce(st_mx[:, v % 2, 0:n], bank[4 + v % 2][:, 0:n * w].rearrange("p (n w) -> p n w", n=n),
                                                 AX.X, ALU.max))
                        line.settle()
                        if nsa:
                            line.put(V.tensor_scalar(st_neg[:, v % 2, 0:n], st_mx[:, v % 2, 0:n], -SCALE, None, ALU.mult), at_neg)
                        else:
                            ns = nsinks.rearrange("p (c a) -> p c a", a=2)[:, ci, :]
                            line.put(V.scalar_tensor_tensor(out=st_neg[:, v % 2, 0:2], in0=st_mx[:, v % 2, 0:2], scalar=-SCALE,
                                                            in1=ns, op0=ALU.mult, op1=ALU.min), at_neg)
                            line.settle()
                            line.put(V.tensor_tensor(st_es[:, v % 2, 0:2], st_neg[:, v % 2, 0:2], ns, ALU.subtract), at_sink)
                    if nsa and i == 0:
                        cmp_softmax()
                        cmp_norm()
                    if 1 <= i <= len(units):
                        v = v0 + i - 1
                        ci, kind = units[i - 1]
                        first = kind == "first"
                        n = 4 if nsa and first else 2
                        dve.wait_ge(at_exp, v + 1)
                        if v >= 2:
                            dve.wait_ge(at_probs, v - 1)
                        den, r = st_den[:, v % 2, 0:n], st_r[:, v % 2, 0:n]
                        if nsa:
                            line.put(V.reciprocal(r, den))
                            line.settle()
                            qb = 0 if first else 1
                            g = gate_of[:, qb, ci]
                            if first:
                                line.put(V.tensor_tensor(r.rearrange("p (a b) -> p a b", a=2), r.rearrange("p (a b) -> p a b", a=2),
                                                         g[:, :, 1:3], ALU.mult), at_r)
                            else:
                                line.put(V.tensor_tensor(r, r, g[:, int(kind[-1]), 1:3], ALU.mult), at_r)
                        else:
                            dve.wait_ge(at_sinkexp, v - v0 + 1)
                            line.put(V.tensor_tensor(den, den, st_es[:, v % 2, 0:2], ALU.add))
                            line.settle()
                            line.put(V.reciprocal(r, den), at_r)
                    if i >= 2:
                        v = v0 + i - 2
                        n = 256 if not nsa and units[i - 2][1] == "first" else 512
                        dve.wait_ge(at_turned, v + 1)
                        if v >= 2:
                            dve.wait_ge(at_pv, v - 1)
                        line.put(V.tensor_copy(S_pt[:, v % 2, 0:n], bank[6 + v % 2][:, 0:n]), at_pt)

            attention(NSA_UNITS, 0, True)

            def add_residual(n0, bias=None):
                for c in range(8):
                    n = n0 + c
                    dve.wait_ge(proj_done, n + 1)
                    if bias is None:
                        line.put(V.tensor_tensor(xT[:, c, 0:T1], bank[bank_of(n)][:, 0:T1], xT[:, c, 0:T1], ALU.add), proj_taken)
                    else:
                        line.put(V.scalar_tensor_tensor(out=xT[:, c, 0:T1], in0=bank[bank_of(n)][:, 0:T1], scalar=vec(bias, c),
                                                        in1=xT[:, c, 0:T1], op0=ALU.add, op1=ALU.add), proj_taken)

            def bank_of(n):
                for l in range(3):
                    if N_FFN[l] <= n < N_FFN[l] + 52:
                        return (n - N_FFN[l]) % 4
                return n % 4

            add_residual(N_NSA_O)
            factor(1, T1)

            def ffn(l, T):
                def tap(name, f):
                    at = vcolc[name][0]
                    if isinstance(f, int):
                        return vecs[:, 1 + l, at + f:at + f + 1]
                    return vecs[:, 1 + l, bass.ds(f + at, 1)]

                def step(k, n, b, p, f, first):
                    dve.wait_ge(proj_done, n + 1)
                    if not first:
                        dve.wait_ge(c1_ready, k - 1)
                    V.tensor_tensor(f_a[:, p, 2:2 + T], bank[b][:, 0:T], rstd[:, 0:T], ALU.mult).then_inc(proj_taken, 1)
                    dve.wait_ge(proj_done, n + 2)
                    if not first:
                        dve.wait_ge(hidden_ready, k - 1)
                    V.tensor_tensor(f_u[:, p, 0:T], bank[b + 1][:, 0:T], rstd[:, 0:T], ALU.mult).then_inc(proj_taken, 1)
                    dve.wait_ge(proj_taken, n + 2)
                    dve.wait_ge(c1_ready, k + 1)
                    V.scalar_tensor_tensor(out=f_c2[:, p, 0:T], in0=f_a[:, p, 1:1 + T], scalar=tap("w1", f),
                                           in1=f_c1[:, p, 0:T], op0=ALU.mult, op1=ALU.add).then_inc(conv_mid, 1)
                    dve.wait_ge(conv_mid, k + 1)
                    if not first:
                        dve.wait_ge(act_ready, k - 1)
                    V.scalar_tensor_tensor(out=f_c3[:, p, 0:T], in0=f_a[:, p, 2:2 + T], scalar=tap("w2", f),
                                           in1=f_c2[:, p, 0:T], op0=ALU.mult, op1=ALU.add).then_inc(conv_ready, 1)

                for f in range(2):
                    step(FC * l + f, N_FFN[l] + 2 * f, 2 * f, f, f, l == 0)
                with dve.Fori(0, (FC // 2 - 1) // 2) as i:
                    for j in range(4):
                        step(i * 4 + (FC * l + 2 + j), i * 8 + (N_FFN[l] + 4 + 2 * j), 2 * (j % 2), j % 2, i * 4 + (2 + j), False)
                line.skip(proj_taken, 2 * FC)
                line.skip(conv_ready, FC)

            ffn(0, T1)
            add_residual(N_FFN[0] + 44)
            factor(2, T1)
            projections(N_SWA, SWA, lambda i: None)
            dve.wait_ge(small_loaded, 16 * SMALL_DMAS)
            line.put(V.tensor_scalar(nsinks, sinks, -1.0, None, ALU.mult))
            line.settle()
            attention(SWA_UNITS, V_SWA, False)
            add_residual(N_SWA_O, "bo")
            factor(3, T1)
            ffn(1, T1)
            add_residual(N_FFN[1] + 44)
            factor(4, T1)
            for c in range(8):
                dve.wait_ge(xg_ready, 8 * 4 + c + 1)
                line.put(V.tensor_tensor(h2[:, c, META:T2], xg[:, c, 0:T1], rstd[:, 0:T1], ALU.mult), h2_ready)
            factor(5, T2)
            for n in range(53):
                place = n if n < 36 else n - 1
                if n == 36:
                    take(N_IN2 + n, glr[0:16, :], 16, T2)
                elif 12 <= n < 16:
                    dve.wait_ge(proj_done, N_IN2 + n + 1)
                    line.put(V.scalar_tensor_tensor(out=big2[:, place, :], in0=bank[(N_IN2 + n) % 4][:, 0:T2], scalar=GDK ** -0.5,
                                                    in1=rstd[:, :], op0=ALU.mult, op1=ALU.mult), proj_taken)
                else:
                    take(N_IN2 + n, big2[:, place, :], 128, T2)
            Z = [bank[0], bank[1], bank[4], bank[5]]
            for i in range(8):
                dve.wait_ge(z_scores, i + 1)
                if i >= 2:
                    dve.wait_ge(z_ln, i - 1)
                    dve.wait_ge(z_soft, i - 1)
                z = Z[i % 4][:, 0:ZW]
                line.put(V.tensor_scalar(z_r[:, i % 2, :], z, 0.0, SCALE, ALU.max, ALU.mult), z_relu)
                line.settle()
                line.put(V.scalar_tensor_tensor(out=z_a[:, i % 2, :], in0=z_r[:, i % 2, :], scalar=2.0 / SCALE, in1=z,
                                                op0=ALU.mult, op1=ALU.subtract), z_abs)
            dve.wait_ge(g_log, 1)
            gx = g_q[:, 0, :].rearrange("p (n t) -> p n t", n=GN)
            dve.wait_ge(z_pv, 8)
            for n in range(GN):
                line.put(V.tensor_scalar(gx[:, n, :], bank[n][:, 0:T2], vec("bgk", n), None, ALU.add), g_x)
            line.settle()
            line.put(V.tensor_scalar(g_q[:, 1, :], g_q[:, 0, :], -1.0, 0.0, ALU.mult, ALU.max))
            line.settle()
            line.put(V.scalar_tensor_tensor(out=g_d[:, 1, :], in0=g_q[:, 1, :], scalar=2.0, in1=g_q[:, 0, :],
                                            op0=ALU.mult, op1=ALU.add), g_abs)
            dve.wait_ge(g_ln, 1)
            line.settle()
            line.put(V.tensor_tensor(g_q[:, 0, :], g_q[:, 1, :], g_d[:, 1, :], ALU.add))
            dve.wait_ge(prepared, 7)
            line.settle()
            line.put(V.tensor_tensor_scan(cum.rearrange("p n t -> p (n t)"), g_k[:, 0, :], g_q[:, 0, :], 0.0, ALU.mult, ALU.add),
                     g_cum)

            def distance(lv):
                b = 1 << (lv - 1)
                if lv >= 3:
                    dve.wait_ge(g_qk, lv - 2)
                d = g_d[:, lv % 2, :].rearrange("p (n t) -> p n t", n=GN)
                if b <= 8:
                    cf = cum.rearrange("p n t -> p (n t)").rearrange("p (q h b) -> p q h b", h=2, b=b)
                    df = g_d[:, lv % 2, :].rearrange("p (q h b) -> p q h b", h=2, b=b)
                    pairs = [(df, cf)]
                else:
                    pairs = [(d[:, n, 0:256].rearrange("p (q h b) -> p q h b", h=2, b=b),
                              cum[:, n, 0:256].rearrange("p (q h b) -> p q h b", h=2, b=b)) for n in range(GN)]
                for x, (dd, cc) in enumerate(pairs):
                    border = cc[:, :, 0, b - 1:b]
                    border = border.broadcast_to([128, border.shape[1], b])
                    line.put(V.tensor_tensor(dd[:, :, 1, :], cc[:, :, 1, :], border, ALU.subtract))
                    line.put(V.tensor_tensor(dd[:, :, 0, :], border, cc[:, :, 0, :], ALU.subtract),
                             g_dist if x == len(pairs) - 1 else None)

            def select(lv):
                dve.wait_ge(g_att, lv + 1)
                m = L("gla")[:, 128 * lv:128 * lv + 128]
                tiles = [(att[:, ck, :, :], bank[2 * (lv % 2) + ck][:, :].rearrange("p (n t) -> p n t", n=GN), m, 128)
                         for ck in range(2)]
                if lv <= 4:
                    tiles.append((att2[0:16, :, :], bank[4 + lv % 2][0:16, 0:64].rearrange("p (n t) -> p n t", n=GN),
                                  m[0:16, 0:16], 16))
                line.settle()
                for x, (dst, src, mask, w) in enumerate(tiles):
                    sig = g_sel if x == len(tiles) - 1 else None
                    if lv == 0:
                        line.put(V.tensor_tensor(dst, src, each(mask, GN), ALU.mult), sig)
                    else:
                        line.put(V.copy_predicated(dst, each(mask.bitcast(U32), GN), src), sig)

            line.settle()
            dve.wait_ge(late_loaded, 16)
            for lv in range(LEVELS + 1):
                if lv < LEVELS:
                    distance(lv + 1)
                select(lv)
            d = g_d[:, 0, :].rearrange("p (n t) -> p n t", n=GN)
            dve.wait_ge(g_qk, LEVELS)
            for ck in range(2):
                end = cum[:, :, 128 * ck + 127:128 * ck + 128].broadcast_to([128, GN, 128])
                line.put(V.tensor_tensor(d[:, :, 128 * ck:128 * ck + 128], end, cum[:, :, 128 * ck:128 * ck + 128], ALU.subtract),
                         k_dist if ck else None)
            dve.wait_ge(s_taken, 1)
            dve.wait_ge(q_decay, 1)
            dve.wait_ge(s_done, 2)
            for n in range(GN):
                line.put(V.scalar_tensor_tensor(out=s2[:, n, :], in0=s1[:, n, :], scalar=cum[:, n, 255:256],
                                                in1=bank[2 + n // 2][:, 256 * (n % 2):256 * (n % 2) + 256],
                                                op0=ALU.mult, op1=ALU.add), state2)
            for o in range(8):
                dve.wait_ge(go_done, o + 1)
                line.put(V.tensor_copy(big2[:, o, :], bank[o % 4][:, 0:T2]), go_taken)
            rs = g_d[:, 1, :].rearrange("p (n t) -> p n t", n=GN)
            for n in range(GN):
                dve.wait_ge(go_root, n + 1)
                line.put(V.reciprocal(rs[:, n, :], rs[:, n, :]))
                line.settle()
                for dv in range(2):
                    o = big2[:, 2 * n + dv, :]
                    line.put(V.scalar_tensor_tensor(out=o, in0=o, scalar=vec("hn", dv), in1=rs[:, n, :], op0=ALU.mult, op1=ALU.mult))
                    line.settle()
                    line.put(V.tensor_tensor(o, o, big2[:, 28 + 2 * n + dv, :], ALU.mult), go_ready)
            for c in range(8):
                n = N_SBO + c
                dve.wait_ge(proj_done, n + 1)
                line.put(V.tensor_tensor(big2[:, 12 + c, :], bank[n % 4][:, 0:T2], big2[:, 36 + c, :], ALU.mult), proj_taken)
            for c in range(8):
                n = N_GLO + c
                dve.wait_ge(proj_done, n + 1)
                line.put(V.tensor_tensor(g_tmp[:, c % 2, :], bank[n % 4][:, 0:T2], big2[:, 44 + c, :], ALU.mult), proj_taken)
                line.settle()
                line.put(V.tensor_tensor(big2[:, 12 + c, :], big2[:, 12 + c, :], g_tmp[:, c % 2, :], ALU.add), mix_ready)

            def copy_out(n0):
                for c in range(8):
                    n = n0 + c
                    dve.wait_ge(proj_done, n + 1)
                    line.put(V.tensor_copy(xT[:, c, :], bank[bank_of(n)][:, 0:T2]), proj_taken)

            def add_normed(i):
                factor(i, T2)
                for c in range(8):
                    dve.wait_ge(xg_ready, 8 * i + c + 1)
                    line.put(V.tensor_tensor(g_tmp[:, c % 2, :], xg[:, c, :], rstd[:, :], ALU.mult))
                    line.settle()
                    line.put(V.tensor_tensor(h2[:, c, :], h2[:, c, :], g_tmp[:, c % 2, :], ALU.add), h2_ready)

            copy_out(N_WO2)
            add_normed(6)
            V.memset(f_a[:, :, 0:2], 0.0)
            factor(7, T2)
            ffn(2, T2)
            copy_out(N_FFN[2] + 44)
            add_normed(8)

        @block.gpsimd
        def _(pool):
            line = Line(pool, pool_step)
            G = nc.gpsimd
            G.memset(eps_col[:, :], EPS)
            line.put(G.memset(vec_in, 0.0), prepared)
            pool.wait_ge(early_loaded, 16)
            G.tensor_copy(ident_b[:, :], ident)
            G.tensor_copy(mask_b[:, 0:128], E("before"))
            line.put(G.tensor_copy(mask_b[:, 128:256], E("causal")), prepared)
            line.put(G.memset(c_p, 0.0), prepared)
            line.put(G.memset(big1[:, K_AT:K_AT + 16, :], 0.0), prepared)
            line.put(G.memset(kcT, 0.0), prepared)
            pool.wait_ge(late_loaded, 16)
            line.put(G.tensor_copy(sbneg_b[:, :], L("sbneg")), prepared)

            def gains(i, T, src, ready):
                for c in range(8):
                    pool.wait_ge(*ready(c))
                    line.put(G.tensor_scalar(xg[:, c, 0:T], src[:, c, 0:T], vec("g", 8 * i + c), None, ALU.mult), xg_ready)

            def taken(n0):
                return lambda c: (proj_taken, n0 + c + 1)

            gains(0, T1, xT, lambda c: (turn_taken, 4 + c // 2))
            rope = {"k": 0}

            def ropes(table, ready):
                for i, (place, r) in enumerate(table):
                    if not r:
                        continue
                    k = rope["k"]
                    pool.wait_ge(*ready(i))
                    line.put(G.tensor_tensor(tcos[:, k % 2, :], xs[:, k % 2, :], E("cos"), ALU.mult), cos_done)
                    pool.wait_ge(sin_done, k + 1)
                    line.settle()
                    if place not in KEYS:
                        line.put(G.tensor_tensor(big1[:, place, :], tcos[:, k % 2, :], tsin[:, k % 2, :], ALU.add), roped)
                    else:
                        for g in range(2):
                            for a in range(2):
                                half = slice(64 * g, 64 * g + 64)
                                line.put(G.tensor_tensor(big1[64 * a:64 * a + 64, K_AT + 2 * (KEYS[place] + g) + a, :],
                                                         tcos[half, k % 2, :], tsin[half, k % 2, :], ALU.add),
                                         roped if g and a else None)
                                line.settle()
                    rope["k"] += 1

            ropes(NSA, lambda i: (proj_taken, i + 1))

            def attention(units, v0, nsa):
                for i, (ci, kind) in enumerate(units):
                    v = v0 + i
                    n, w = (4 if nsa else 2, 128) if kind == "first" else (2, 256)
                    pool.wait_ge(at_r, v + 1)
                    p = S_p[:, v % 2, 0:n * w].rearrange("p (n w) -> p n w", n=n)
                    r = st_r[:, v % 2, 0:n].unsqueeze(2).broadcast_to([128, n, w])
                    line.put(G.tensor_tensor(p, p, r, ALU.mult), at_probs)

            attention(NSA_UNITS, 0, True)
            gains(1, T1, xT, taken(N_NSA_O))

            def ffn(l, T):
                def step(k, n, p, dst):
                    pool.wait_ge(proj_taken, n + 2)
                    pool.wait_ge(act_ready, k + 1)
                    G.tensor_tensor(dst, f_s[:, p, 0:T], f_u[:, p, 0:T], ALU.mult).then_inc(hidden_ready, 1)

                for f in range(2):
                    step(FC * l + f, N_FFN[l] + 2 * f, f, big[:, f * T:f * T + T])
                with pool.Fori(0, (FC // 2 - 1) // 2) as i:
                    for j in range(4):
                        step(i * 4 + (FC * l + 2 + j), i * 8 + (N_FFN[l] + 4 + 2 * j), j % 2,
                             big[:, bass.ds(i * (4 * T) + (2 + j) * T, T)])
                line.skip(hidden_ready, FC)

            ffn(0, T1)
            gains(2, T1, xT, taken(N_FFN[0] + 44))
            ropes(SWA, lambda i: (biased, i + 1))
            attention(SWA_UNITS, V_SWA, False)
            gains(3, T1, xT, taken(N_SWA_O))
            ffn(1, T1)
            gains(4, T1, xT, taken(N_FFN[1] + 44))
            gains(5, T2, h2, lambda c: (h2_ready, c + 1))
            pool.wait_ge(proj_taken, N_IN2 + 8)
            G.dma_start(up_sb[0:16, :], A["w_gk_up_2"][0]).then_inc(up_loaded, 16)
            line.put(G.memset(kpad, 0.0))
            line.settle()
            line.put(G.tensor_copy(kpad[:, :, 0:16], big2[:, 4:8, 256:T2]), kpad_ready)
            for i in range(8):
                pool.wait_ge(z_ln, i + 1)
                pool.wait_ge(z_relu, i + 1)
                if i >= 2:
                    pool.wait_ge(z_tri, i - 1)
                line.put(G.tensor_tensor(z_u[:, i % 2, :], z_l[:, i % 2, :], z_r[:, i % 2, :], ALU.add))
                line.settle()
                line.put(G.tensor_tensor(z_u[:, i % 2, :], z_u[:, i % 2, :], L("sbvalid"), ALU.mult), z_soft)
            pool.wait_ge(z_pv, 8)
            line.put(G.memset(g_k[:, 0, :], 1.0))
            line.settle()
            line.put(G.memset(g_k[:, 0, :].rearrange("p (n t) -> p n t", n=GN)[:, :, 0:T2:128], 0.0), prepared)
            pool.wait_ge(g_cum, 1)
            for v in (g_q, g_k):
                line.put(G.memset(v, 0.0))
            line.settle()
            for lv in range(1, LEVELS + 1):
                b = 1 << (lv - 1)
                pool.wait_ge(g_decay, lv)
                if lv >= 2:
                    pool.wait_ge(g_att, lv - 1)

                def split(v, n=None):
                    v = v if n is None else v[:, T2 * n:T2 * n + 256]
                    return v.rearrange("p (q h b) -> p q h b", h=2, b=b)

                d = g_d[:, lv % 2, :]
                q, k = big2[:, 12:16, :].rearrange("p n t -> p (n t)"), big2[:, 16:20, :].rearrange("p n t -> p (n t)")
                for n in ([None] if b <= 8 else range(GN)):
                    line.put(G.tensor_tensor(split(g_q[:, lv % 2, :], n)[:, :, 1, :], split(q, n)[:, :, 1, :],
                                             split(d, n)[:, :, 1, :], ALU.mult))
                    line.put(G.tensor_tensor(split(g_k[:, lv % 2, :], n)[:, :, 0, :], split(k, n)[:, :, 0, :],
                                             split(d, n)[:, :, 0, :], ALU.mult), g_qk if n in (None, GN - 1) else None)

            def by_head(v):
                return v.rearrange("p (n t) -> p n t", n=GN)

            pool.wait_ge(k_decay, 1)
            pool.wait_ge(g_att, LEVELS)
            line.put(G.tensor_tensor(by_head(g_k[:, 0, :])[:, :, 0:256], big2[:, 16:20, 0:256], by_head(g_d[:, 0, :])[:, :, 0:256],
                                     ALU.mult), k_dec)
            pool.wait_ge(q_decay, 1)
            line.put(G.tensor_tensor(by_head(g_q[:, 0, :])[:, :, 128:T2], big2[:, 12:16, 128:T2], cum[:, :, 128:T2], ALU.mult),
                     q_dec)
            gains(6, T2, xT, taken(N_WO2))
            gains(7, T2, h2, lambda c: (h2_ready, 8 + c + 1))
            ffn(2, T2)
            gains(8, T2, xT, taken(N_FFN[2] + 44))
    return nc


_INS = ["x", "nsa_w_in", "nsa_cmp_pe", "nsa_cmp_w1", "nsa_cmp_w2", "nsa_gate_b", "nsa_w_o", "swa_w_qkv", "swa_b_qkv",
        "swa_sinks", "swa_w_o", "swa_b_o", "ffn_w_gu", "ffn_conv_w", "ffn_conv_b", "ffn_w_down", "norm_mix", "norm_ffn",
        "norm_final", "meta_tokens_2", "norm_mix_pre_2", "w_in_2", "w_gk_up_2", "b_gk_2", "gla_head_norm_2", "w_sb_out_2",
        "w_gla_out_2", "w_o_2", "norm_mix_post_2", "norm_ffn_pre_2", "w_ffn_up_2", "w_ffn_gate_2", "conv_w_2", "conv_b_2",
        "w_ffn_down_2", "norm_ffn_post_2"]


def kernel(**inputs):
    import numpy as _np
    import concourse.bacc as _bacc
    from concourse import mybir as _mybir
    from concourse.bass_utils import run_bass_kernel_spmd as _run

    nc = _bacc.Bacc("TRN2", target_bir_lowering=False, num_devices=1)
    arrays, aps = {}, {}
    e, l = constants()
    for name, a in [(n, inputs[n]) for n in _INS] + [("early_c", e), ("late_c", l)]:
        a = _np.ascontiguousarray(a)
        arrays[f"in_{name}"] = a
        aps[name] = nc.dram_tensor(f"in_{name}", a.shape, _mybir.dt.from_np(a.dtype), kind="ExternalInput").ap()
    out = nc.dram_tensor("out_0", (1, SEQ, D), _mybir.dt.float32, kind="ExternalOutput").ap()
    build(nc, aps, out)
    r = _run(nc, [arrays], core_ids=[0])
    return r.results[0]["out_0"]
```

```python
import concourse.bass as bass
from concourse import mybir
from contextlib import ExitStack
import numpy as np

F32 = mybir.dt.float32
F32R = mybir.dt.float32r
BF16 = mybir.dt.bfloat16
U16 = mybir.dt.uint16
ALU = mybir.AluOpType
ACT = mybir.ActivationFunctionType
AX = mybir.AxisListType

D, SEQ, META = 1024, 256, 16
SLAB = 2048
T1, T2 = SEQ, SEQ + META
KC = D // 128
DFF = 2816
FC = DFF // 128
HD = 64
EPS = 1e-6
SCALE = HD ** -0.5
NEG = -1e30
NCMP, CSTR, CLEN = 15, 16, 32
GN, GDK = 4, 128
LEVELS = 7
ZW = 272 + 144 + 16

EARLY = {"ident": 128, "ones": 128, "rot": 128, "cos": T1, "sin": T1, "causal": 128, "before": 128, "cmpneg": 2 * NCMP}
LATE = {"tri": 128, "all": 128, "sbvalid": ZW, "sbneg": ZW, "gla": (LEVELS + 1) * 128}


def columns(parts):
    at, out = 0, {}
    for name, width in parts.items():
        out[name] = (at, at + width)
        at += width
    return out, at


def constants():
    p = np.arange(128)
    q = np.arange(128)
    early, n = columns(EARLY)
    e = np.zeros((128, n), np.float32)

    def put(a, cols, name, v):
        a[:, cols[name][0]:cols[name][1]] = v

    put(e, early, "ident", np.eye(128))
    put(e, early, "ones", 1.0 / D)
    rot = np.zeros((128, 128), np.float32)
    for m in range(128):
        if m % 64 < 32:
            rot[m + 32, m] = -1.0
        else:
            rot[m - 32, m] = 1.0
    put(e, early, "rot", rot)
    inv = (np.float32(10000.0) ** (-np.arange(0, HD, 2, dtype=np.float32) / np.float32(HD))).astype(np.float32)
    ang = inv[p % 32][:, None] * np.arange(T1, dtype=np.float32)[None, :]
    put(e, early, "cos", np.cos(ang.astype(np.float32)))
    put(e, early, "sin", np.sin(ang.astype(np.float32)))
    put(e, early, "causal", np.where(q[None, :] <= p[:, None], 0.0, NEG))
    put(e, early, "before", np.where(q[None, :] > p[:, None], 0.0, NEG))
    c = np.arange(NCMP)
    cm = [np.where(c[None, :] * CSTR + CLEN - 1 <= (p + 128 * b)[:, None], 0.0, NEG) for b in range(2)]
    put(e, early, "cmpneg", np.concatenate(cm, 1))

    late, n = columns(LATE)
    l = np.zeros((128, n), np.float32)
    valid = []
    for b in range(3):
        t = np.arange(128 * b, T2)
        s = p + 128 * b
        valid.append((s[:, None] < t[None, :]) & (s[:, None] < T2))
    valid = np.concatenate(valid, 1)
    put(l, late, "sbvalid", valid)
    put(l, late, "sbneg", np.where(valid, 0.0, NEG))
    put(l, late, "tri", np.where(p[:, None] >= q[None, :], -1.0 / SCALE, 0.0))
    put(l, late, "all", -1.0 / SCALE)
    g = [p[:, None] == q[None, :]]
    for i in range(LEVELS):
        b = 1 << i
        g.append((p[:, None] // (2 * b) == q[None, :] // (2 * b)) & (p[:, None] % (2 * b) < b) & (q[None, :] % (2 * b) >= b))
    put(l, late, "gla", np.concatenate(g, 1))
    return e, l


VEC0 = {"g": 9 * KC, "bo": KC, "hn": 2, "bgk": 4, "bqkv": 10, "gb": 1}
VEC_CONV = {"w0": FC, "w1": FC, "w2": FC, "b": FC}


def vector_loads(vec_in, pe_in, meta_in, A):
    at, _ = columns(VEC0)
    loads = []

    def rows(table, r, vector):
        n = vector.shape[0] // 128
        loads.append((vec_in[r:r + n, table, :], vector.rearrange("(c p) -> c p", p=128)))

    gains = [A["norm_mix"][0], A["norm_ffn"][0], A["norm_mix"][1], A["norm_ffn"][1], A["norm_final"],
             A["norm_mix_pre_2"][0], A["norm_mix_post_2"][0], A["norm_ffn_pre_2"][0], A["norm_ffn_post_2"][0]]
    for i, g in enumerate(gains):
        rows(0, at["g"][0] + KC * i, g)
    rows(0, at["bo"][0], A["swa_b_o"][0])
    rows(0, at["hn"][0], A["gla_head_norm_2"][0])
    rows(0, at["bgk"][0], A["b_gk_2"][0])
    rows(0, at["bqkv"][0], A["swa_b_qkv"][0])
    r = at["gb"][0]
    loads.append((vec_in[r:r + 1, 0, 0:48], A["nsa_gate_b"]))
    for table, w, b in ((1, A["ffn_conv_w"][0], A["ffn_conv_b"][0]), (2, A["ffn_conv_w"][1], A["ffn_conv_b"][1]),
                        (3, A["conv_w_2"][0], A["conv_b_2"][0])):
        for k in range(3):
            rows(table, FC * k, w[k])
        rows(table, FC * 3, b)
    for kv in range(2):
        for twice in range(2):
            loads.append((pe_in[:, kv, twice, :], A["nsa_cmp_pe"][0][kv]))
    loads.append((meta_in, A["meta_tokens_2"]))
    return loads


def build(nc, A, out):
    ctx = ExitStack()
    with ctx:
        def sb(name, shape, dt=F32):
            return ctx.enter_context(nc.sbuf_tensor(name, shape, dt))

        def sem(name):
            return ctx.enter_context(nc.semaphore(name))

        ecol, en = columns(EARLY)
        lcol, ln = columns(LATE)
        early = sb("early", [128, en])
        tri_all = sb("tri_all", [128, 256])
        late_b = sb("late_b", [128, ln - 256], BF16)

        def E(name):
            return early[:, ecol[name][0]:ecol[name][1]]

        def L(name):
            a, b = lcol[name]
            return tri_all[:, a:b] if b <= 256 else late_b[:, a - 256:b - 256]

        ident, ones = E("ident"), E("ones")
        ident_b = sb("ident_b", [128, 128], BF16)
        mask_b = sb("mask_b", [128, 256], BF16)
        vcol0, _ = columns(VEC0)
        vcolc, vcn = columns(VEC_CONV)
        vecs = sb("vecs", [128, 4, 128])

        def vec(name, i):
            at = vcol0[name][0] + i
            return vecs[:, 0, at:at + 1]

        raw = sb("raw", [128, 2, SLAB])
        w_h, w_l = sb("w_h", [128, 2, SLAB], F32R), sb("w_l", [128, 2, SLAB], F32R)
        xT = sb("xT", [128, KC, T2])
        h2 = sb("h2", [128, KC, T2])
        xh, xl = sb("xh", [128, KC, T2], F32R), sb("xl", [128, KC, T2], F32R)
        sq = sb("sq", [128, 4, T2])
        rstd = sb("rstd", [128, T2])
        root = sb("root", [128, T2])
        eps_col = sb("eps_col", [128, 8])
        big_at = nc.sbuf_base
        big = sb("big", [128, 52 * T2])
        hid_h = nc.alloc_sbuf_tensor_at("hid_h", [128, FC, T2], F32R, offset=big_at)
        hid_l = nc.alloc_sbuf_tensor_at("hid_l", [128, FC, T2], F32R, offset=big_at + 4 * FC * T2)
        AT_PLACE = 34
        at_h = nc.alloc_sbuf_tensor_at("at_h", [128, KC, T1], F32R, offset=big_at + 4 * AT_PLACE * T1)
        at_l = nc.alloc_sbuf_tensor_at("at_l", [128, KC, T1], F32R, offset=big_at + 4 * (AT_PLACE + KC) * T1)
        NW = 10928
        work = sb("work", [128, NW])

        def chunks(T):
            return big[:, 0:(52 * T2 // T) * T].rearrange("p (c t) -> p c t", t=T)

        big1, big2 = chunks(T1), chunks(T2)

        class Carver:
            def __init__(self):
                self.at = 0

            def __call__(self, *shape):
                n = int(np.prod(shape))
                v = work[:, self.at:self.at + n]
                self.at += n
                assert self.at <= NW, self.at
                if len(shape) == 2:
                    return v.rearrange("p (a b) -> p a b", b=shape[1])
                if len(shape) == 3:
                    return v.rearrange("p (a b c) -> p a b c", b=shape[1], c=shape[2])
                return v

        bank = [ctx.enter_context(nc.psum_tensor(f"bank{i}", [128, 512], F32)) for i in range(8)]

        x_in = big[:, 0:2048].rearrange("p (b n) -> p b n", b=2)
        vec_in = big[:, 2048:2560].rearrange("p (v n) -> p v n", v=4)
        pe_in = big[0:32, 2560:2816].rearrange("p (k u d) -> p k u d", k=2, u=2)
        meta_in = big[0:META, 2816:3840]
        late_in = big[:, 52 * T2 - ln:52 * T2]

        vec_loads = vector_loads(vec_in, pe_in, meta_in, A)
        VEC_DMAS, SMALL_DMAS = len(vec_loads), 4

        cv = Carver()
        xs, tcos, tsin = cv(2, T1), cv(2, T1), cv(2, T1)
        vtok = cv(2, 2, 256)
        S_p, S_pt = cv(2, 512), cv(2, 512)
        st_mx, st_neg, st_den, st_r, st_es = cv(2, 4), cv(2, 4), cv(2, 4), cv(2, 4), cv(2, 4)
        sinks, nsinks = cv(16), cv(16)
        pe_dup = cv(2, CLEN)
        w2k_sb, w2v_sb = cv(2, 128), cv(2, HD)
        gates = cv(2, 48)
        egate = cv(2, 48)
        blkT = cv(2, 16, 60)
        hidT = cv(2, 2, 60)
        kcT = cv(2, 60)
        vc_rep = cv(256)
        c_s, c_e = cv(32, NCMP), cv(32, NCMP)
        c_mx, c_den = cv(32), cv(32)
        c_p = cv(32, 32)
        c_pt = cv(2, 4, 128)
        cv = Carver()
        f_a, f_u, f_c1, f_c2, f_c3, f_s, f_h = cv(2, T2 + 2), *(cv(2, T2) for _ in range(6))
        cv = Carver()
        glr = cv(T2)
        up_sb = cv(512)
        stage = cv.at
        sv_tok = cv(3, 512)
        kpad = cv(4, 128)
        z_a, z_r, z_l, z_u, z_w = cv(2, ZW), cv(2, ZW), cv(2, ZW), cv(2, ZW), cv(2, ZW)
        cv.at = stage
        gv_tok = big[:, 0:3072].rearrange("p (b n) -> p b n", b=3)
        g_o = big2[:, 20:28, :]
        cum = cv(GN, T2)
        g_d, g_q, g_k = cv(2, GN * T2), cv(2, GN * T2), cv(2, GN * T2)
        att = cv(2, GN, 128)
        att2 = cv(GN, 16)
        g_tmp = cv(2, T2)
        kdT = g_q[:, 1, 0:1024].rearrange("p (c k) -> p c k", c=2)
        s1 = g_k[:, 1, 0:1024].rearrange("p (n v) -> p n v", n=GN)
        s2 = g_d[:, 0, 0:1024].rearrange("p (n v) -> p n v", n=GN)

        early_loaded, x_loaded, vec_loaded, small_loaded, late_loaded = map(sem, (
            "early_loaded", "x_loaded", "vec_loaded", "small_loaded", "late_loaded"))
        raw_loaded = [sem("raw_loaded0"), sem("raw_loaded1")]
        w_hi, w_lo = sem("w_hi"), sem("w_lo")
        out_stored = sem("out_stored")
        proj_done, proj_taken, down_part = map(sem, ("proj_done", "proj_taken", "down_part"))
        xh_even, xh_odd, xl_ready, sq_ready, ss_step, root_ready = map(sem, ("xh_even", "xh_odd", "xl_ready", "sq_ready", "ss_step", "root_ready"))
        turn_done, turn_taken = sem("turn_done"), sem("turn_taken")
        prepared = sem("prepared")
        biased = sem("biased")
        perm_done, cos_done, sin_done, roped = map(sem, ("perm_done", "cos_done", "sin_done", "roped"))
        vt_done, vt_taken = sem("vt_done"), sem("vt_taken")
        gate_moved, gate_exp, gates_ready = map(sem, ("gate_moved", "gate_exp", "gates_ready"))
        blk_ready, cmp_hid, cmp_act, cmp_kv, cmp_kv_taken = map(sem, (
            "blk_ready", "cmp_hid", "cmp_act", "cmp_kv", "cmp_kv_taken"))
        cmp_scores, cmp_centered, cmp_exp, cmp_probs, cmp_turned, cmp_pt = map(sem, (
            "cmp_scores", "cmp_centered", "cmp_exp", "cmp_probs", "cmp_turned", "cmp_pt"))
        at_scores, at_neg, at_exp, at_r, at_probs, at_turned, at_pt, at_pv, at_out = map(sem, (
            "at_scores", "at_neg", "at_exp", "at_r", "at_probs", "at_turned", "at_pt", "at_pv", "at_out"))
        at_sink, at_sinkexp, at_high = sem("at_sink"), sem("at_sinkexp"), sem("at_high")
        c1_ready, conv_mid, conv_ready, act_ready, hid_full, hid_high, hidden_ready = map(sem, (
            "c1_ready", "conv_mid", "conv_ready", "act_ready", "hid_full", "hid_high", "hidden_ready"))
        h2_ready = sem("h2_ready")
        kpad_ready, up_loaded, state2 = sem("kpad_ready"), sem("up_loaded"), sem("state2")
        z_scores, z_abs, z_relu, z_ln, z_soft, z_tri, z_weights, z_pv, z_out = map(sem, (
            "z_scores", "z_abs", "z_relu", "z_ln", "z_soft", "z_tri", "z_weights", "z_pv", "z_out"))
        g_log, g_x, g_abs, g_ln, g_cum = map(sem, ("g_log", "g_x", "g_abs", "g_ln", "g_cum"))
        g_dist, g_decay, g_qk, g_att, g_sel = map(sem, ("g_dist", "g_decay", "g_qk", "g_att", "g_sel"))
        k_dist, k_decay, k_dec, k_turned, k_tok, q_decay, q_dec = map(sem, (
            "k_dist", "k_decay", "k_dec", "k_turned", "k_tok", "q_decay", "q_dec"))
        s_done, s_taken, go_done, go_taken, go_sq, go_ss, go_root, go_ready = map(sem, (
            "s_done", "s_taken", "go_done", "go_taken", "go_sq", "go_ss", "go_root", "go_ready"))
        mix_full, mix_high, mix_ready, z_high, go_full, go_high = map(sem, (
            "mix_full", "mix_high", "mix_ready", "z_high", "go_full", "go_high"))
        y_turned, y_taken = sem("y_turned"), sem("y_taken")

        def rows(w):
            return w.rearrange("(k p) n -> p k n", p=128)

        def view(buf, s, k, n):
            return buf[:, s, 0:k * n].rearrange("p (k n) -> p k n", n=n)

        slabs, sizes, release, loaded, split_at, used = [], [], [], [], [], []
        per_slot = [0, 0]
        tally = {"chunk": 0, "part": 0, "hid": 0, "split": 0}

        def slab(k, n, parts, chunks_after=0, raw_use=False):
            s = len(slabs) % 2
            slabs.append([(dst(view(raw, s, k, n)), src) for dst, src in parts])
            sizes.append((k, n))
            per_slot[s] += 16 * len(parts)
            loaded.append(per_slot[s])
            if raw_use:
                tally["hid"] += 1
                release.append((cmp_hid, tally["hid"]))
                return
            tally["split"] += 1
            split_at.append(len(slabs) - 1)
            release.append((w_lo, tally["split"]))
            tally["chunk"] += chunks_after
            if chunks_after:
                used.append((proj_done, tally["chunk"]))
            else:
                tally["part"] += 1
                used.append((down_part, tally["part"]))

        def plain(w, c0, c1, k=KC):
            slab(k, c1 - c0, [(lambda v: v, rows(w)[:, :, c0:c1])], max(1, (c1 - c0) // 128))

        DOWN_PARTS = [(k, min(k + 4, FC)) for k in range(0, FC, 4)]

        def updown(wg, wu, wd):
            at = len(slabs), len(split_at)
            for f in range(FC):
                cols = slice(128 * f, 128 * f + 128)
                slab(KC, 256, [(lambda v: v[:, :, 0:128], rows(wg)[:, :, cols]),
                               (lambda v: v[:, :, 128:256], rows(wu)[:, :, cols])], 2)
            for g in range(2):
                for k0, k1 in DOWN_PARTS:
                    h = (k1 - k0) // 2
                    src = rows(wd)[:, k0:k1, g * 512:(g + 1) * 512]
                    slab(k1 - k0, 512, [(lambda v, h=h: v[:, 0:h, :], src[:, 0:h, :]), (lambda v, h=h: v[:, h:2 * h, :], src[:, h:, :])],
                         4 if k1 == FC else 0)
            return at

        w_in = A["nsa_w_in"][0]
        for c0 in range(1024, 2560, 256):
            plain(w_in, c0, c0 + 256)
        plain(w_in, 2560, 2608)
        for c0 in range(0, 1024, 256):
            plain(w_in, c0, c0 + 256)
        for kv in range(2):
            for half in range(2):
                src = A["nsa_cmp_w1"][0][kv].rearrange("(k p) n -> p k n", p=128)[:, 8 * half:8 * half + 8, :]
                slab(8, 256, [(lambda v: v, src)], raw_use=True)
        for c0 in range(0, 1024, 256):
            plain(A["nsa_w_o"][0], c0, c0 + 256)
        gu = A["ffn_w_gu"]
        ffn_at = [updown(gu[0][:, 0:DFF], gu[0][:, DFF:2 * DFF], A["ffn_w_down"][0])]
        M_SWA = len(split_at)
        w_qkv = A["swa_w_qkv"][0]
        for c0 in (1024, 0, 256, 512, 768):
            plain(w_qkv, c0, c0 + 256)
        for c0 in range(0, 1024, 256):
            plain(A["swa_w_o"][0], c0, c0 + 256)
        ffn_at.append(updown(gu[1][:, 0:DFF], gu[1][:, DFF:2 * DFF], A["ffn_w_down"][1]))
        M_IN2 = len(split_at)
        w2_in = A["w_in_2"][0]
        for c0 in range(0, 4608, 256):
            plain(w2_in, c0, c0 + 256)
        plain(w2_in, 4608, 4624)
        for c0 in range(4624, 6672, 256):
            plain(w2_in, c0, c0 + 256)
        M_SBO = len(split_at)
        for c0 in (0, 512):
            plain(A["w_sb_out_2"][0], c0, c0 + 512, k=4)
        M_GLO = len(split_at)
        for w in (A["w_gla_out_2"][0], A["w_o_2"][0]):
            for c0 in range(0, 1024, 256):
                plain(w, c0, c0 + 256)
        ffn_at.append(updown(A["w_ffn_up_2"][0], A["w_ffn_gate_2"][0], A["w_ffn_down_2"][0]))
        ups = [(gu[0][:, 0:DFF], gu[0][:, DFF:2 * DFF]), (gu[1][:, 0:DFF], gu[1][:, DFF:2 * DFF]),
               (A["w_ffn_up_2"][0], A["w_ffn_gate_2"][0])]
        def hidden(v, T):
            return v[:, :, :].rearrange("p f t -> p (f t)")[:, 0:FC * T].rearrange("p (f t) -> p f t", t=T)

        N_CMP = 11

        N_NSA = 0
        N_NSA_O = 21
        N_FFN = [29, 29 + 52 + 10 + 8, 0]
        N_SWA = N_FFN[0] + 52
        N_SWA_O = N_SWA + 10
        N_IN2 = N_FFN[1] + 52
        N_SBO = N_IN2 + 36 + 1 + 16
        N_GLO = N_SBO + 8
        N_WO2 = N_GLO + 8
        N_FFN[2] = N_WO2 + 8

        class Line:
            def __init__(self, eng, own):
                self.eng, self.own, self.count, self.last = eng, own, {}, None

            def put(self, ins, signal=None):
                s = self.own if signal is None else signal
                self.count[id(s)] = self.count.get(id(s), 0) + 1
                ins.then_inc(s, 1)
                self.last = (s, self.count[id(s)])

            def skip(self, signal, n):
                self.count[id(signal)] = self.count.get(id(signal), 0) + n
                self.last = (signal, self.count[id(signal)])

            def settle(self):
                self.eng.wait_ge(*self.last)

        act_step, dve_step, pool_step = sem("act_step"), sem("dve_step"), sem("pool_step")

        def each(ap, n, axis=1):
            v = ap.unsqueeze(axis)
            return v.broadcast_to([*v.shape[:axis], n, *v.shape[axis + 1:]])

        NSA = [(8, 1), (9, 1), (10, 0), (11, 0), ("k", 0), ("k", 2), (12, 0), (13, 0), ("k", 4), ("k", 6), (14, 0), (15, 0),
               (16, 0)] + [(i, 1) for i in range(8)]
        SWA = [("k", 0), (9, 0)] + [(i, 1) for i in range(8)]
        K_AT = 17

        def is_roped(entry):
            return entry[0] == "k" or entry[1] == 1

        STREAMS = {0: 0, 1: 1, 2: 2, 3: 3, 5: 4, 7: 5}
        NSA_ROPED, SWA_ROPED = 14, 9
        NSA_UNITS = [(ci, kind) for ci in range(8) for kind in ("first", "second0", "second1")]
        SWA_UNITS = [(ci, kind) for ci in range(8) for kind in ("first", "second")]
        V_SWA = len(NSA_UNITS)

        def out_bank(ci, nsa):
            return 2 + ci % 2 if nsa else ci % 2

        def down_bank(c):
            return c % 4 if c < 48 or c == 51 else c - 44

        block = ctx.enter_context(nc.Block())

        @block.sync
        def _(sp):
            def issue(n):
                if n >= 2:
                    sp.wait_ge(*release[n - 2])
                for dst, src in slabs[n]:
                    sp.dma_start(dst, src).then_inc(raw_loaded[n % 2], 16)

            def issue_ffn(l):
                n0, m0 = ffn_at[l]
                first, second = ups[l]
                issue(n0)
                issue(n0 + 1)
                with sp.Fori(0, (FC - 2) // 2) as i:
                    for j in range(2):
                        sp.wait_ge(w_lo, i * 2 + (m0 + j + 1))
                        s = (n0 + j) % 2
                        for half, w in enumerate((first, second)):
                            sp.dma_start(view(raw, s, KC, 256)[:, :, 128 * half:128 * half + 128],
                                         rows(w)[:, :, bass.ds(i * 256 + 128 * (2 + j), 128)]).then_inc(raw_loaded[s], 16)
                for n in range(n0 + FC, n0 + FC + 12):
                    issue(n)

            n = 0
            for l in range(3):
                while n < ffn_at[l][0]:
                    issue(n)
                    n += 1
                issue_ffn(l)
                n = ffn_at[l][0] + FC + 12
            assert n == len(slabs)
            o_sb = big[:, 0:2048].rearrange("p (b n) -> p b n", b=2)
            for tb in range(2):
                sp.wait_ge(y_taken, 2 * tb + 2)
                sp.dma_start(out[0][128 * tb:128 * tb + 128, :], o_sb[:, tb, :]).then_inc(out_stored, 16)
            sp.wait_ge(out_stored, 32)

        @block.tensor
        def _(pe):
            mm = nc.tensor.matmul
            line = {"n": 0}

            def split(m):
                k, n = sizes[split_at[m]]
                pe.wait_ge(w_lo, m + 1)
                return view(w_h, m % 2, k, n), view(w_l, m % 2, k, n)

            def product(dst, parts, k, cols, high, low, first, last):
                wh, wl = parts[0][:, k, cols], parts[1][:, k, cols]
                mm(dst, wh, high, start=first, stop=False)
                mm(dst, wh, low, start=False, stop=False)
                return mm(dst, wl, high, start=False, stop=last)

            def chunk(parts, c, K, M, T, ready=None, source=(xh, xl)):
                n = line["n"]
                if n >= 4:
                    pe.wait_ge(proj_taken, n - 3)
                for k in range(K):
                    if ready is not None:
                        pe.wait_ge(ready[0], ready[1] + k + 1)
                    last = product(bank[n % 4][0:M, 0:T], parts, k, slice(128 * c, 128 * c + M), source[0][:, k, 0:T],
                                   source[1][:, k, 0:T], k == 0, k == K - 1)
                last.then_inc(proj_done, 1)
                line["n"] += 1

            def turn(ins, signal):
                for dst, src in ins:
                    k = src.shape[0]
                    last = nc.tensor.transpose(dst, src, ident[0:k, 0:k])
                last.then_inc(signal, 1)

            def sum_squares(i, T, c0, c1):
                for c in range(c0, c1):
                    pe.wait_ge(sq_ready, 8 * i + c + 1)
                    mm(bank[7][:, 0:T], ones, sq[:, c % 4, 0:T], start=c == 0, stop=c == 7).then_inc(ss_step, 1)

            pe.wait_ge(early_loaded, 16)
            pe.wait_ge(vec_loaded, 16 * VEC_DMAS)
            pe.wait_ge(prepared, 2)
            turn([(bank[4][:, 128 * v:128 * v + 128], vec_in[:, v, :]) for v in range(4)], turn_done)
            turn([(bank[5][:, 32 * k:32 * k + 32], pe_in[:, k, :, :].rearrange("p u d -> p (u d)")) for k in range(2)],
                 turn_done)
            turn([(bank[6][:, 16 * c:16 * c + 16], meta_in[:, 128 * c:128 * c + 128]) for c in range(8)], turn_done)
            pe.wait_ge(x_loaded, 32)
            for b in range(4):
                turn([(bank[b][:, 256 * c + 128 * tb:256 * c + 128 * tb + 128],
                          x_in[:, tb, 128 * (2 * b + c):128 * (2 * b + c) + 128]) for c in range(2) for tb in range(2)],
                     turn_done)
            sum_squares(0, T1, 0, 8)
            pe.wait_ge(turn_taken, 7)

            rope = {"k": 0}

            def permute(after):
                k = rope["k"]
                pe.wait_ge(*after)
                if k >= 2:
                    pe.wait_ge(sin_done, k - 1)
                mm(bank[4 + k % 2][:, 0:T1], E("rot"), xs[:, k % 2, :], start=True, stop=True).then_inc(perm_done, 1)
                rope["k"] += 1

            m = 0
            for n in range(21):
                if n <= 12 and n % 2 == 0 or n > 12 and n % 2:
                    parts = split(m)
                    m += 1
                chunk(parts, 0 if n == 12 else n % 2 if n < 12 else (n - 13) % 2, KC, 48 if n == 12 else 128, T1,
                      (xl_ready, 0) if n == 0 else None)
                if n >= 1 and is_roped(NSA[n - 1]):
                    permute((proj_taken, n))
                if n == 13:
                    pe.wait_ge(proj_taken, 12)
                    for w in range(2):
                        turn([(bank[6 + w][:, 256 * kb + 128 * j:256 * kb + 128 * j + 128],
                                      big1[:, 12 + 2 * w + j, 128 * kb:128 * kb + 128]) for kb in range(2) for j in range(2)],
                             vt_done)
                if n == 15:
                    pe.wait_ge(gate_moved, 1)
                    pe.wait_ge(vt_taken, 1)
                    turn([(bank[6][:, 48 * qb:48 * qb + 48], big1[0:48, 16, 128 * qb:128 * qb + 128]) for qb in range(2)],
                         vt_done)
            permute((proj_taken, 21))

            pe.wait_ge(proj_taken, 21)
            for kv in range(2):
                pe.wait_ge(blk_ready, 8 * kv + 8)
                for half in range(2):
                    n = N_CMP + 2 * kv + half
                    pe.wait_ge(raw_loaded[n % 2], loaded[n])
                    w1 = view(raw, n % 2, 8, 256)
                    for p in range(8 * half, 8 * half + 8):
                        for hc in range(2):
                            last = mm(bank[2 + kv][:, 60 * hc:60 * hc + 60], w1[:, p % 8, 128 * hc:128 * hc + 128],
                                      blkT[:, kv, p, :], start=p == 0 and hc == 0, stop=p == 15, skip_group_check=True)
                    last.then_inc(cmp_hid, 1)
            pe.wait_ge(cmp_act, 2)
            pe.wait_ge(small_loaded, 16 * SMALL_DMAS)
            for hc in range(2):
                mm(bank[3][:, 0:60], w2k_sb[:, hc, :], hidT[:, 0, hc, :], start=hc == 0, stop=hc == 1)
            for g in range(4):
                for hc in range(2):
                    last = mm(bank[3][0:NCMP, 64 + 64 * g:128 + 64 * g], hidT[:, 1, hc, NCMP * g:NCMP * g + NCMP],
                              w2v_sb[:, hc, :], start=hc == 0, stop=hc == 1)
            last.then_inc(cmp_kv, 1)
            pe.wait_ge(cmp_kv_taken, 6)
            pe.wait_ge(roped, NSA_ROPED)

            def q_of(ci, qb):
                return big1[:, ci, 128 * qb:128 * qb + 128]

            for qb in range(2):
                for h in range(16):
                    g, a = h // 4, h % 2
                    c = NCMP * (16 * qb + h)
                    last = mm(bank[2][:, c:c + NCMP], q_of(h // 2, qb), kcT[:, a, NCMP * g:NCMP * g + NCMP],
                              start=True, stop=True, skip_group_check=True)
            last.then_inc(cmp_scores, 1)

            def cmp_turn():
                pe.wait_ge(cmp_probs, 1)
                pe.wait_ge(vt_taken, 3)
                for qb in range(2):
                    turn([(bank[6 + qb][:, 128 * hg:128 * hg + 128],
                                   c_p[:, 16 * qb + 4 * hg:16 * qb + 4 * hg + 4, :].rearrange("p h c -> p (h c)"))
                                  for hg in range(4)], cmp_turned)

            def unit_scores(v, u, nsa):
                ci, kind = u
                if v >= 2:
                    pe.wait_ge(at_exp, v - 1)
                S = bank[4 + v % 2]
                causal, before = mask_b[:, 128:256], mask_b[:, 0:128]
                if nsa:
                    ks = [[big1[:, K_AT + 2 * (4 * b + ci // 2) + a, :] for a in range(2)] for b in range(2)]
                    if kind == "first":
                        mm(S[:, :], ident_b[:, :], each(causal, 4), start=True, stop=False, skip_group_check=True)
                        for a in range(2):
                            for b in range(2):
                                o = 256 * a + 128 * b
                                last = mm(S[:, o:o + 128], q_of(ci, 0), ks[b][a][:, 0:128],
                                          start=False, stop=True, skip_group_check=True)
                    else:
                        a = int(kind[-1])
                        mm(S[:, :].rearrange("p (b k) -> p b k", b=2)[:, :, 128:256], ident_b[:, :], each(causal, 2),
                           start=True, stop=False, skip_group_check=True)
                        for b in range(2):
                            last = mm(S[:, 256 * b:256 * b + 256], q_of(ci, 1), ks[b][a],
                                      start=False, stop=True, skip_group_check=True)
                else:
                    k = [big1[:, K_AT + 2 * (ci // 4) + a, :] for a in range(2)]
                    if kind == "first":
                        mm(S[:, 0:256], ident_b[:, :], each(causal, 2), start=True, stop=False, skip_group_check=True)
                        for a in range(2):
                            last = mm(S[:, 128 * a:128 * a + 128], q_of(ci, 0), k[a][:, 0:128],
                                      start=False, stop=True, skip_group_check=True)
                    else:
                        mm(S[:, :], ident_b[:, :], each(mask_b[:, :], 2), start=True, stop=False, skip_group_check=True)
                        for a in range(2):
                            last = mm(S[:, 256 * a:256 * a + 256], q_of(ci, 1), k[a],
                                      start=False, stop=True, skip_group_check=True)
                last.then_inc(at_scores, 1)

            def unit_turn(v, u, nsa):
                pe.wait_ge(at_probs, v + 1)
                if v >= 2:
                    pe.wait_ge(at_pt, v - 1)
                n = 2 if not nsa and u[1] == "first" else 4
                turn([(bank[6 + v % 2][:, 128 * i:128 * i + 128], S_p[:, v % 2, 128 * i:128 * i + 128])
                         for i in range(n)], at_turned)

            def unit_pv(v, u, nsa, c0):
                ci, kind = u
                pe.wait_ge(at_pt, v + 1)
                if kind == "first" and c0 + ci >= 2:
                    pe.wait_ge(at_out, c0 + ci - 1)
                O = bank[out_bank(ci, nsa)]

                def piece(a, qb, i, w, kb, g, first=False):
                    return mm(O[64 * a:64 * a + 64, 128 * qb:128 * qb + 128], vtok[:, w, kb, 64 * g:64 * g + 64],
                              S_pt[:, v % 2, 128 * i:128 * i + 128], start=first, stop=True, skip_group_check=True)

                if nsa:
                    g = ci // 2
                    if kind == "first":
                        for a in range(2):
                            r = (2 * ci + a) % 4
                            mm(O[64 * a:64 * a + 64, 0:256], vc_rep[32 * r:32 * r + NCMP, 64 * g:64 * g + 64],
                               c_pt[32 * r:32 * r + NCMP, :, g, :], start=True, stop=False, skip_group_check=True)
                            for b in range(2):
                                last = piece(a, 0, 2 * a + b, b, 0, g)
                    else:
                        a = int(kind[-1])
                        for b in range(2):
                            for kb in range(2):
                                last = piece(a, 1, 2 * b + kb, b, kb, g)
                elif kind == "first":
                    for a in range(2):
                        last = piece(a, 0, a, 0, 0, ci // 4, first=True)
                else:
                    for a in range(2):
                        for kb in range(2):
                            last = piece(a, 1, 2 * a + kb, 0, kb, ci // 4)
                last.then_inc(at_pv, 1)

            def attention(units, v0, nsa, c0):
                for i in range(len(units) + 2):
                    if i < len(units):
                        unit_scores(v0 + i, units[i], nsa)
                    if nsa and i == 1:
                        cmp_turn()
                        pe.wait_ge(cmp_pt, 2)
                    if 1 <= i <= len(units):
                        unit_turn(v0 + i - 1, units[i - 1], nsa)
                    if i >= 2:
                        unit_pv(v0 + i - 2, units[i - 2], nsa, c0)

            attention(NSA_UNITS, 0, True, 0)

            def out_proj(m0, ready, T, norm, K=KC, source=(xh, xl)):
                for c in range(8):
                    if c % (16 // K) == 0:
                        parts = split(m0 + c // (16 // K))
                    chunk(parts, c % (16 // K), K, 128, T, ready if c == 0 else None, source)
                    if norm is not None and c >= 2:
                        sum_squares(norm, T, c - 2, c - 1)
                if norm is not None:
                    sum_squares(norm, T, 6, 8)

            def ffn(l, T, norm):
                m0, n0 = ffn_at[l][1], N_FFN[l]
                assert line["n"] == n0, (line["n"], n0)
                pe.wait_ge(proj_taken, n0)

                def up(b, m, n, q0, stream=None):
                    pe.wait_ge(w_lo, m + 1)
                    parts = view(w_h, b, KC, 256), view(w_l, b, KC, 256)
                    for q in range(2):
                        pe.wait_ge(proj_taken, n + q - 3)
                        for k in range(KC):
                            if stream is not None and q == 0:
                                pe.wait_ge(xl_ready, 8 * stream + k + 1)
                            last = product(bank[q0 + q][:, 0:T], parts, k, slice(128 * q, 128 * q + 128), xh[:, k, 0:T],
                                           xl[:, k, 0:T], k == 0, k == KC - 1)
                        last.then_inc(proj_done, 1)

                up(m0 % 2, m0, n0, 0, STREAMS[norm - 1])
                up((m0 + 1) % 2, m0 + 1, n0 + 2, 2)
                with pe.Fori(0, (FC - 2) // 2) as i:
                    for j in range(2):
                        up((m0 + j) % 2, i * 2 + (m0 + 2 + j), i * 4 + (n0 + 4 + 2 * j), 2 * j)
                line["n"] += 2 * FC
                hh, hl = hidden(hid_h, T), hidden(hid_l, T)
                for g in range(2):
                    for part, (k0, k1) in enumerate(DOWN_PARTS):
                        parts = split(m0 + FC + len(DOWN_PARTS) * g + part)
                        pe.wait_ge(hidden_ready, FC * l + k1)
                        for c in range(4):
                            if part == 0 and (g == 0 or c == 3):
                                pe.wait_ge(proj_taken, line["n"] + c - 3)
                            for k in range(k0, k1):
                                last = product(bank[down_bank(44 + 4 * g + c)][:, 0:T], parts, k - k0, slice(128 * c, 128 * c + 128), hh[:, k, :],
                                               hl[:, k, :], k == 0, k == FC - 1)
                            if k1 == FC:
                                last.then_inc(proj_done, 1)
                        if k1 < FC:
                            last.then_inc(down_part, 1)
                        if g and part == 0:
                            sum_squares(norm, T, 0, 4)
                    line["n"] += 4
                sum_squares(norm, T, 4, 8)

            out_proj(11, (at_out, 0), T1, 1, source=(at_h, at_l))
            ffn(0, T1, 2)

            for n in range(10):
                if n % 2 == 0:
                    parts = split(M_SWA + n // 2)
                chunk(parts, n % 2, KC, 128, T1, (xl_ready, 8 * STREAMS[2]) if n == 0 else None)
                if n >= 1 and is_roped(SWA[n - 1]):
                    permute((biased, n))
                if n == 3:
                    pe.wait_ge(biased, 2)
                    turn([(bank[6][:, 128 * kb:128 * kb + 128], big1[:, 9, 128 * kb:128 * kb + 128]) for kb in range(2)],
                         vt_done)
            permute((biased, 10))
            pe.wait_ge(roped, NSA_ROPED + SWA_ROPED)
            pe.wait_ge(vt_taken, 4)
            pe.wait_ge(proj_taken, N_SWA + 10)
            attention(SWA_UNITS, V_SWA, False, 8)
            out_proj(M_SWA + 5, (at_out, 8), T1, 3, source=(at_h, at_l))
            ffn(1, T1, 4)

            sum_squares(5, T2, 0, 8)
            for n in range(53):
                if n <= 36 and n % 2 == 0 or n > 36 and n % 2:
                    parts = split(M_IN2 + (n // 2 if n <= 36 else 19 + (n - 37) // 2))
                chunk(parts, 0 if n == 36 else n % 2 if n < 36 else (n - 37) % 2, KC, 16 if n == 36 else 128, T2,
                      (xl_ready, 8 * STREAMS[5]) if n == 0 else None)

            pe.wait_ge(proj_taken, N_IN2 + 53)
            for tb in range(3):
                w = min(128, T2 - 128 * tb)
                turn([(bank[4 + tb][0:w, 128 * c:128 * c + 128], big2[:, 8 + c, 128 * tb:128 * tb + w])
                              for c in range(4)], vt_done)
            pe.wait_ge(vt_taken, 4 + 3)
            pe.wait_ge(kpad_ready, 1)
            Z = [bank[0], bank[1], bank[4], bank[5]]
            parts = [(0, 0, T2), (1, 272, 144), (2, 416, 16)]

            def z_score(i):
                if i >= 4:
                    pe.wait_ge(z_weights, i - 3)
                c, a = i // 2, i % 2
                for b, at, w in parts:
                    k = kpad[64 * a:64 * a + 64, c, :] if b == 2 else big2[64 * a:64 * a + 64, 4 + c, 128 * b:128 * b + 128]
                    last = mm(Z[i % 4][:, at:at + w], k, big2[64 * a:64 * a + 64, c, T2 - w:T2], start=b == 0, stop=True,
                              skip_group_check=True)
                last.then_inc(z_scores, 1)

            def z_sum(i):
                pe.wait_ge(z_soft, i + 1)
                for b, at, w in parts:
                    for b2, at2, w2 in parts[b:]:
                        last = mm(Z[i % 4][:, at + w - w2:at + w], L("tri") if b2 == b else L("all"),
                                  z_u[:, i % 2, at2:at2 + w2], start=False, stop=True, skip_group_check=True)
                mm(Z[i % 4][:, 0:ZW], ident_b[:, :], L("sbneg"), start=False, stop=True, skip_group_check=True)\
                    .then_inc(z_tri, 1)

            def z_value(i):
                pe.wait_ge(z_weights, i + 1)
                c, a = i // 2, i % 2
                if a == 0 and c >= 2:
                    pe.wait_ge(z_out, c - 1)
                for b, at, w in parts:
                    n = 16 if b == 2 else 128
                    last = mm(bank[2 + c % 2][64 * a:64 * a + 64, T2 - w:T2], sv_tok[0:n, b, 64 * i:64 * i + 64],
                              z_w[0:n, i % 2, at:at + w], start=b == 0, stop=True, skip_group_check=True)
                last.then_inc(z_pv, 1)

            for i in range(8 + 2):
                if i < 8:
                    z_score(i)
                if 1 <= i <= 8:
                    z_sum(i - 1)
                if i >= 2:
                    z_value(i - 2)

            out_proj(M_SBO, (z_out, 0), T2, None, K=4)

            pe.wait_ge(proj_taken, N_GLO)
            pe.wait_ge(up_loaded, 16)
            for n in range(GN):
                last = mm(bank[n][:, 0:T2], up_sb[0:16, 128 * n:128 * n + 128], glr[0:16, :], start=True, stop=True)
            last.then_inc(g_log, 1)
            for tb in range(3):
                w = min(128, T2 - 128 * tb)
                for half in range(2):
                    i = 2 * tb + half
                    if i >= 4:
                        pe.wait_ge(vt_taken, 7 + i - 3)
                    turn([(bank[4 + i % 4][0:w, 128 * c:128 * c + 128], big2[:, 20 + 4 * half + c, 128 * tb:128 * tb + w])
                             for c in range(4)], vt_done)

            def level(lv):
                if lv == 0:
                    pe.wait_ge(g_x, GN)
                    pe.wait_ge(vt_taken, 7 + 6)
                    q, k = big2[:, 12:16, :], big2[:, 16:20, :]
                else:
                    pe.wait_ge(g_qk, lv)
                    q = g_q[:, lv % 2, :].rearrange("p (n t) -> p n t", n=GN)
                    k = g_k[:, lv % 2, :].rearrange("p (n t) -> p n t", n=GN)
                if lv >= 2:
                    pe.wait_ge(g_sel, lv - 1)
                for ck in range(2):
                    for n in range(GN):
                        last = mm(bank[2 * (lv % 2) + ck][:, 128 * n:128 * n + 128], k[:, n, 128 * ck:128 * ck + 128],
                                  q[:, n, 128 * ck:128 * ck + 128], start=True, stop=True, skip_group_check=True)
                if lv <= 4:
                    for n in range(GN):
                        last = mm(bank[4 + lv % 2][0:16, 16 * n:16 * n + 16], k[:, n, 256:T2], q[:, n, 256:T2],
                                  start=True, stop=True, skip_group_check=True)
                last.then_inc(g_att, 1)

            for lv in range(LEVELS + 1):
                level(lv)
            pe.wait_ge(k_dec, 1)
            for ck in range(2):
                turn([(bank[6 + ck][:, 128 * n:128 * n + 128],
                          g_k[:, 0, :].rearrange("p (n t) -> p n t", n=GN)[:, n, 128 * ck:128 * ck + 128])
                         for n in range(GN)], k_turned)
            pe.wait_ge(g_sel, LEVELS + 1)
            for ck in range(2):
                pe.wait_ge(k_tok, ck + 1)
                for n in range(GN):
                    last = mm(bank[2 * ck + 4 * (1 - ck) + n // 2][:, 256 * (n % 2):256 * (n % 2) + 256],
                              kdT[:, ck, 128 * n:128 * n + 128], gv_tok[:, ck, 256 * n:256 * n + 256],
                              start=True, stop=True, skip_group_check=True)
                last.then_inc(s_done, 1)
            pe.wait_ge(state2, GN)
            pe.wait_ge(q_dec, 1)
            for o in range(8):
                n, dv = o // 2, o % 2
                b = bank[o % 4]
                if o >= 4:
                    pe.wait_ge(go_taken, o - 3)
                cols = slice(256 * n + 128 * dv, 256 * n + 128 * dv + 128)
                qt = g_q[:, 0, :].rearrange("p (n t) -> p n t", n=GN)
                mm(b[:, 0:128], gv_tok[:, 0, cols], att[:, 0, n, :], start=True, stop=True, skip_group_check=True)
                mm(b[:, 128:256], gv_tok[:, 1, cols], att[:, 1, n, :], start=False, stop=True, skip_group_check=True)
                mm(b[:, 128:256], s1[:, n, 128 * dv:128 * dv + 128], qt[:, n, 128:256], start=False, stop=True,
                   skip_group_check=True)
                mm(b[:, 256:T2], gv_tok[0:16, 2, cols], att2[0:16, n, :], start=False, stop=True, skip_group_check=True)
                mm(b[:, 256:T2], s2[:, n, 128 * dv:128 * dv + 128], qt[:, n, 256:T2], start=False, stop=True,
                   skip_group_check=True).then_inc(go_done, 1)
            for n in range(GN):
                for dv in range(2):
                    pe.wait_ge(go_sq, 2 * n + dv + 1)
                    mm(bank[4 + n][:, 0:T2], ones, sq[:, (2 * n + dv) % 4, :], start=dv == 0, stop=dv == 1).then_inc(go_ss, 1)

            out_proj(M_GLO, (go_ready, 0), T2, None)
            out_proj(M_GLO + 4, (mix_ready, 0), T2, 6)
            sum_squares(7, T2, 0, 8)
            ffn(2, T2, 8)
            for tb in range(2):
                for half in range(2):
                    pe.wait_ge(h2_ready, 24 if half else 20)
                    i = 2 * tb + half
                    turn([(bank[i][:, 128 * c:128 * c + 128],
                              h2[:, 4 * half + c, META + 128 * tb:META + 128 * tb + 128]) for c in range(4)], y_turned)

        @block.scalar
        def _(act):
            line = Line(act, act_step)
            fn = nc.scalar.activation

            def high(m):
                n = split_at[m]
                act.wait_ge(raw_loaded[n % 2], loaded[n])
                if m >= 2:
                    act.wait_ge(*used[m - 2])
                size = sizes[n][0] * sizes[n][1]
                fn(w_h[:, m % 2, 0:size], raw[:, n % 2, 0:size], ACT.Copy).then_inc(w_hi, 1)
            act.dma_start(early[:, :], A["early_c"]).then_inc(early_loaded, 16)
            for tb in range(2):
                act.dma_start(x_in[:, tb, :], A["x"][0][128 * tb:128 * tb + 128, :]).then_inc(x_loaded, 16)
            act.wait_ge(prepared, 1)
            for dst, src in vec_loads:
                act.dma_start(dst, src).then_inc(vec_loaded, 16)
            w2 = [A["nsa_cmp_w2"][0][kv].rearrange("(c p) d -> p c d", p=128) for kv in range(2)]
            for dst, src in ((w2k_sb[:, :, 0:64], w2[0]), (w2k_sb[:, :, 64:128], w2[0]), (w2v_sb, w2[1])):
                act.dma_start(dst, src).then_inc(small_loaded, 16)
            act.dma_start(sinks, A["swa_sinks"][0].unsqueeze(0).broadcast_to([128, 16])).then_inc(small_loaded, 16)
            act.dma_start(late_in, A["late_c"]).then_inc(late_loaded, 16)
            high(0)
            high(1)

            def squares(i, T, src, ready, after=None):
                for c in range(8):
                    act.wait_ge(*ready(c))
                    if c >= 4:
                        act.wait_ge(ss_step, 8 * i + c - 3)
                    if c % 2 and i in STREAMS:
                        line.put(fn(xh[:, c, 0:T], src[:, c, 0:T], ACT.Copy, scale=vec("g", 8 * i + c)), xh_odd)
                    line.put(fn(sq[:, c % 4, 0:T], src[:, c, 0:T], ACT.Square), sq_ready)
                    if after is not None:
                        after(c)
                act.wait_ge(ss_step, 8 * i + 8)
                line.put(fn(root[:, 0:T], bank[7][:, 0:T], ACT.Sqrt, bias=eps_col[:, 0:1]), root_ready)

            def taken(n0):
                return lambda c: (proj_taken, n0 + c + 1)

            squares(0, T1, xT, lambda c: (turn_taken, 4 + c // 2))
            for m in range(2, 10):
                high(m)
            for w in range(2):
                act.wait_ge(vt_done, w + 1)
                line.put(fn(vtok[:, w, :, :].rearrange("p a b -> p (a b)"), bank[6 + w][:, :], ACT.Copy), vt_taken)
            high(10)
            act.wait_ge(vt_done, 3)
            line.put(fn(egate.rearrange("p a b -> p (a b)"), bank[6][:, 0:96], ACT.Exp, scale=-1.0), vt_taken)
            for kv in range(2):
                act.wait_ge(cmp_hid, 2 * kv + 2)
                line.put(fn(hidT[:, kv, :, :].rearrange("p b c -> p (b c)"), bank[2 + kv][:, 0:120], ACT.Gelu_apprx_tanh), cmp_act)
            act.wait_ge(cmp_kv, 1)
            act.wait_ge(prepared, 5)
            for a in range(2):
                half = slice(64 * a, 64 * a + 64)
                line.put(fn(kcT[half, a, :], bank[3][half, 0:60], ACT.Copy), cmp_kv_taken)
            for r in range(4):
                line.put(fn(vc_rep[32 * r:32 * r + NCMP, :], bank[3][0:NCMP, 64:320], ACT.Copy), cmp_kv_taken)

            def attention(units, v0, nsa, c0):
                for i in range(len(units) + 3):
                    if i < len(units):
                        v = v0 + i
                        first = units[i][1] == "first"
                        act.wait_ge(at_neg, v + 1)
                        if v >= 2:
                            act.wait_ge(at_turned, v - 1)
                        n, w = (4 if nsa else 2, 128) if first else (2, 256)
                        for k in range(n):
                            ins = fn(S_p[:, v % 2, w * k:w * k + w], bank[4 + v % 2][:, w * k:w * k + w], ACT.Exp,
                                     scale=SCALE, bias=st_neg[:, v % 2, k:k + 1], accum_out=st_den[:, v % 2, k:k + 1])
                        line.put(ins, at_exp)
                        if not nsa:
                            act.wait_ge(at_sink, v - v0 + 1)
                            line.put(fn(st_es[:, v % 2, 0:2], st_es[:, v % 2, 0:2], ACT.Exp), at_sinkexp)
                    if nsa and i == 0:
                        act.wait_ge(cmp_centered, 1)
                        line.put(fn(c_e, c_s, ACT.Exp, scale=SCALE), cmp_exp)
                    if nsa and i == 1:
                        for qb in range(2):
                            act.wait_ge(cmp_turned, qb + 1)
                            line.put(fn(c_pt[:, qb, :, :].rearrange("p a b -> p (a b)"), bank[6 + qb][:, :], ACT.Copy), cmp_pt)
                    j = i - 3
                    if j >= 0 and units[j][1] in ("second", "second1"):
                        act.wait_ge(at_pv, v0 + j + 1)
                        ci = units[j][0]
                        line.put(fn(at_h[:, ci, :], bank[out_bank(ci, nsa)][:, 0:256], ACT.Copy), at_high)

            high(11)
            high(12)
            attention(NSA_UNITS, 0, True, 0)
            squares(1, T1, xT, taken(N_NSA_O), lambda c: high(13 + c // 2) if c % 2 else None)

            def ffn(l, T, func):
                n0, m0 = ffn_at[l]

                def step(k, n, p, w0, b, slab, target, m, first):
                    act.wait_ge(proj_taken, n + 1)
                    if not first:
                        act.wait_ge(conv_mid, k - 1)
                    fn(f_c1[:, p, 0:T], f_a[:, p, 0:T], ACT.Identity, scale=w0, bias=b).then_inc(c1_ready, 1)
                    act.wait_ge(raw_loaded[slab], target)
                    act.wait_ge(proj_done, n + 2)
                    fn(w_h[:, m, :], raw[:, slab, :], ACT.Copy).then_inc(w_hi, 1)
                    act.wait_ge(conv_ready, k + 1)
                    if not first:
                        act.wait_ge(hid_full, k - 1)
                    fn(f_s[:, p, 0:T], f_c3[:, p, 0:T], func).then_inc(act_ready, 1)

                def tap(name, f):
                    at = vcolc[name][0]
                    if isinstance(f, int):
                        return vecs[:, 1 + l, at + f:at + f + 1]
                    return vecs[:, 1 + l, bass.ds(f + at, 1)]

                for f in range(2):
                    step(FC * l + f, N_FFN[l] + 2 * f, f, tap("w0", f), tap("b", f), (n0 + f) % 2, loaded[n0 + f + 2],
                         (m0 + f) % 2, l == 0)
                with act.Fori(0, (FC - 2) // 2) as i:
                    for j in range(2):
                        step(i * 2 + (FC * l + 2 + j), i * 4 + (N_FFN[l] + 4 + 2 * j), j, tap("w0", i * 2 + (2 + j)),
                             tap("b", i * 2 + (2 + j)), (n0 + j) % 2, i * 32 + loaded[n0 + 4 + j], (m0 + j) % 2, False)

            def down(l, i, T):
                m = ffn_at[l][1] + FC
                highs = lambda a, b: [high(m + x) for x in range(a, b) if m + x < len(split_at)]
                highs(2, 8)
                squares(i, T, xT, taken(N_FFN[l] + 44), lambda c: highs(8, 12) if c == 3 else highs(12, 13) if c == 7 else None)
                highs(13, 14)

            ffn(0, T1, ACT.Silu)
            down(0, 2, T1)
            rope = 0
            for n in range(10):
                place, r = SWA[n][0], is_roped(SWA[n])
                act.wait_ge(proj_taken, N_SWA + n + 1)
                t = xs[:, (NSA_ROPED + rope) % 2, :] if r else big1[:, place, :]
                line.put(fn(t, t, ACT.Identity, bias=vec("bqkv", 8 if n == 0 else 9 if n == 1 else n - 2)), biased)
                rope += r
                if n % 2:
                    high(M_SWA + 2 + n // 2)
                if n == 3:
                    act.wait_ge(vt_done, 4)
                    line.put(fn(vtok[:, 0, :, 0:128], bank[6][:, 0:256].rearrange("p (a b) -> p a b", a=2), ACT.Copy),
                             vt_taken)
            attention(SWA_UNITS, V_SWA, False, 8)
            squares(3, T1, xT, taken(N_SWA_O), lambda c: high(M_SWA + 7 + c // 2) if c % 2 else None)
            ffn(1, T1, ACT.Silu)
            down(1, 4, T1)
            squares(5, T2, h2, lambda c: (h2_ready, c + 1))
            for m in range(M_IN2 + 2, M_IN2 + 17):
                high(m)
            for c in range(8):
                act.wait_ge(proj_taken, N_IN2 + 28 + c + 1)
                t = big2[:, 28 + c, :]
                line.put(fn(t, t, ACT.Silu))
                if c % 2:
                    high(M_IN2 + 17 + c // 2)
            for c in range(16):
                act.wait_ge(proj_taken, N_IN2 + 37 + c + 1)
                t = big2[:, 36 + c, :]
                line.put(fn(t, t, ACT.Sigmoid))
                if c % 2:
                    high(M_IN2 + 21 + c // 2)
            for tb in range(3):
                w = min(128, T2 - 128 * tb)
                act.wait_ge(vt_done, 5 + tb)
                line.put(fn(sv_tok[0:w, tb, :], bank[4 + tb][0:w, :], ACT.Copy), vt_taken)
            Z = [bank[0], bank[1], bank[4], bank[5]]

            def z_final(i):
                act.wait_ge(z_tri, i + 1)
                if i >= 2:
                    act.wait_ge(z_pv, i - 1)
                line.put(fn(z_w[:, i % 2, :], Z[i % 4][:, 0:ZW], ACT.Exp, scale=SCALE), z_weights)

            def z_evac(i):
                if i % 2:
                    act.wait_ge(z_pv, i + 1)
                    line.put(fn(xh[:, i // 2, :], bank[2 + (i // 2) % 2][:, 0:T2], ACT.Copy), z_high)

            for i in range(8):
                act.wait_ge(z_abs, i + 1)
                if i >= 2:
                    act.wait_ge(z_soft, i - 1)
                line.put(fn(z_l[:, i % 2, :], z_a[:, i % 2, :], ACT.Exp, scale=-SCALE))
                line.settle()
                line.put(fn(z_l[:, i % 2, :], z_l[:, i % 2, :], ACT.Ln, bias=1.0), z_ln)
                if i >= 1:
                    z_final(i - 1)
                if i >= 2:
                    z_evac(i - 2)
            z_final(7)
            z_evac(6)
            z_evac(7)
            high(M_GLO)
            high(M_GLO + 1)
            act.wait_ge(g_abs, 1)
            ga = g_d[:, 1, :]
            line.put(fn(ga, ga, ACT.Exp, scale=-1.0))
            line.settle()
            line.put(fn(ga, ga, ACT.Ln, bias=1.0), g_ln)
            for i in range(6):
                tb, half = i // 2, i % 2
                w = min(128, T2 - 128 * tb)
                act.wait_ge(vt_done, 8 + i)
                line.put(fn(gv_tok[0:w, tb, 512 * half:512 * half + 512], bank[4 + i % 4][0:w, :], ACT.Copy), vt_taken)
            for lv in range(1, LEVELS + 1):
                act.wait_ge(g_dist, lv)
                line.put(fn(g_d[:, lv % 2, :], g_d[:, lv % 2, :], ACT.Exp, scale=-1.0 / 16), g_decay)
            act.wait_ge(k_dist, 1)
            line.put(fn(g_d[:, 0, :], g_d[:, 0, :], ACT.Exp, scale=-1.0 / 16), k_decay)
            line.put(fn(cum, cum, ACT.Exp, scale=-1.0 / 16), q_decay)
            for ck in range(2):
                act.wait_ge(k_turned, ck + 1)
                line.put(fn(kdT[:, ck, :], bank[6 + ck][:, :], ACT.Copy), k_tok)
            act.wait_ge(s_done, 1)
            for half in range(2):
                ins = fn(s1[:, 2 * half:2 * half + 2, :].rearrange("p a b -> p (a b)"), bank[4 + half][:, :], ACT.Copy)
                if half:
                    line.put(ins, s_taken)
            for o in range(8):
                act.wait_ge(go_taken, o + 1)
                if o >= 4:
                    act.wait_ge(go_ss, o - 3)
                line.put(fn(sq[:, o % 4, :], g_o[:, o, :], ACT.Square), go_sq)
            rs = g_d[:, 1, :].rearrange("p (n t) -> p n t", n=GN)
            for n in range(GN):
                act.wait_ge(go_ss, 2 * n + 2)
                line.put(fn(rs[:, n, :], bank[4 + n][:, 0:T2], ACT.Sqrt, scale=float(D // 256), bias=eps_col[:, 0:1]), go_root)
            for o in range(8):
                act.wait_ge(go_full, o + 1)
                line.put(fn(xh[:, o, :], g_o[:, o, :], ACT.Copy), go_high)
            for c in range(8):
                if c % 2:
                    high(M_GLO + 2 + c // 2)
            for c in range(8):
                act.wait_ge(mix_full, c + 1)
                line.put(fn(xh[:, c, :], big2[:, 36 + c, :], ACT.Copy), mix_high)
            squares(6, T2, xT, taken(N_WO2), lambda c: high(M_GLO + 6 + c // 2) if c % 2 else None)
            squares(7, T2, h2, lambda c: (h2_ready, 8 + c + 1))
            ffn(2, T2, ACT.Gelu_apprx_tanh)
            down(2, 8, T2)
            o_sb = big[:, 0:2048].rearrange("p (b n) -> p b n", b=2)
            for i in range(4):
                act.wait_ge(y_turned, i + 1)
                line.put(fn(o_sb[:, i // 2, 512 * (i % 2):512 * (i % 2) + 512], bank[i][:, :], ACT.Copy), y_taken)

        @block.vector
        def _(dve):
            line = Line(dve, dve_step)
            V = nc.vector

            def factor(i, T):
                dve.wait_ge(root_ready, i + 1)
                line.put(V.reciprocal(rstd[:, 0:T], root[:, 0:T]))
                line.settle()

            def low(m):
                n = split_at[m]
                size = sizes[n][0] * sizes[n][1]
                dve.wait_ge(w_hi, m + 1)
                V.tensor_tensor(w_l[:, m % 2, 0:size], raw[:, n % 2, 0:size], w_h[:, m % 2, 0:size].bitcast(F32), ALU.subtract)\
                    .then_inc(w_lo, 1)

            def stream_low(i, T, src, c):
                dve.wait_ge(xh_odd if c % 2 else xh_even, 4 * STREAMS[i] + c // 2 + 1)
                line.put(V.scalar_tensor_tensor(out=xl[:, c, 0:T], in0=src[:, c, 0:T], scalar=vec("g", 8 * i + c),
                                                in1=xh[:, c, 0:T].bitcast(F32), op0=ALU.mult, op1=ALU.subtract), xl_ready)

            def take(n, dst, M, T, signal=proj_taken):
                dve.wait_ge(proj_done, n + 1)
                line.put(V.tensor_tensor(dst, bank[n % 4][0:M, 0:T], rstd[0:M, 0:T], ALU.mult), signal)

            dve.wait_ge(turn_done, 1)
            line.put(V.tensor_copy(vecs[:, :, :],
                                   bank[4][:, :].rearrange("p (a b) -> p a b", a=4)), turn_taken)
            dve.wait_ge(turn_done, 2)
            line.put(V.tensor_copy(pe_dup, bank[5][:, 0:64].rearrange("p (a b) -> p a b", a=2)), turn_taken)
            dve.wait_ge(turn_done, 3)
            line.put(V.tensor_copy(h2[:, :, 0:META], bank[6][:, 0:128].rearrange("p (a b) -> p a b", a=8)), turn_taken)
            for b in range(4):
                dve.wait_ge(turn_done, 4 + b)
                line.put(V.tensor_copy(xT[:, 2 * b:2 * b + 2, 0:T1], bank[b][:, :].rearrange("p (a b) -> p a b", a=2)),
                         turn_taken)
            low(0)
            for c in range(8):
                stream_low(0, T1, xT, c)
            low(1)
            factor(0, T1)

            rope = {"k": 0}

            def rope_sin():
                k = rope["k"]
                dve.wait_ge(perm_done, k + 1)
                if k >= 2:
                    dve.wait_ge(roped, k - 1)
                line.put(V.tensor_tensor(tsin[:, k % 2, :], bank[4 + k % 2][:, 0:T1], E("sin"), ALU.mult), sin_done)
                rope["k"] += 1

            def projections(n0, table, each_after):
                k0 = rope["k"]
                seen = 0
                for i, entry in enumerate(table):
                    place, r = entry[0], is_roped(entry)
                    if r:
                        k = k0 + seen
                        if k >= 2:
                            dve.wait_ge(perm_done, k - 1)
                            dve.wait_ge(cos_done, k - 1)
                        dst, seen = xs[:, k % 2, :], seen + 1
                    else:
                        dst = big1[:, place, :]
                    if n0 == 0 and i == 12:
                        take(n0 + i, dst[0:48], 48, T1)
                    else:
                        take(n0 + i, dst, 128, T1)
                    if i >= 1 and is_roped(table[i - 1]):
                        rope_sin()
                    each_after(i)
                rope_sin()

            def nsa_extra(i):
                if i < 12 and i % 2 or i >= 12 and i % 2 == 0:
                    m = i // 2 if i < 12 else 6 + (i - 12) // 2
                    if m + 2 <= 10:
                        low(m + 2)
                if i == 12:
                    line.settle()
                    line.put(V.tensor_scalar(big1[0:48, 16, :], big1[0:48, 16, :],
                                             vecs[0:48, 0, vcol0["gb"][0]:vcol0["gb"][0] + 1], None, ALU.add), gate_moved)
                if i in (14, 16):
                    kv = (i - 14) // 2
                    dve.wait_ge(roped, 2)
                    for a in range(2):
                        for par in range(2):
                            for lh in range(2):
                                src = big1[64 * a:64 * a + 64, 8 + 2 * kv:10 + 2 * kv, :]\
                                    .rearrange("p j (c l s) -> p j c l s", l=8, s=2)[:, :, lh:lh + NCMP, :, par]
                                dst = blkT[64 * par:64 * par + 64, kv, 8 * lh:8 * lh + 8, :]\
                                    .rearrange("p l (j a c) -> p a j c l", j=2, a=2)[:, a]
                                pos = pe_dup[64 * a:64 * a + 64, kv, 16 * lh:16 * lh + 16]\
                                    .rearrange("p (l s) -> p l s", s=2)[:, :, par]
                                pos = each(each(pos, NCMP), 2)
                                line.put(V.tensor_tensor(dst, src, pos, ALU.add), blk_ready)
                if i == 18:
                    dve.wait_ge(vt_taken, 3)
                    e = egate.rearrange("p a b -> p (a b)")
                    line.put(V.tensor_scalar(e, e, 1.0, None, ALU.add))
                    line.settle()
                    line.put(V.reciprocal(gates.rearrange("p a b -> p (a b)"), e), gates_ready)

            projections(0, NSA, nsa_extra)

            gate_of = gates.rearrange("p q (c a b) -> p q c a b", c=8, a=2)

            def cmp_softmax():
                dve.wait_ge(cmp_scores, 1)
                neg = E("cmpneg").rearrange("p (q c) -> p q c", q=2)
                line.put(V.tensor_tensor(c_s.rearrange("p (q h) c -> p q h c", q=2),
                                         bank[2][:, 0:480].rearrange("p (q h c) -> p q h c", q=2, h=16),
                                         each(neg, 16, axis=2), ALU.add))
                line.settle()
                line.put(V.tensor_reduce(c_mx, c_s, AX.X, ALU.max))
                line.settle()
                line.put(V.tensor_scalar(c_mx, c_mx, -1e20, None, ALU.max))
                line.settle()
                line.put(V.tensor_tensor(c_s, c_s, each(c_mx, NCMP, axis=2), ALU.subtract), cmp_centered)

            def cmp_norm():
                dve.wait_ge(cmp_exp, 1)
                dve.wait_ge(prepared, 3)
                line.put(V.tensor_reduce(c_den, c_e, AX.X, ALU.add))
                line.settle()
                line.put(V.tensor_scalar(c_den, c_den, 1e-6, None, ALU.max))
                line.settle()
                line.put(V.reciprocal(c_mx, c_den))
                line.settle()
                line.put(V.tensor_tensor(c_den.rearrange("p (q h) -> p q h", q=2), c_mx.rearrange("p (q h) -> p q h", q=2),
                                         gates.rearrange("p q (h b) -> p q h b", b=3)[:, :, :, 0], ALU.mult))
                line.settle()
                line.put(V.tensor_tensor(c_p[:, :, 0:NCMP], c_e, each(c_den, NCMP, axis=2), ALU.mult), cmp_probs)

            def attention_low(ci, c0, nsa):
                dve.wait_ge(at_high, c0 + ci + 1)
                line.put(V.tensor_tensor(at_l[:, ci, :], bank[out_bank(ci, nsa)][:, 0:T1], at_h[:, ci, :].bitcast(F32), ALU.subtract),
                         at_out)

            def attention(units, v0, nsa, c0):
                for i in range(len(units) + 3):
                    if 1 <= i <= len(units):
                        v = v0 + i - 1
                        ci, kind = units[i - 1]
                        first = kind == "first"
                        n = 4 if nsa and first else 2
                        dve.wait_ge(at_exp, v + 1)
                        if v >= 2:
                            dve.wait_ge(at_probs, v - 1)
                        den, r = st_den[:, v % 2, 0:n], st_r[:, v % 2, 0:n]
                        if nsa:
                            line.put(V.reciprocal(r, den))
                            line.settle()
                            qb = 0 if first else 1
                            g = gate_of[:, qb, ci]
                            if first:
                                line.put(V.tensor_tensor(r.rearrange("p (a b) -> p a b", a=2), r.rearrange("p (a b) -> p a b", a=2),
                                                         g[:, :, 1:3], ALU.mult), at_r)
                            else:
                                line.put(V.tensor_tensor(r, r, g[:, int(kind[-1]), 1:3], ALU.mult), at_r)
                        else:
                            dve.wait_ge(at_sinkexp, v - v0 + 1)
                            line.put(V.tensor_tensor(den, den, st_es[:, v % 2, 0:2], ALU.add))
                            line.settle()
                            line.put(V.reciprocal(r, den), at_r)
                    if 2 <= i < len(units) + 2:
                        v = v0 + i - 2
                        n = 256 if not nsa and units[i - 2][1] == "first" else 512
                        dve.wait_ge(at_turned, v + 1)
                        if v >= 2:
                            dve.wait_ge(at_pv, v - 1)
                        line.put(V.tensor_copy(S_pt[:, v % 2, 0:n], bank[6 + v % 2][:, 0:n]), at_pt)
                    if i < len(units):
                        v = v0 + i
                        ci, kind = units[i]
                        first = kind == "first"
                        n, w = (4 if nsa else 2, 128) if first else (2, 256)
                        dve.wait_ge(at_scores, v + 1)
                        line.put(V.tensor_reduce(st_mx[:, v % 2, 0:n], bank[4 + v % 2][:, 0:n * w].rearrange("p (n w) -> p n w", n=n),
                                                 AX.X, ALU.max))
                        line.settle()
                        if nsa:
                            line.put(V.tensor_scalar(st_neg[:, v % 2, 0:n], st_mx[:, v % 2, 0:n], -SCALE, None, ALU.mult), at_neg)
                        else:
                            ns = nsinks.rearrange("p (c a) -> p c a", a=2)[:, ci, :]
                            line.put(V.scalar_tensor_tensor(out=st_neg[:, v % 2, 0:2], in0=st_mx[:, v % 2, 0:2], scalar=-SCALE,
                                                            in1=ns, op0=ALU.mult, op1=ALU.min), at_neg)
                            line.settle()
                            line.put(V.tensor_tensor(st_es[:, v % 2, 0:2], st_neg[:, v % 2, 0:2], ns, ALU.subtract), at_sink)
                    if nsa and i == 0:
                        cmp_softmax()
                        cmp_norm()
                    if i >= 3 and units[i - 3][1] in ("second", "second1"):
                        attention_low(units[i - 3][0], c0, nsa)

            low(11)
            low(12)
            attention(NSA_UNITS, 0, True, 0)

            def add_chunk(n0, c, bias=None):
                n = n0 + c
                dve.wait_ge(proj_done, n + 1)
                if bias is None:
                    line.put(V.tensor_tensor(xT[:, c, 0:T1], bank[bank_of(n)][:, 0:T1], xT[:, c, 0:T1], ALU.add), proj_taken)
                else:
                    line.put(V.scalar_tensor_tensor(out=xT[:, c, 0:T1], in0=bank[bank_of(n)][:, 0:T1], scalar=vec(bias, c),
                                                    in1=xT[:, c, 0:T1], op0=ALU.add, op1=ALU.add), proj_taken)

            def add_residual(n0, bias, norm, after):
                for c in range(8):
                    add_chunk(n0, c, bias)
                    if c >= 1:
                        stream_low(norm, T1, xT, c - 1)
                    if c < 7:
                        after(c)
                stream_low(norm, T1, xT, 7)
                after(7)

            def bank_of(n):
                for l in range(3):
                    if N_FFN[l] <= n < N_FFN[l] + 52:
                        return down_bank(n - N_FFN[l])
                return n % 4

            add_residual(N_NSA_O, None, 1, lambda c: low(13 + c // 2) if c % 2 else None)
            factor(1, T1)

            def ffn(l, T):
                def tap(name, f):
                    at = vcolc[name][0]
                    if isinstance(f, int):
                        return vecs[:, 1 + l, at + f:at + f + 1]
                    return vecs[:, 1 + l, bass.ds(f + at, 1)]

                n0, m0 = ffn_at[l]

                def step(k, n, b, p, f, slab, m, mb, first):
                    dve.wait_ge(proj_done, n + 1)
                    if not first:
                        dve.wait_ge(c1_ready, k - 1)
                    V.tensor_tensor(f_a[:, p, 2:2 + T], bank[b][:, 0:T], rstd[:, 0:T], ALU.mult).then_inc(proj_taken, 1)
                    dve.wait_ge(proj_done, n + 2)
                    if not first:
                        dve.wait_ge(hid_full, k - 1)
                    V.tensor_tensor(f_u[:, p, 0:T], bank[b + 1][:, 0:T], rstd[:, 0:T], ALU.mult).then_inc(proj_taken, 1)
                    dve.wait_ge(proj_taken, n + 2)
                    dve.wait_ge(c1_ready, k + 1)
                    V.scalar_tensor_tensor(out=f_c2[:, p, 0:T], in0=f_a[:, p, 1:1 + T], scalar=tap("w1", f),
                                           in1=f_c1[:, p, 0:T], op0=ALU.mult, op1=ALU.add).then_inc(conv_mid, 1)
                    dve.wait_ge(conv_mid, k + 1)
                    if not first:
                        dve.wait_ge(act_ready, k - 1)
                    V.scalar_tensor_tensor(out=f_c3[:, p, 0:T], in0=f_a[:, p, 2:2 + T], scalar=tap("w2", f),
                                           in1=f_c2[:, p, 0:T], op0=ALU.mult, op1=ALU.add).then_inc(conv_ready, 1)
                    dve.wait_ge(w_hi, m + 1)
                    V.tensor_tensor(w_l[:, mb, :], raw[:, slab, :], w_h[:, mb, :].bitcast(F32), ALU.subtract).then_inc(w_lo, 1)

                for f in range(2):
                    step(FC * l + f, N_FFN[l] + 2 * f, 2 * f, f, f, (n0 + f) % 2, m0 + f + 2, (m0 + f) % 2, l == 0)
                with dve.Fori(0, (FC - 2) // 2) as i:
                    for j in range(2):
                        step(i * 2 + (FC * l + 2 + j), i * 4 + (N_FFN[l] + 4 + 2 * j), 2 * j, j, i * 2 + (2 + j),
                             (n0 + j) % 2, i * 2 + (m0 + 4 + j), (m0 + j) % 2, False)
                line.skip(proj_taken, 2 * FC)
                line.skip(conv_ready, FC)

            def down(l, put, norm=None):
                m0 = ffn_at[l][1]
                def lows(a, b):
                    for m in range(m0 + FC + a, min(m0 + FC + b, len(split_at))):
                        low(m)

                lows(2, 7)
                for c in range(4):
                    put(c)
                lows(7, 8)
                if norm is not None:
                    for c in range(4):
                        stream_low(norm, T1, xT, c)
                lows(8, 12)
                for c in range(4, 8):
                    put(c)
                    if norm is not None and c > 4:
                        stream_low(norm, T1, xT, c - 1)
                if norm is not None:
                    stream_low(norm, T1, xT, 7)
                lows(12, 14)

            V.memset(f_a[:, :, 0:2], 0.0)
            ffn(0, T1)
            down(0, lambda c: add_chunk(N_FFN[0] + 44, c), 2)
            factor(2, T1)
            projections(N_SWA, SWA, lambda i: low(M_SWA + 2 + i // 2) if i % 2 else None)
            dve.wait_ge(small_loaded, 16 * SMALL_DMAS)
            line.put(V.tensor_scalar(nsinks, sinks, -1.0, None, ALU.mult))
            line.settle()
            attention(SWA_UNITS, V_SWA, False, 8)
            add_residual(N_SWA_O, "bo", 3, lambda c: low(M_SWA + 7 + c // 2) if c % 2 else None)
            factor(3, T1)
            V.memset(f_a[:, :, 0:2], 0.0)
            ffn(1, T1)
            down(1, lambda c: add_chunk(N_FFN[1] + 44, c))
            factor(4, T1)
            for c in range(8):
                line.put(V.scalar_tensor_tensor(out=h2[:, c, META:T2], in0=xT[:, c, 0:T1], scalar=vec("g", 8 * 4 + c),
                                                in1=rstd[:, 0:T1], op0=ALU.mult, op1=ALU.mult), h2_ready)
                if c >= 1:
                    stream_low(5, T2, h2, c - 1)
            stream_low(5, T2, h2, 7)
            factor(5, T2)
            for n in range(53):
                place = n if n < 36 else n - 1
                if n == 36:
                    take(N_IN2 + n, glr[0:16, :], 16, T2)
                elif 12 <= n < 16:
                    dve.wait_ge(proj_done, N_IN2 + n + 1)
                    line.put(V.scalar_tensor_tensor(out=big2[:, place, :], in0=bank[(N_IN2 + n) % 4][:, 0:T2], scalar=GDK ** -0.5,
                                                    in1=rstd[:, :], op0=ALU.mult, op1=ALU.mult), proj_taken)
                else:
                    take(N_IN2 + n, big2[:, place, :], 128, T2)
                if n < 36 and n % 2 or n >= 36 and n % 2 == 0:
                    low(M_IN2 + 2 + (n // 2 if n <= 36 else 19 + (n - 37) // 2))
            def z_low(c):
                dve.wait_ge(z_high, c + 1)
                line.put(V.tensor_tensor(xl[:, c, :], bank[2 + c % 2][:, 0:T2], xh[:, c, :].bitcast(F32), ALU.subtract), z_out)

            Z = [bank[0], bank[1], bank[4], bank[5]]
            for i in range(8):
                dve.wait_ge(z_scores, i + 1)
                if i >= 2:
                    dve.wait_ge(z_ln, i - 1)
                    dve.wait_ge(z_soft, i - 1)
                z = Z[i % 4][:, 0:ZW]
                line.put(V.tensor_scalar(z_r[:, i % 2, :], z, 0.0, SCALE, ALU.max, ALU.mult), z_relu)
                line.settle()
                line.put(V.scalar_tensor_tensor(out=z_a[:, i % 2, :], in0=z_r[:, i % 2, :], scalar=2.0 / SCALE, in1=z,
                                                op0=ALU.mult, op1=ALU.subtract), z_abs)
                if i >= 3 and i % 2:
                    z_low(i // 2 - 1)
            for c in (3,):
                z_low(c)
            for c in range(8):
                n = N_SBO + c
                dve.wait_ge(proj_done, n + 1)
                t = big2[:, 36 + c, :]
                line.put(V.tensor_tensor(t, bank[n % 4][:, 0:T2], t, ALU.mult), proj_taken)
                if c % 4 == 3:
                    low(M_GLO + c // 4)
            dve.wait_ge(g_log, 1)
            gx = g_q[:, 0, :].rearrange("p (n t) -> p n t", n=GN)
            dve.wait_ge(z_pv, 8)
            for n in range(GN):
                line.put(V.tensor_scalar(gx[:, n, :], bank[n][:, 0:T2], vec("bgk", n), None, ALU.add), g_x)
            line.settle()
            line.put(V.tensor_scalar(g_q[:, 1, :], g_q[:, 0, :], -1.0, 0.0, ALU.mult, ALU.max))
            line.settle()
            line.put(V.scalar_tensor_tensor(out=g_d[:, 1, :], in0=g_q[:, 1, :], scalar=2.0, in1=g_q[:, 0, :],
                                            op0=ALU.mult, op1=ALU.add), g_abs)
            dve.wait_ge(g_ln, 1)
            line.settle()
            line.put(V.tensor_tensor(g_q[:, 0, :], g_q[:, 1, :], g_d[:, 1, :], ALU.add))
            dve.wait_ge(prepared, 7)
            line.settle()
            line.put(V.tensor_tensor_scan(cum.rearrange("p n t -> p (n t)"), g_k[:, 0, :], g_q[:, 0, :], 0.0, ALU.mult, ALU.add),
                     g_cum)

            def distance(lv):
                b = 1 << (lv - 1)
                if lv >= 3:
                    dve.wait_ge(g_qk, lv - 2)
                d = g_d[:, lv % 2, :].rearrange("p (n t) -> p n t", n=GN)
                if b <= 8:
                    cf = cum.rearrange("p n t -> p (n t)").rearrange("p (q h b) -> p q h b", h=2, b=b)
                    df = g_d[:, lv % 2, :].rearrange("p (q h b) -> p q h b", h=2, b=b)
                    pairs = [(df, cf)]
                else:
                    pairs = [(d[:, n, 0:256].rearrange("p (q h b) -> p q h b", h=2, b=b),
                              cum[:, n, 0:256].rearrange("p (q h b) -> p q h b", h=2, b=b)) for n in range(GN)]
                for x, (dd, cc) in enumerate(pairs):
                    border = cc[:, :, 0, b - 1:b]
                    border = border.broadcast_to([128, border.shape[1], b])
                    line.put(V.tensor_tensor(dd[:, :, 1, :], cc[:, :, 1, :], border, ALU.subtract))
                    line.put(V.tensor_tensor(dd[:, :, 0, :], border, cc[:, :, 0, :], ALU.subtract),
                             g_dist if x == len(pairs) - 1 else None)

            def select(lv):
                dve.wait_ge(g_att, lv + 1)
                m = L("gla")[:, 128 * lv:128 * lv + 128]
                tiles = [(att[:, ck, :, :], bank[2 * (lv % 2) + ck][:, :].rearrange("p (n t) -> p n t", n=GN), m, 128)
                         for ck in range(2)]
                if lv <= 4:
                    tiles.append((att2[0:16, :, :], bank[4 + lv % 2][0:16, 0:64].rearrange("p (n t) -> p n t", n=GN),
                                  m[0:16, 0:16], 16))
                line.settle()
                for x, (dst, src, mask, w) in enumerate(tiles):
                    sig = g_sel if x == len(tiles) - 1 else None
                    if lv == 0:
                        line.put(V.tensor_tensor(dst, src, each(mask, GN), ALU.mult), sig)
                    else:
                        line.put(V.copy_predicated(dst, each(mask.bitcast(U16), GN), src), sig)

            line.settle()
            dve.wait_ge(late_loaded, 16)
            for lv in range(LEVELS + 1):
                if lv < LEVELS:
                    distance(lv + 1)
                select(lv)
            d = g_d[:, 0, :].rearrange("p (n t) -> p n t", n=GN)
            dve.wait_ge(g_qk, LEVELS)
            for ck in range(2):
                end = cum[:, :, 128 * ck + 127:128 * ck + 128].broadcast_to([128, GN, 128])
                line.put(V.tensor_tensor(d[:, :, 128 * ck:128 * ck + 128], end, cum[:, :, 128 * ck:128 * ck + 128], ALU.subtract),
                         k_dist if ck else None)
            dve.wait_ge(s_taken, 1)
            dve.wait_ge(q_decay, 1)
            dve.wait_ge(s_done, 2)
            for n in range(GN):
                line.put(V.scalar_tensor_tensor(out=s2[:, n, :], in0=s1[:, n, :], scalar=cum[:, n, 255:256],
                                                in1=bank[2 + n // 2][:, 256 * (n % 2):256 * (n % 2) + 256],
                                                op0=ALU.mult, op1=ALU.add), state2)
            for o in range(8):
                dve.wait_ge(go_done, o + 1)
                line.put(V.tensor_copy(g_o[:, o, :], bank[o % 4][:, 0:T2]), go_taken)
            rs = g_d[:, 1, :].rearrange("p (n t) -> p n t", n=GN)

            def go_low(o):
                dve.wait_ge(go_high, o + 1)
                line.put(V.tensor_tensor(xl[:, o, :], g_o[:, o, :], xh[:, o, :].bitcast(F32), ALU.subtract), go_ready)

            for n in range(GN):
                dve.wait_ge(go_root, n + 1)
                line.put(V.reciprocal(rs[:, n, :], rs[:, n, :]))
                line.settle()
                for dv in range(2):
                    o = g_o[:, 2 * n + dv, :]
                    line.put(V.scalar_tensor_tensor(out=o, in0=o, scalar=vec("hn", dv), in1=rs[:, n, :], op0=ALU.mult, op1=ALU.mult))
                    line.settle()
                    line.put(V.tensor_tensor(o, o, big2[:, 28 + 2 * n + dv, :], ALU.mult), go_full)
                    if n or dv:
                        go_low(2 * n + dv - 1)
            go_low(7)
            for c in range(8):
                n = N_GLO + c
                dve.wait_ge(proj_done, n + 1)
                line.put(V.tensor_tensor(g_tmp[:, c % 2, :], bank[n % 4][:, 0:T2], big2[:, 44 + c, :], ALU.mult), proj_taken)
                line.settle()
                line.put(V.tensor_tensor(big2[:, 36 + c, :], big2[:, 36 + c, :], g_tmp[:, c % 2, :], ALU.add), mix_full)
                if c % 2:
                    low(M_GLO + 2 + c // 2)
            for c in range(8):
                dve.wait_ge(mix_high, c + 1)
                line.put(V.tensor_tensor(xl[:, c, :], big2[:, 36 + c, :], xh[:, c, :].bitcast(F32), ALU.subtract), mix_ready)

            def copy_chunk(n0, c):
                n = n0 + c
                dve.wait_ge(proj_done, n + 1)
                line.put(V.tensor_copy(xT[:, c, :], bank[bank_of(n)][:, 0:T2]), proj_taken)

            def add_normed(i, norm=None):
                factor(i, T2)
                for c in range(8):
                    line.put(V.scalar_tensor_tensor(out=g_tmp[:, c % 2, :], in0=xT[:, c, :], scalar=vec("g", 8 * i + c),
                                                    in1=rstd[:, :], op0=ALU.mult, op1=ALU.mult))
                    line.settle()
                    line.put(V.tensor_tensor(h2[:, c, :], h2[:, c, :], g_tmp[:, c % 2, :], ALU.add), h2_ready)
                    if norm is not None and c >= 1:
                        stream_low(norm, T2, h2, c - 1)
                if norm is not None:
                    stream_low(norm, T2, h2, 7)

            for c in range(8):
                copy_chunk(N_WO2, c)
                if c % 2:
                    low(M_GLO + 6 + c // 2)
            add_normed(6, 7)
            V.memset(f_a[:, :, 0:2], 0.0)
            factor(7, T2)
            ffn(2, T2)
            down(2, lambda c: copy_chunk(N_FFN[2] + 44, c))
            add_normed(8)

        @block.gpsimd
        def _(pool):
            line = Line(pool, pool_step)
            G = nc.gpsimd
            G.memset(eps_col[:, :], EPS)
            line.put(G.memset(vec_in, 0.0), prepared)
            pool.wait_ge(early_loaded, 16)
            G.tensor_copy(ident_b[:, :], ident)
            G.tensor_copy(mask_b[:, 0:128], E("before"))
            line.put(G.tensor_copy(mask_b[:, 128:256], E("causal")), prepared)
            line.put(G.memset(c_p, 0.0), prepared)
            line.put(G.memset(big1[:, K_AT:K_AT + 16, :], 0.0), prepared)
            line.put(G.memset(kcT, 0.0), prepared)
            pool.wait_ge(late_loaded, 16)
            G.tensor_copy(tri_all[:, :], late_in[:, 0:256])
            line.put(G.tensor_copy(late_b[:, :], late_in[:, 256:ln]), prepared)

            def gains(i, T, src, ready):
                for c in range(0, 8, 2):
                    pool.wait_ge(*ready(c))
                    line.put(G.tensor_scalar(xh[:, c, 0:T], src[:, c, 0:T], vec("g", 8 * i + c), None, ALU.mult), xh_even)

            def taken(n0):
                return lambda c: (proj_taken, n0 + c + 1)

            gains(0, T1, xT, lambda c: (turn_taken, 4 + c // 2))
            rope = {"k": 0}

            def ropes(table, ready):
                for i, (place, r) in enumerate(table):
                    if not r and place != "k":
                        continue
                    k = rope["k"]
                    pool.wait_ge(*ready(i))
                    line.put(G.tensor_tensor(tcos[:, k % 2, :], xs[:, k % 2, :], E("cos"), ALU.mult), cos_done)
                    pool.wait_ge(sin_done, k + 1)
                    line.settle()
                    if place != "k":
                        line.put(G.tensor_tensor(big1[:, place, :], tcos[:, k % 2, :], tsin[:, k % 2, :], ALU.add), roped)
                    else:
                        for g in range(2):
                            for a in range(2):
                                half = slice(64 * g, 64 * g + 64)
                                line.put(G.tensor_tensor(big1[64 * a:64 * a + 64, K_AT + 2 * (r + g) + a, :],
                                                         tcos[half, k % 2, :], tsin[half, k % 2, :], ALU.add),
                                         roped if g and a else None)
                                line.settle()
                    rope["k"] += 1

            ropes(NSA, lambda i: (proj_taken, i + 1))

            def attention(units, v0, nsa):
                for i, (ci, kind) in enumerate(units):
                    v = v0 + i
                    n, w = (4 if nsa else 2, 128) if kind == "first" else (2, 256)
                    pool.wait_ge(at_r, v + 1)
                    p = S_p[:, v % 2, 0:n * w].rearrange("p (n w) -> p n w", n=n)
                    r = st_r[:, v % 2, 0:n].unsqueeze(2).broadcast_to([128, n, w])
                    line.put(G.tensor_tensor(p, p, r, ALU.mult), at_probs)

            attention(NSA_UNITS, 0, True)
            gains(1, T1, xT, taken(N_NSA_O))

            def ffn(l, T):
                hh, hl = (hidden(v, T).rearrange("p f t -> p (f t)") for v in (hid_h, hid_l))

                def step(k, n, p, at):
                    pool.wait_ge(proj_taken, n + 2)
                    pool.wait_ge(act_ready, k + 1)
                    G.tensor_tensor(f_h[:, p, 0:T], f_s[:, p, 0:T], f_u[:, p, 0:T], ALU.mult).then_inc(hid_full, 1)
                    pool.wait_ge(hid_full, k + 1)
                    G.tensor_copy(hh[:, at], f_h[:, p, 0:T]).then_inc(hid_high, 1)
                    pool.wait_ge(hid_high, k + 1)
                    G.tensor_tensor(hl[:, at], f_h[:, p, 0:T], hh[:, at].bitcast(F32), ALU.subtract).then_inc(hidden_ready, 1)

                for f in range(2):
                    step(FC * l + f, N_FFN[l] + 2 * f, f, slice(f * T, f * T + T))
                with pool.Fori(0, (FC - 2) // 2) as i:
                    for j in range(2):
                        step(i * 2 + (FC * l + 2 + j), i * 4 + (N_FFN[l] + 4 + 2 * j), j, bass.ds(i * (2 * T) + (2 + j) * T, T))
                line.skip(hidden_ready, FC)

            ffn(0, T1)
            gains(2, T1, xT, taken(N_FFN[0] + 44))
            pool.wait_ge(proj_done, N_FFN[0] + 52)
            line.put(G.memset(big1[:, K_AT:K_AT + 4, :], 0.0))
            line.settle()
            ropes(SWA, lambda i: (biased, i + 1))
            attention(SWA_UNITS, V_SWA, False)
            gains(3, T1, xT, taken(N_SWA_O))
            ffn(1, T1)
            gains(5, T2, h2, lambda c: (h2_ready, c + 1))
            pool.wait_ge(proj_taken, N_IN2 + 8)
            G.dma_start(up_sb[0:16, :], A["w_gk_up_2"][0]).then_inc(up_loaded, 16)
            line.put(G.memset(kpad, 0.0))
            line.settle()
            line.put(G.tensor_copy(kpad[:, :, 0:16], big2[:, 4:8, 256:T2]), kpad_ready)
            for i in range(8):
                pool.wait_ge(z_ln, i + 1)
                pool.wait_ge(z_relu, i + 1)
                if i >= 2:
                    pool.wait_ge(z_tri, i - 1)
                line.put(G.tensor_tensor(z_u[:, i % 2, :], z_l[:, i % 2, :], z_r[:, i % 2, :], ALU.add))
                line.settle()
                line.put(G.tensor_tensor(z_u[:, i % 2, :], z_u[:, i % 2, :], L("sbvalid"), ALU.mult), z_soft)
            pool.wait_ge(z_pv, 8)
            line.put(G.memset(g_k[:, 0, :], 1.0))
            line.settle()
            line.put(G.memset(g_k[:, 0, :].rearrange("p (n t) -> p n t", n=GN)[:, :, 0:T2:128], 0.0), prepared)
            pool.wait_ge(g_cum, 1)
            for v in (g_q, g_k):
                line.put(G.memset(v, 0.0))
            line.settle()
            for lv in range(1, LEVELS + 1):
                b = 1 << (lv - 1)
                pool.wait_ge(g_decay, lv)
                if lv >= 2:
                    pool.wait_ge(g_att, lv - 1)

                def split(v, n=None):
                    v = v if n is None else v[:, T2 * n:T2 * n + 256]
                    return v.rearrange("p (q h b) -> p q h b", h=2, b=b)

                d = g_d[:, lv % 2, :]
                q, k = big2[:, 12:16, :].rearrange("p n t -> p (n t)"), big2[:, 16:20, :].rearrange("p n t -> p (n t)")
                for n in ([None] if b <= 8 else range(GN)):
                    line.put(G.tensor_tensor(split(g_q[:, lv % 2, :], n)[:, :, 1, :], split(q, n)[:, :, 1, :],
                                             split(d, n)[:, :, 1, :], ALU.mult))
                    line.put(G.tensor_tensor(split(g_k[:, lv % 2, :], n)[:, :, 0, :], split(k, n)[:, :, 0, :],
                                             split(d, n)[:, :, 0, :], ALU.mult), g_qk if n in (None, GN - 1) else None)

            def by_head(v):
                return v.rearrange("p (n t) -> p n t", n=GN)

            pool.wait_ge(k_decay, 1)
            pool.wait_ge(g_att, LEVELS)
            line.put(G.tensor_tensor(by_head(g_k[:, 0, :])[:, :, 0:256], big2[:, 16:20, 0:256], by_head(g_d[:, 0, :])[:, :, 0:256],
                                     ALU.mult), k_dec)
            pool.wait_ge(q_decay, 1)
            line.put(G.tensor_tensor(by_head(g_q[:, 0, :])[:, :, 128:T2], big2[:, 12:16, 128:T2], cum[:, :, 128:T2], ALU.mult),
                     q_dec)
            gains(7, T2, h2, lambda c: (h2_ready, 8 + c + 1))
            ffn(2, T2)
    return nc


_INS = ["x", "nsa_w_in", "nsa_cmp_pe", "nsa_cmp_w1", "nsa_cmp_w2", "nsa_gate_b", "nsa_w_o", "swa_w_qkv", "swa_b_qkv",
        "swa_sinks", "swa_w_o", "swa_b_o", "ffn_w_gu", "ffn_conv_w", "ffn_conv_b", "ffn_w_down", "norm_mix", "norm_ffn",
        "norm_final", "meta_tokens_2", "norm_mix_pre_2", "w_in_2", "w_gk_up_2", "b_gk_2", "gla_head_norm_2", "w_sb_out_2",
        "w_gla_out_2", "w_o_2", "norm_mix_post_2", "norm_ffn_pre_2", "w_ffn_up_2", "w_ffn_gate_2", "conv_w_2", "conv_b_2",
        "w_ffn_down_2", "norm_ffn_post_2"]


def kernel(**inputs):
    import numpy as _np
    import concourse.bacc as _bacc
    from concourse import mybir as _mybir
    from concourse.bass_utils import run_bass_kernel_spmd as _run

    nc = _bacc.Bacc("TRN2", target_bir_lowering=False, num_devices=1)
    arrays, aps = {}, {}
    e, l = constants()
    for name, a in [(n, inputs[n]) for n in _INS] + [("early_c", e), ("late_c", l)]:
        a = _np.ascontiguousarray(a)
        arrays[f"in_{name}"] = a
        aps[name] = nc.dram_tensor(f"in_{name}", a.shape, _mybir.dt.from_np(a.dtype), kind="ExternalInput").ap()
    out = nc.dram_tensor("out_0", (1, SEQ, D), _mybir.dt.float32, kind="ExternalOutput").ap()
    build(nc, aps, out)
    r = _run(nc, [arrays], core_ids=[0])
    return r.results[0]["out_0"]
```

```python
import concourse.bass as bass
from concourse import mybir
from contextlib import ExitStack
import numpy as np

F32 = mybir.dt.float32
F32R = mybir.dt.float32r
BF16 = mybir.dt.bfloat16
U16 = mybir.dt.uint16
ALU = mybir.AluOpType
ACT = mybir.ActivationFunctionType
AX = mybir.AxisListType

D, SEQ, META = 1024, 256, 16
SLAB = 2048
T1, T2 = SEQ, SEQ + META
KC = D // 128
DFF = 2816
FC = DFF // 128
HD = 64
EPS = 1e-6
SCALE = HD ** -0.5
NEG = -1e30
NCMP, CSTR, CLEN = 15, 16, 32
GN, GDK = 4, 128
LEVELS = 7
ZW = 272 + 144 + 16

EARLY = {"ident": 128, "ones": 128, "rot": 128, "cos": T1, "sin": T1, "causal": 128, "before": 128, "cmpneg": 2 * NCMP}
LATE = {"tri": 128, "all": 128, "sbvalid": ZW, "sbneg": ZW, "gla": (LEVELS + 1) * 128}


def columns(parts):
    at, out = 0, {}
    for name, width in parts.items():
        out[name] = (at, at + width)
        at += width
    return out, at


def constants():
    p = np.arange(128)
    q = np.arange(128)
    early, n = columns(EARLY)
    e = np.zeros((128, n), np.float32)

    def put(a, cols, name, v):
        a[:, cols[name][0]:cols[name][1]] = v

    put(e, early, "ident", np.eye(128))
    put(e, early, "ones", 1.0 / D)
    rot = np.zeros((128, 128), np.float32)
    for m in range(128):
        if m % 64 < 32:
            rot[m + 32, m] = -1.0
        else:
            rot[m - 32, m] = 1.0
    put(e, early, "rot", rot)
    inv = (np.float32(10000.0) ** (-np.arange(0, HD, 2, dtype=np.float32) / np.float32(HD))).astype(np.float32)
    ang = inv[p % 32][:, None] * np.arange(T1, dtype=np.float32)[None, :]
    put(e, early, "cos", np.cos(ang.astype(np.float32)))
    put(e, early, "sin", np.sin(ang.astype(np.float32)))
    put(e, early, "causal", np.where(q[None, :] <= p[:, None], 0.0, NEG))
    put(e, early, "before", np.where(q[None, :] > p[:, None], 0.0, NEG))
    c = np.arange(NCMP)
    cm = [np.where(c[None, :] * CSTR + CLEN - 1 <= (p + 128 * b)[:, None], 0.0, NEG) for b in range(2)]
    put(e, early, "cmpneg", np.concatenate(cm, 1))

    late, n = columns(LATE)
    l = np.zeros((128, n), np.float32)
    valid = []
    for b in range(3):
        t = np.arange(128 * b, T2)
        s = p + 128 * b
        valid.append((s[:, None] < t[None, :]) & (s[:, None] < T2))
    valid = np.concatenate(valid, 1)
    put(l, late, "sbvalid", valid)
    put(l, late, "sbneg", np.where(valid, 0.0, NEG))
    put(l, late, "tri", np.where(p[:, None] >= q[None, :], -1.0 / SCALE, 0.0))
    put(l, late, "all", -1.0 / SCALE)
    g = [p[:, None] == q[None, :]]
    for i in range(LEVELS):
        b = 1 << i
        g.append((p[:, None] // (2 * b) == q[None, :] // (2 * b)) & (p[:, None] % (2 * b) < b) & (q[None, :] % (2 * b) >= b))
    put(l, late, "gla", np.concatenate(g, 1))
    return e, l


VEC0 = {"g": 9 * KC, "bo": KC, "hn": 2, "bgk": 4, "bqkv": 10, "gb": 1}
VEC_CONV = {"w0": FC, "w1": FC, "w2": FC, "b": FC}


def vector_loads(vec_in, pe_in, meta_in, A):
    at, _ = columns(VEC0)
    loads = []

    def rows(table, r, vector):
        n = vector.shape[0] // 128
        loads.append((vec_in[r:r + n, table, :], vector.rearrange("(c p) -> c p", p=128)))

    gains = [A["norm_mix"][0], A["norm_ffn"][0], A["norm_mix"][1], A["norm_ffn"][1], A["norm_final"],
             A["norm_mix_pre_2"][0], A["norm_mix_post_2"][0], A["norm_ffn_pre_2"][0], A["norm_ffn_post_2"][0]]
    for i, g in enumerate(gains):
        rows(0, at["g"][0] + KC * i, g)
    rows(0, at["bo"][0], A["swa_b_o"][0])
    rows(0, at["hn"][0], A["gla_head_norm_2"][0])
    rows(0, at["bgk"][0], A["b_gk_2"][0])
    rows(0, at["bqkv"][0], A["swa_b_qkv"][0])
    r = at["gb"][0]
    loads.append((vec_in[r:r + 1, 0, 0:48], A["nsa_gate_b"]))
    for table, w, b in ((1, A["ffn_conv_w"][0], A["ffn_conv_b"][0]), (2, A["ffn_conv_w"][1], A["ffn_conv_b"][1]),
                        (3, A["conv_w_2"][0], A["conv_b_2"][0])):
        loads.append((vec_in[0:3 * FC, table, :], w.rearrange("k (c p) -> (k c) p", p=128)))
        rows(table, FC * 3, b)
    for kv in range(2):
        for twice in range(2):
            loads.append((pe_in[:, kv, twice, :], A["nsa_cmp_pe"][0][kv]))
    loads.append((meta_in, A["meta_tokens_2"]))
    return loads


def build(nc, A, out):
    ctx = ExitStack()
    with ctx:
        def sb(name, shape, dt=F32):
            return ctx.enter_context(nc.sbuf_tensor(name, shape, dt))

        def sem(name):
            return ctx.enter_context(nc.semaphore(name))

        ecol, en = columns(EARLY)
        lcol, ln = columns(LATE)
        early = sb("early", [128, en])
        tri_all = sb("tri_all", [128, 256])
        late_b = sb("late_b", [128, ln - 256], BF16)

        def E(name):
            return early[:, ecol[name][0]:ecol[name][1]]

        def L(name):
            a, b = lcol[name]
            return tri_all[:, a:b] if b <= 256 else late_b[:, a - 256:b - 256]

        ident, ones = E("ident"), E("ones")
        ident_b = sb("ident_b", [128, 128], BF16)
        mask_b = sb("mask_b", [128, 256], BF16)
        vcol0, _ = columns(VEC0)
        vcolc, vcn = columns(VEC_CONV)
        vecs = sb("vecs", [128, 4, 128])

        def vec(name, i):
            at = vcol0[name][0] + i
            return vecs[:, 0, at:at + 1]

        raw = sb("raw", [128, 2, SLAB])
        w_h, w_l = sb("w_h", [128, 2, SLAB], F32R), sb("w_l", [128, 2, SLAB], F32R)
        x_at = nc.sbuf_base
        xT = sb("xT", [128, KC, T2])
        h2 = sb("h2", [128, KC, T2])
        xh, xl = sb("xh", [128, KC, T2], F32R), sb("xl", [128, KC, T2], F32R)
        sq = sb("sq", [128, 4, T2])
        rstd = sb("rstd", [128, T2])
        root = sb("root", [128, T2])
        eps_col = sb("eps_col", [128, 8])
        scrap = sb("scrap", [128, 8])[:, 0:1]
        big_at = nc.sbuf_base
        big = sb("big", [128, 52 * T2])
        hid_h = nc.alloc_sbuf_tensor_at("hid_h", [128, FC, T2], F32R, offset=big_at)
        hid_l = nc.alloc_sbuf_tensor_at("hid_l", [128, FC, T2], F32R, offset=big_at + 4 * FC * T2)
        AT_PLACE = 33
        at_h = nc.alloc_sbuf_tensor_at("at_h", [128, KC, T1], F32R, offset=big_at + 4 * AT_PLACE * T1)
        at_l = nc.alloc_sbuf_tensor_at("at_l", [128, KC, T1], F32R, offset=big_at + 4 * (AT_PLACE + KC) * T1)
        z_h = nc.alloc_sbuf_tensor_at("z_h", [128, 4, T2], F32R, offset=x_at)
        z_lo = nc.alloc_sbuf_tensor_at("z_lo", [128, 4, T2], F32R, offset=x_at + 4 * 4 * T2)
        go_h, go_l = hid_h[:, 0:8, :], hid_h[:, 8:16, :]
        NW = 11500
        work = sb("work", [128, NW])

        def chunks(T):
            return big[:, 0:(52 * T2 // T) * T].rearrange("p (c t) -> p c t", t=T)

        big1, big2 = chunks(T1), chunks(T2)

        class Carver:
            def __init__(self):
                self.at = 0

            def __call__(self, *shape):
                n = int(np.prod(shape))
                v = work[:, self.at:self.at + n]
                self.at += n
                assert self.at <= NW, self.at
                if len(shape) == 2:
                    return v.rearrange("p (a b) -> p a b", b=shape[1])
                if len(shape) == 3:
                    return v.rearrange("p (a b c) -> p a b c", b=shape[1], c=shape[2])
                return v

        bank = [ctx.enter_context(nc.psum_tensor(f"bank{i}", [128, 512], F32)) for i in range(8)]

        x_in = big[:, 0:2048].rearrange("p (b n) -> p b n", b=2)
        vec_in = big[:, 2048:2560].rearrange("p (v n) -> p v n", v=4)
        pe_in = big[0:32, 2560:2816].rearrange("p (k u d) -> p k u d", k=2, u=2)
        meta_in = big[0:META, 2816:3840]
        late_in = big[:, 52 * T2 - ln:52 * T2]
        cmp_w = big[:, AT_PLACE * T1:AT_PLACE * T1 + 2 * SLAB].rearrange("p (s k n) -> p s k n", s=2, n=256)

        gain_load, *vec_loads = vector_loads(vec_in, pe_in, meta_in, A)
        SMALL_DMAS = 4

        cv = Carver()
        xs, tcos, tsin = cv(2, T1), cv(2, T1), cv(2, T1)
        vtok = cv(2, 2, 256)
        S_p, S_pt = cv(3, 512), cv(2, 512)
        st_mx, st_neg, st_den, st_r, st_es = (cv(3, 4) for _ in range(5))
        sinks, nsinks = cv(16), cv(16)
        pe_dup = cv(2, CLEN)
        w2k_sb, w2v_sb = cv(2, 128), cv(2, HD)
        gates = cv(2, 48)
        egate = cv(2, 48)
        blkT = cv(2, 16, 60)
        hidT = cv(2, 2, 60)
        kcT = cv(2, 60)
        vc_rep = cv(256)
        c_s, c_e = cv(32, NCMP), cv(32, NCMP)
        c_mx, c_den = cv(32), cv(32)
        c_p = cv(32, 32)
        c_pt = cv(2, 4, 128)
        cv = Carver()
        f_a, f_u, f_c1, f_c2, f_c3, f_s, f_h = cv(2, T2 + 2), *(cv(2, T2) for _ in range(6))
        cv = Carver()
        glr = cv(T2)
        up_sb = cv(512)
        stage = cv.at
        sv_tok = cv(3, 512)
        kpad = cv(4, 128)
        z_a, z_r, z_l, z_u, z_w = cv(2, ZW), cv(2, ZW), cv(2, ZW), cv(2, ZW), cv(2, ZW)
        cv.at = stage
        gv_tok = big[:, 0:3072].rearrange("p (b n) -> p b n", b=3)
        g_o = big2[:, 20:28, :]
        cum = cv(GN, T2)
        g_d, g_q, g_k = cv(2, GN * T2), cv(2, GN * T2), cv(2, GN * T2)
        att = cv(2, GN, 128)
        att2 = cv(GN, 16)
        g_tmp = cv(4, T2)
        kdT = g_q[:, 1, 0:1024].rearrange("p (c k) -> p c k", c=2)
        s1 = g_k[:, 1, 0:1024].rearrange("p (n v) -> p n v", n=GN)
        s2 = g_d[:, 0, 0:1024].rearrange("p (n v) -> p n v", n=GN)

        early_loaded, x_loaded, gain_loaded, vec_loaded, small_loaded, late_loaded = map(sem, (
            "early_loaded", "x_loaded", "gain_loaded", "vec_loaded", "small_loaded", "late_loaded"))
        raw_loaded = [sem("raw_loaded0"), sem("raw_loaded1")]
        w_hi, w_lo = sem("w_hi"), sem("w_lo")
        out_stored = sem("out_stored")
        proj_done, proj_taken, down_part = map(sem, ("proj_done", "proj_taken", "down_part"))
        xh_even, xh_odd, xl_ready, sq_ready, ss_step, root_ready = map(sem, ("xh_even", "xh_odd", "xl_ready", "sq_ready", "ss_step", "root_ready"))
        turn_done, turn_taken = sem("turn_done"), sem("turn_taken")
        prepared = sem("prepared")
        biased = sem("biased")
        perm_done, cos_done, sin_done, roped = map(sem, ("perm_done", "cos_done", "sin_done", "roped"))
        vt_done, vt_taken = sem("vt_done"), sem("vt_taken")
        gate_moved, gate_exp, gates_ready = map(sem, ("gate_moved", "gate_exp", "gates_ready"))
        cmp_loaded = [sem("cmp_loaded0"), sem("cmp_loaded1")]
        blk_ready, cmp_hid, cmp_act, cmp_kv, cmp_kv_taken = map(sem, (
            "blk_ready", "cmp_hid", "cmp_act", "cmp_kv", "cmp_kv_taken"))
        cmp_scores, cmp_centered, cmp_exp, cmp_probs, cmp_turned, cmp_pt = map(sem, (
            "cmp_scores", "cmp_centered", "cmp_exp", "cmp_probs", "cmp_turned", "cmp_pt"))
        at_scores, at_neg, at_exp, at_r, at_probs, at_turned, at_pt, at_pv, at_out = map(sem, (
            "at_scores", "at_neg", "at_exp", "at_r", "at_probs", "at_turned", "at_pt", "at_pv", "at_out"))
        at_sink, at_sinkexp, at_high = sem("at_sink"), sem("at_sinkexp"), sem("at_high")
        c1_ready, conv_mid, conv_ready, act_ready, hid_full, hid_high, hidden_ready = map(sem, (
            "c1_ready", "conv_mid", "conv_ready", "act_ready", "hid_full", "hid_high", "hidden_ready"))
        h2_ready, h2_even, h2_odd, normed = map(sem, ("h2_ready", "h2_even", "h2_odd", "normed"))
        kpad_ready, up_loaded, state2 = sem("kpad_ready"), sem("up_loaded"), sem("state2")
        z_scores, z_abs, z_relu, z_ln, z_soft, z_tri, z_weights, z_pv, z_out = map(sem, (
            "z_scores", "z_abs", "z_relu", "z_ln", "z_soft", "z_tri", "z_weights", "z_pv", "z_out"))
        g_log, g_x, g_abs, g_ln, g_cum = map(sem, ("g_log", "g_x", "g_abs", "g_ln", "g_cum"))
        g_dist, g_decay, g_qk, g_att, g_sel = map(sem, ("g_dist", "g_decay", "g_qk", "g_att", "g_sel"))
        k_dist, k_decay, k_dec, k_turned, k_tok, q_decay, q_dec = map(sem, (
            "k_dist", "k_decay", "k_dec", "k_turned", "k_tok", "q_decay", "q_dec"))
        s_done, s_taken, go_done, go_taken, go_sq, go_ss, go_root, go_ready = map(sem, (
            "s_done", "s_taken", "go_done", "go_taken", "go_sq", "go_ss", "go_root", "go_ready"))
        gate_ready, go_normed, mix_full, mix_high, mix_ready, z_high, go_full, go_high = map(sem, (
            "gate_ready", "go_normed", "mix_full", "mix_high", "mix_ready", "z_high", "go_full", "go_high"))
        y_turned, y_taken = sem("y_turned"), sem("y_taken")

        def rows(w):
            return w.rearrange("(k p) n -> p k n", p=128)

        def view(buf, s, k, n):
            return buf[:, s, 0:k * n].rearrange("p (k n) -> p k n", n=n)

        slabs, sizes, release, loaded, split_at, used = [], [], [], [], [], []
        per_slot = [0, 0]
        tally = {"chunk": 0, "part": 0, "split": 0}

        def slab(k, n, parts, chunks_after=0):
            s = len(slabs) % 2
            slabs.append([(dst(view(raw, s, k, n)), src) for dst, src in parts])
            sizes.append((k, n))
            per_slot[s] += 16 * len(parts)
            loaded.append(per_slot[s])
            tally["split"] += 1
            split_at.append(len(slabs) - 1)
            release.append((w_lo, tally["split"]))
            tally["chunk"] += chunks_after
            if chunks_after:
                used.append((proj_done, tally["chunk"]))
            else:
                tally["part"] += 1
                used.append((down_part, tally["part"]))

        def plain(w, c0, c1, k=KC):
            slab(k, c1 - c0, [(lambda v: v, rows(w)[:, :, c0:c1])], max(1, (c1 - c0) // 128))

        DOWN_PARTS = [(k, min(k + 4, FC)) for k in range(0, FC, 4)]

        def updown(wg, wu, wd):
            at = len(slabs), len(split_at)
            for f in range(FC):
                cols = slice(128 * f, 128 * f + 128)
                slab(KC, 256, [(lambda v: v[:, :, 0:128], rows(wg)[:, :, cols]),
                               (lambda v: v[:, :, 128:256], rows(wu)[:, :, cols])], 2)
            for g in range(2):
                for k0, k1 in DOWN_PARTS:
                    h = (k1 - k0) // 2
                    src = rows(wd)[:, k0:k1, g * 512:(g + 1) * 512]
                    slab(k1 - k0, 512, [(lambda v, h=h: v[:, 0:h, :], src[:, 0:h, :]), (lambda v, h=h: v[:, h:2 * h, :], src[:, h:, :])],
                         4 if k1 == FC else 0)
            return at

        w_in = A["nsa_w_in"][0]
        for c0 in range(1024, 2560, 256):
            plain(w_in, c0, c0 + 256)
        plain(w_in, 2560, 2608)
        for i in range(4):
            plain(w_in, 256 * i, 256 * i + 256)
        for c0 in range(0, 1024, 256):
            plain(A["nsa_w_o"][0], c0, c0 + 256)
        gu = A["ffn_w_gu"]
        ffn_at = [updown(gu[0][:, 0:DFF], gu[0][:, DFF:2 * DFF], A["ffn_w_down"][0])]
        M_SWA = len(split_at)
        w_qkv = A["swa_w_qkv"][0]
        for c0 in (1024, 0, 256, 512, 768):
            plain(w_qkv, c0, c0 + 256)
        for c0 in range(0, 1024, 256):
            plain(A["swa_w_o"][0], c0, c0 + 256)
        ffn_at.append(updown(gu[1][:, 0:DFF], gu[1][:, DFF:2 * DFF], A["ffn_w_down"][1]))
        M_IN2 = len(split_at)
        w2_in = A["w_in_2"][0]
        for c0 in range(0, 3584, 256):
            plain(w2_in, c0, c0 + 256)
        plain(w2_in, 4608, 4624)
        for c0 in range(3584, 4608, 256):
            plain(w2_in, c0, c0 + 256)
        for c0 in range(4624, 6672, 256):
            plain(w2_in, c0, c0 + 256)
        M_SBO = len(split_at)
        for c0 in (0, 512):
            plain(A["w_sb_out_2"][0], c0, c0 + 512, k=4)
        M_GLO = len(split_at)
        for w in (A["w_gla_out_2"][0], A["w_o_2"][0]):
            for c0 in range(0, 1024, 256):
                plain(w, c0, c0 + 256)
        ffn_at.append(updown(A["w_ffn_up_2"][0], A["w_ffn_gate_2"][0], A["w_ffn_down_2"][0]))
        ups = [(gu[0][:, 0:DFF], gu[0][:, DFF:2 * DFF]), (gu[1][:, 0:DFF], gu[1][:, DFF:2 * DFF]),
               (A["w_ffn_up_2"][0], A["w_ffn_gate_2"][0])]
        def hidden(v, T):
            return v[:, :, :].rearrange("p f t -> p (f t)")[:, 0:FC * T].rearrange("p (f t) -> p f t", t=T)


        N_NSA = 0
        N_NSA_O = 21
        N_FFN = [29, 29 + 52 + 10 + 8, 0]
        N_SWA = N_FFN[0] + 52
        N_SWA_O = N_SWA + 10
        N_IN2 = N_FFN[1] + 52
        N_SBO = N_IN2 + 36 + 1 + 16
        N_GLO = N_SBO + 8
        N_WO2 = N_GLO + 8
        N_FFN[2] = N_WO2 + 8

        class Line:
            def __init__(self, eng, own):
                self.eng, self.own, self.count, self.last = eng, own, {}, None

            def put(self, ins, signal=None):
                s = self.own if signal is None else signal
                self.count[id(s)] = self.count.get(id(s), 0) + 1
                ins.then_inc(s, 1)
                self.last = (s, self.count[id(s)])

            def skip(self, signal, n):
                self.count[id(signal)] = self.count.get(id(signal), 0) + n
                self.last = (signal, self.count[id(signal)])

            def settle(self):
                self.eng.wait_ge(*self.last)

        act_step, dve_step, pool_step = sem("act_step"), sem("dve_step"), sem("pool_step")

        def each(ap, n, axis=1):
            v = ap.unsqueeze(axis)
            return v.broadcast_to([*v.shape[:axis], n, *v.shape[axis + 1:]])

        NSA = [(8, 1), (9, 1), (10, 0), (11, 0), ("k", 0), ("k", 2), (12, 0), (13, 0), ("k", 4), ("k", 6), (14, 0), (15, 0),
               (16, 0)] + [(i, 1) for i in range(8)]
        SWA = [("k", 0), (9, 0)] + [(i, 1) for i in range(8)]
        K_AT = 17

        GO_NORM = (6, 7, 2, 3)

        def is_roped(entry):
            return entry[0] == "k" or entry[1] == 1

        STREAMS = {0: 0, 1: 1, 2: 2, 3: 3, 5: 4, 7: 5}
        NSA_ROPED, SWA_ROPED = 14, 9
        NSA_UNITS = [(ci, kind) for ci in range(8) for kind in ("first", "second0", "second1")]
        SWA_UNITS = [(ci, kind) for ci in range(8) for kind in ("first", "second")]
        V_SWA = len(NSA_UNITS)

        def out_bank(ci, nsa):
            return 2 + ci % 2 if nsa else ci % 2

        def bank_of(n):
            for l in range(3):
                if N_FFN[l] <= n < N_FFN[l] + 52:
                    return down_bank(n - N_FFN[l])
            return n % 2 if N_IN2 + 12 <= n < N_WO2 else n % 4

        def bank_free(n):
            last = [x for x in range(max(0, n - 8), n) if bank_of(x) == bank_of(n)]
            return last[-1] + 1 if last else 0

        def place2(c):
            return c if c < 28 else c - 1

        PAIR = {c: c // 2 for c in range(28)} | {28: 14} | {c: 15 + (c - 29) // 2 for c in range(29, 53)}

        def down_bank(c):
            return c % 4 if c < 48 or c == 51 else c - 44

        block = ctx.enter_context(nc.Block())

        @block.sync
        def _(sp):
            def issue(n):
                if n >= 2:
                    sp.wait_ge(*release[n - 2])
                for dst, src in slabs[n]:
                    sp.dma_start(dst, src).then_inc(raw_loaded[n % 2], 16)

            def issue_ffn(l):
                n0, m0 = ffn_at[l]
                first, second = ups[l]
                issue(n0)
                issue(n0 + 1)
                with sp.Fori(0, (FC - 2) // 2) as i:
                    for j in range(2):
                        sp.wait_ge(w_lo, i * 2 + (m0 + j + 1))
                        s = (n0 + j) % 2
                        for half, w in enumerate((first, second)):
                            sp.dma_start(view(raw, s, KC, 256)[:, :, 128 * half:128 * half + 128],
                                         rows(w)[:, :, bass.ds(i * 256 + 128 * (2 + j), 128)]).then_inc(raw_loaded[s], 16)
                for n in range(n0 + FC, n0 + FC + 12):
                    issue(n)

            for tb in range(2):
                sp.dma_start(x_in[:, tb, :], A["x"][0][128 * tb:128 * tb + 128, :]).then_inc(x_loaded, 16)
            issue(0)
            issue(1)
            sp.wait_ge(prepared, 1)
            for dst, src in vec_loads:
                sp.dma_start(dst, src).then_inc(vec_loaded, 16)
            n = 2
            for l in range(3):
                while n < ffn_at[l][0]:
                    issue(n)
                    n += 1
                issue_ffn(l)
                n = ffn_at[l][0] + FC + 12
            assert n == len(slabs)
            o_sb = big[:, 0:2048].rearrange("p (b n) -> p b n", b=2)
            for tb in range(2):
                sp.wait_ge(y_taken, 3 + tb)
                sp.dma_start(out[0][128 * tb:128 * tb + 128, :], o_sb[:, tb, :]).then_inc(out_stored, 16)
            sp.wait_ge(out_stored, 32)

        @block.tensor
        def _(pe):
            mm = nc.tensor.matmul
            line = {"n": 0}

            def split(m):
                k, n = sizes[split_at[m]]
                pe.wait_ge(w_lo, m + 1)
                return view(w_h, m % 2, k, n), view(w_l, m % 2, k, n)

            def product(dst, parts, k, cols, high, low, first, last):
                wh, wl = parts[0][:, k, cols], parts[1][:, k, cols]
                mm(dst, wh, high, start=first, stop=False)
                mm(dst, wh, low, start=False, stop=False)
                return mm(dst, wl, high, start=False, stop=last)

            def chunk(parts, c, K, M, T, ready=None, source=(xh, xl)):
                n = line["n"]
                if bank_free(n):
                    pe.wait_ge(proj_taken, bank_free(n))
                for k in range(K):
                    if ready is not None:
                        pe.wait_ge(ready[0], ready[1] + k + 1)
                    last = product(bank[bank_of(n)][0:M, 0:T], parts, k, slice(128 * c, 128 * c + M), source[0][:, k, 0:T],
                                   source[1][:, k, 0:T], k == 0, k == K - 1)
                last.then_inc(proj_done, 1)
                line["n"] += 1

            def turn(ins, signal):
                for dst, src in ins:
                    k = src.shape[0]
                    last = nc.tensor.transpose(dst, src, ident[0:k, 0:k])
                last.then_inc(signal, 1)

            def sum_squares(i, T, c0, c1):
                for c in range(c0, c1):
                    pe.wait_ge(sq_ready, 8 * i + c + 1)
                    mm(bank[7][:, 0:T], ones, sq[:, c % 4, 0:T], start=c == 0, stop=c == 7).then_inc(ss_step, 1)

            pe.wait_ge(early_loaded, 16)
            pe.wait_ge(x_loaded, 32)
            for b in range(4):
                turn([(bank[b][:, 256 * c + 128 * tb:256 * c + 128 * tb + 128],
                          x_in[:, tb, 128 * (2 * b + c):128 * (2 * b + c) + 128]) for c in range(2) for tb in range(2)],
                     turn_done)
            pe.wait_ge(gain_loaded, 16)
            turn([(bank[4][:, 0:KC], vec_in[0:KC, 0, :])], turn_done)

            def turn_small():
                pe.wait_ge(vec_loaded, 16 * len(vec_loads))
                turn([(bank[5][:, 128 * v:128 * v + 128], vec_in[:, v, :]) for v in range(4)], turn_done)
                turn([(bank[6][:, 32 * k:32 * k + 32], pe_in[:, k, :, :].rearrange("p u d -> p (u d)")) for k in range(2)]
                     + [(bank[6][:, 128 + 16 * c:144 + 16 * c], meta_in[:, 128 * c:128 * c + 128]) for c in range(8)], turn_done)

            rope = {"k": 0}

            def permute(after):
                k = rope["k"]
                pe.wait_ge(*after)
                if k >= 2:
                    pe.wait_ge(sin_done, k - 1)
                mm(bank[4 + k % 2][:, 0:T1], E("rot"), xs[:, k % 2, :], start=True, stop=True).then_inc(perm_done, 1)
                rope["k"] += 1

            def compress(i):
                kv, half = i // 2, i % 2
                pe.wait_ge(blk_ready, 8 * kv + 8)
                pe.wait_ge(cmp_loaded[half], 16 * (kv + 1))
                w1 = cmp_w[:, half, :, :]
                for p in range(8 * half, 8 * half + 8):
                    for hc in range(2):
                        last = mm(bank[7 - kv][:, 60 * hc:60 * hc + 60], w1[:, p % 8, 128 * hc:128 * hc + 128],
                                  blkT[:, kv, p, :], start=p == 0 and hc == 0, stop=p == 15, skip_group_check=True)
                last.then_inc(cmp_hid, 1)

            m = 0
            for n in range(21):
                if n <= 12 and n % 2 == 0 or n > 12 and n % 2:
                    parts = split(m)
                    m += 1
                chunk(parts, 0 if n == 12 else n % 2 if n < 12 else (n - 13) % 2, KC, 48 if n == 12 else 128, T1,
                      (xl_ready, 0) if n == 0 else None)
                if n == 0:
                    sum_squares(0, T1, 0, 8)
                    turn_small()
                if n == 1:
                    pe.wait_ge(turn_taken, 9)
                if n >= 1 and is_roped(NSA[n - 1]):
                    permute((proj_taken, n))
                if n == 13:
                    pe.wait_ge(proj_taken, 12)
                    for w in range(2):
                        turn([(bank[6 + w][:, 256 * kb + 128 * j:256 * kb + 128 * j + 128],
                                      big1[:, 12 + 2 * w + j, 128 * kb:128 * kb + 128]) for kb in range(2) for j in range(2)],
                             vt_done)
                if n == 15:
                    pe.wait_ge(gate_moved, 1)
                    pe.wait_ge(vt_taken, 1)
                    turn([(bank[6][:, 48 * qb:48 * qb + 48], big1[0:48, 16, 128 * qb:128 * qb + 128]) for qb in range(2)],
                         vt_done)
                if n >= 14 and n % 2 == 0:
                    pe.wait_ge(vt_taken, 2 if n < 18 else 3)
                    compress((n - 14) // 2)
                if n == 18:
                    pe.wait_ge(cmp_act, 1)
                    pe.wait_ge(small_loaded, 16 * SMALL_DMAS)
                    for hc in range(2):
                        last = mm(bank[7][:, 0:60], w2k_sb[:, hc, :], hidT[:, 0, hc, :], start=hc == 0, stop=hc == 1)
                    last.then_inc(cmp_kv, 1)
            permute((proj_taken, 21))
            pe.wait_ge(proj_taken, 21)
            pe.wait_ge(cmp_kv_taken, 2)
            pe.wait_ge(roped, NSA_ROPED)

            def q_of(ci, qb):
                return big1[:, ci, 128 * qb:128 * qb + 128]

            for qb in range(2):
                for ci in range(8):
                    c, g = NCMP * (16 * qb + 2 * ci), ci // 2
                    last = mm(bank[2][:, c:c + 2 * NCMP].rearrange("p (a c) -> p a c", a=2), q_of(ci, qb),
                              kcT[:, :, NCMP * g:NCMP * g + NCMP], start=True, stop=True, skip_group_check=True)
            last.then_inc(cmp_scores, 1)

            def cmp_values():
                pe.wait_ge(cmp_act, 2)
                for g in range(4):
                    for hc in range(2):
                        last = mm(bank[7][0:NCMP, 64 * g:64 + 64 * g], hidT[:, 1, hc, NCMP * g:NCMP * g + NCMP],
                                  w2v_sb[:, hc, :], start=hc == 0, stop=hc == 1)
                last.then_inc(cmp_kv, 1)

            def cmp_turn():
                pe.wait_ge(cmp_probs, 1)
                pe.wait_ge(cmp_kv_taken, 6)
                for qb in range(2):
                    turn([(bank[6 + qb][:, 128 * hg:128 * hg + 128],
                                   c_p[:, 16 * qb + 4 * hg:16 * qb + 4 * hg + 4, :].rearrange("p h c -> p (h c)"))
                                  for hg in range(4)], cmp_turned)

            def unit_scores(v, u, nsa):
                ci, kind = u
                if v >= 2:
                    pe.wait_ge(at_exp, v - 1)
                if not nsa:
                    pe.wait_ge(roped, NSA_ROPED + ci + 2)
                S = bank[4 + v % 2]
                causal, before = mask_b[:, 128:256], mask_b[:, 0:128]
                if nsa:
                    ks = [[big1[:, K_AT + 2 * (4 * b + ci // 2) + a, :] for a in range(2)] for b in range(2)]
                    if kind == "first":
                        mm(S[:, :], ident_b[:, :], each(causal, 4), start=True, stop=False, skip_group_check=True)
                        for a in range(2):
                            for b in range(2):
                                o = 256 * a + 128 * b
                                last = mm(S[:, o:o + 128], q_of(ci, 0), ks[b][a][:, 0:128],
                                          start=False, stop=True, skip_group_check=True)
                    else:
                        a = int(kind[-1])
                        mm(S[:, :].rearrange("p (b k) -> p b k", b=2)[:, :, 128:256], ident_b[:, :], each(causal, 2),
                           start=True, stop=False, skip_group_check=True)
                        for b in range(2):
                            last = mm(S[:, 256 * b:256 * b + 256], q_of(ci, 1), ks[b][a],
                                      start=False, stop=True, skip_group_check=True)
                else:
                    k = [big1[:, K_AT + 2 * (ci // 4) + a, :] for a in range(2)]
                    if kind == "first":
                        mm(S[:, 0:256], ident_b[:, :], each(causal, 2), start=True, stop=False, skip_group_check=True)
                        for a in range(2):
                            last = mm(S[:, 128 * a:128 * a + 128], q_of(ci, 0), k[a][:, 0:128],
                                      start=False, stop=True, skip_group_check=True)
                    else:
                        mm(S[:, :], ident_b[:, :], each(mask_b[:, :], 2), start=True, stop=False, skip_group_check=True)
                        for a in range(2):
                            last = mm(S[:, 256 * a:256 * a + 256], q_of(ci, 1), k[a],
                                      start=False, stop=True, skip_group_check=True)
                last.then_inc(at_scores, 1)

            def unit_turn(v, u, nsa):
                pe.wait_ge(at_probs, v + 1)
                if v >= 2:
                    pe.wait_ge(at_pt, v - 1)
                n = 2 if not nsa and u[1] == "first" else 4
                turn([(bank[6 + v % 2][:, 128 * i:128 * i + 128], S_p[:, v % 3, 128 * i:128 * i + 128])
                         for i in range(n)], at_turned)

            def unit_pv(v, u, nsa, c0):
                ci, kind = u
                pe.wait_ge(at_pt, v + 1)
                if kind == "first" and c0 + ci >= 2:
                    pe.wait_ge(at_out, c0 + ci - 1)
                O = bank[out_bank(ci, nsa)]

                def piece(a, qb, i, w, kb, g, first=False):
                    return mm(O[64 * a:64 * a + 64, 128 * qb:128 * qb + 128], vtok[:, w, kb, 64 * g:64 * g + 64],
                              S_pt[:, v % 2, 128 * i:128 * i + 128], start=first, stop=True, skip_group_check=True)

                if nsa:
                    g = ci // 2
                    if kind == "first":
                        for a in range(2):
                            r = (2 * ci + a) % 4
                            mm(O[64 * a:64 * a + 64, 0:256], vc_rep[32 * r:32 * r + NCMP, 64 * g:64 * g + 64],
                               c_pt[32 * r:32 * r + NCMP, :, g, :], start=True, stop=False, skip_group_check=True)
                            for b in range(2):
                                last = piece(a, 0, 2 * a + b, b, 0, g)
                    else:
                        a = int(kind[-1])
                        for b in range(2):
                            for kb in range(2):
                                last = piece(a, 1, 2 * b + kb, b, kb, g)
                elif kind == "first":
                    for a in range(2):
                        last = piece(a, 0, a, 0, 0, ci // 4, first=True)
                else:
                    for a in range(2):
                        for kb in range(2):
                            last = piece(a, 1, 2 * a + kb, 0, kb, ci // 4)
                last.then_inc(at_pv, 1)

            def attention(units, v0, nsa, c0):
                for i in range(len(units) + 3):
                    if i < len(units):
                        unit_scores(v0 + i, units[i], nsa)
                    if nsa and i == 0:
                        cmp_values()
                    if nsa and i == 2:
                        cmp_turn()
                        pe.wait_ge(cmp_pt, 2)
                    if 2 <= i < len(units) + 2:
                        unit_turn(v0 + i - 2, units[i - 2], nsa)
                    if i >= 3:
                        unit_pv(v0 + i - 3, units[i - 3], nsa, c0)

            attention(NSA_UNITS, 0, True, 0)

            def out_proj(m0, ready, T, norm, K=KC, source=(xh, xl)):
                for c in range(8):
                    if c % (16 // K) == 0:
                        parts = split(m0 + c // (16 // K))
                    chunk(parts, c % (16 // K), K, 128, T, ready if c == 0 else None, source)
                    if norm is not None and c >= 2:
                        sum_squares(norm, T, c - 2, c - 1)
                if norm is not None:
                    sum_squares(norm, T, 6, 8)

            def ffn(l, T, norm):
                m0, n0 = ffn_at[l][1], N_FFN[l]
                assert line["n"] == n0, (line["n"], n0)
                pe.wait_ge(proj_taken, n0)

                def up(b, m, n, q0, stream=None):
                    pe.wait_ge(w_lo, m + 1)
                    parts = view(w_h, b, KC, 256), view(w_l, b, KC, 256)
                    for q in range(2):
                        pe.wait_ge(proj_taken, n + q - 3)
                        for k in range(KC):
                            if stream is not None and q == 0:
                                pe.wait_ge(xl_ready, 8 * stream + k + 1)
                            last = product(bank[q0 + q][:, 0:T], parts, k, slice(128 * q, 128 * q + 128), xh[:, k, 0:T],
                                           xl[:, k, 0:T], k == 0, k == KC - 1)
                        last.then_inc(proj_done, 1)

                up(m0 % 2, m0, n0, 0, STREAMS[norm - 1])
                up((m0 + 1) % 2, m0 + 1, n0 + 2, 2)
                with pe.Fori(0, (FC - 2) // 2) as i:
                    for j in range(2):
                        up((m0 + j) % 2, i * 2 + (m0 + 2 + j), i * 4 + (n0 + 4 + 2 * j), 2 * j)
                line["n"] += 2 * FC
                hh, hl = hidden(hid_h, T), hidden(hid_l, T)
                for g in range(2):
                    for part, (k0, k1) in enumerate(DOWN_PARTS):
                        parts = split(m0 + FC + len(DOWN_PARTS) * g + part)
                        pe.wait_ge(hidden_ready, FC * l + k1)
                        for c in range(4):
                            if part == 0 and (g == 0 or c == 3):
                                pe.wait_ge(proj_taken, line["n"] + c - 3)
                            for k in range(k0, k1):
                                last = product(bank[down_bank(44 + 4 * g + c)][:, 0:T], parts, k - k0, slice(128 * c, 128 * c + 128), hh[:, k, :],
                                               hl[:, k, :], k == 0, k == FC - 1)
                            if k1 == FC:
                                last.then_inc(proj_done, 1)
                        if k1 < FC:
                            last.then_inc(down_part, 1)
                        if g and part == 0:
                            sum_squares(norm, T, 0, 4)
                    line["n"] += 4
                sum_squares(norm, T, 4, 8)

            out_proj(11, (at_out, 0), T1, 1, source=(at_h, at_l))
            ffn(0, T1, 2)

            for n in range(10):
                if n % 2 == 0:
                    parts = split(M_SWA + n // 2)
                chunk(parts, n % 2, KC, 128, T1, (xl_ready, 8 * STREAMS[2]) if n == 0 else None)
                if n >= 1 and is_roped(SWA[n - 1]):
                    permute((biased, n))
                if n == 3:
                    pe.wait_ge(biased, 2)
                    turn([(bank[6][:, 128 * kb:128 * kb + 128], big1[:, 9, 128 * kb:128 * kb + 128]) for kb in range(2)],
                         vt_done)
            permute((biased, 10))
            pe.wait_ge(sin_done, NSA_ROPED + SWA_ROPED)
            pe.wait_ge(vt_taken, 4)
            pe.wait_ge(proj_taken, N_SWA + 10)
            attention(SWA_UNITS, V_SWA, False, 8)
            out_proj(M_SWA + 5, (at_out, 8), T1, 3, source=(at_h, at_l))
            ffn(1, T1, 4)

            sum_squares(5, T2, 0, 8)
            in2 = {}

            def project2(c0, c1):
                for c in range(c0, c1):
                    j = PAIR[c]
                    if j not in in2:
                        in2[j] = split(M_IN2 + j)
                    chunk(in2[j], 0 if c == 28 else c % 2 if c < 28 else (c - 29) % 2, KC, 16 if c == 28 else 128, T2,
                          (xl_ready, 8 * STREAMS[5]) if c == 0 else None)

            project2(0, 12)

            pe.wait_ge(proj_taken, N_IN2 + 12)
            for tb in range(3):
                w = min(128, T2 - 128 * tb)
                turn([(bank[4 + tb][0:w, 128 * c:128 * c + 128], big2[:, 8 + c, 128 * tb:128 * tb + w])
                              for c in range(4)], vt_done)
            pe.wait_ge(vt_taken, 4 + 3)
            pe.wait_ge(kpad_ready, 1)
            Z = bank[4:8]
            parts = [(0, 0, T2), (1, 272, 144), (2, 416, 16)]

            def z_score(i):
                if i >= 4:
                    pe.wait_ge(z_weights, i - 3)
                c, a = i // 2, i % 2
                for b, at, w in parts:
                    k = kpad[64 * a:64 * a + 64, c, :] if b == 2 else big2[64 * a:64 * a + 64, 4 + c, 128 * b:128 * b + 128]
                    last = mm(Z[i % 4][:, at:at + w], k, big2[64 * a:64 * a + 64, c, T2 - w:T2], start=b == 0, stop=True,
                              skip_group_check=True)
                last.then_inc(z_scores, 1)

            def z_sum(i):
                pe.wait_ge(z_soft, i + 1)
                for b, at, w in parts:
                    for b2, at2, w2 in parts[b:]:
                        last = mm(Z[i % 4][:, at + w - w2:at + w], L("tri") if b2 == b else L("all"),
                                  z_u[:, i % 2, at2:at2 + w2], start=False, stop=True, skip_group_check=True)
                mm(Z[i % 4][:, 0:ZW], ident_b[:, :], L("sbneg"), start=False, stop=True, skip_group_check=True)\
                    .then_inc(z_tri, 1)

            def z_value(i):
                pe.wait_ge(z_weights, i + 1)
                c, a = i // 2, i % 2
                if a == 0 and c >= 2:
                    pe.wait_ge(z_out, c - 1)
                for b, at, w in parts:
                    n = 16 if b == 2 else 128
                    last = mm(bank[2 + c % 2][64 * a:64 * a + 64, T2 - w:T2], sv_tok[0:n, b, 64 * i:64 * i + 64],
                              z_w[0:n, i % 2, at:at + w], start=b == 0, stop=True, skip_group_check=True)
                last.then_inc(z_pv, 1)

            for i in range(8 + 2):
                if i < 8:
                    z_score(i)
                if 1 <= i <= 8:
                    z_sum(i - 1)
                if i == 9:
                    project2(29, 31)
                if i >= 2:
                    z_value(i - 2)
                if i < 8:
                    project2(12 + 2 * i, 14 + 2 * i)
                if i == 8:
                    project2(28, 29)

            pe.wait_ge(proj_taken, N_IN2 + 29)
            pe.wait_ge(up_loaded, 16)
            for n in range(GN):
                last = mm(bank[4 + n][:, 0:T2], up_sb[0:16, 128 * n:128 * n + 128], glr[0:16, :], start=True, stop=True)
            last.then_inc(g_log, 1)
            for tb in range(3):
                if tb < 2:
                    project2(31 + 2 * tb, 33 + 2 * tb)
                w = min(128, T2 - 128 * tb)
                for half in range(2):
                    i = 2 * tb + half
                    pe.wait_ge(*((vt_taken, 7 + i - 1) if i >= 2 else (g_x, GN)))
                    turn([(bank[6 + i % 2][0:w, 128 * c:128 * c + 128], big2[:, 20 + 4 * half + c, 128 * tb:128 * tb + w])
                             for c in range(4)], vt_done)

            def level(lv):
                if lv == 0:
                    pe.wait_ge(g_x, GN)
                    pe.wait_ge(vt_taken, 7 + 6)
                    q, k = big2[:, 12:16, :], big2[:, 16:20, :]
                else:
                    pe.wait_ge(g_qk, lv)
                    q = g_q[:, lv % 2, :].rearrange("p (n t) -> p n t", n=GN)
                    k = g_k[:, lv % 2, :].rearrange("p (n t) -> p n t", n=GN)
                if lv >= 2:
                    pe.wait_ge(g_sel, lv - 1)
                for ck in range(2):
                    for n in range(GN):
                        last = mm(bank[2 + 2 * (lv % 2) + ck][:, 128 * n:128 * n + 128], k[:, n, 128 * ck:128 * ck + 128],
                                  q[:, n, 128 * ck:128 * ck + 128], start=True, stop=True, skip_group_check=True)
                if lv <= 4:
                    for n in range(GN):
                        last = mm(bank[6 + lv % 2][0:16, 16 * n:16 * n + 16], k[:, n, 256:T2], q[:, n, 256:T2],
                                  start=True, stop=True, skip_group_check=True)
                last.then_inc(g_att, 1)

            level(0)
            for lv in range(1, LEVELS + 1):
                if lv > 1:
                    project2(31 + 2 * lv, 33 + 2 * lv)
                level(lv)
            project2(47, 49)
            pe.wait_ge(k_dec, 1)
            for ck in range(2):
                turn([(bank[6 + ck][:, 128 * n:128 * n + 128],
                          g_k[:, 0, :].rearrange("p (n t) -> p n t", n=GN)[:, n, 128 * ck:128 * ck + 128])
                         for n in range(GN)], k_turned)
            pe.wait_ge(g_sel, LEVELS + 1)
            for ck in range(2):
                pe.wait_ge(k_tok, ck + 1)
                for n in range(GN):
                    last = mm(bank[2 + 2 * ck + n // 2][:, 256 * (n % 2):256 * (n % 2) + 256],
                              kdT[:, ck, 128 * n:128 * n + 128], gv_tok[:, ck, 256 * n:256 * n + 256],
                              start=True, stop=True, skip_group_check=True)
                last.then_inc(s_done, 1)
            pe.wait_ge(state2, GN)
            pe.wait_ge(q_dec, 1)
            for o in range(8):
                n, dv = o // 2, o % 2
                b = bank[2 + o % 4]
                if o >= 4:
                    pe.wait_ge(go_taken, o - 3)
                cols = slice(256 * n + 128 * dv, 256 * n + 128 * dv + 128)
                qt = g_q[:, 0, :].rearrange("p (n t) -> p n t", n=GN)
                mm(b[:, 0:128], gv_tok[:, 0, cols], att[:, 0, n, :], start=True, stop=True, skip_group_check=True)
                mm(b[:, 128:256], gv_tok[:, 1, cols], att[:, 1, n, :], start=False, stop=True, skip_group_check=True)
                mm(b[:, 128:256], s1[:, n, 128 * dv:128 * dv + 128], qt[:, n, 128:256], start=False, stop=True,
                   skip_group_check=True)
                mm(b[:, 256:T2], gv_tok[0:16, 2, cols], att2[0:16, n, :], start=False, stop=True, skip_group_check=True)
                mm(b[:, 256:T2], s2[:, n, 128 * dv:128 * dv + 128], qt[:, n, 256:T2], start=False, stop=True,
                   skip_group_check=True).then_inc(go_done, 1)
            project2(49, 51)
            pe.wait_ge(go_taken, 6)
            for n in range(GN):
                for dv in range(2):
                    pe.wait_ge(go_sq, 2 * n + dv + 1)
                    mm(bank[GO_NORM[n]][:, 0:T2], ones, sq[:, (2 * n + dv) % 4, :], start=dv == 0, stop=dv == 1).then_inc(go_ss, 1)

            project2(51, 53)
            out_proj(M_SBO, (z_out, 0), T2, None, K=4, source=(z_h, z_lo))
            out_proj(M_GLO, (go_ready, 0), T2, None, source=(go_h, go_l))
            out_proj(M_GLO + 4, (mix_ready, 0), T2, 6)
            sum_squares(7, T2, 0, 8)
            ffn(2, T2, 8)
            for half in range(2):
                pe.wait_ge(h2_even, 6 + 2 * half)
                pe.wait_ge(h2_odd, 6 + 2 * half)
                for tb in range(2):
                    i = 2 * tb + half
                    turn([(bank[i][:, 128 * c:128 * c + 128],
                              h2[:, 4 * half + c, META + 128 * tb:META + 128 * tb + 128]) for c in range(4)], y_turned)

        @block.scalar
        def _(act):
            line = Line(act, act_step)
            fn = nc.scalar.activation

            def high(m):
                n = split_at[m]
                act.wait_ge(raw_loaded[n % 2], loaded[n])
                if m >= 2:
                    act.wait_ge(*used[m - 2])
                size = sizes[n][0] * sizes[n][1]
                fn(w_h[:, m % 2, 0:size], raw[:, n % 2, 0:size], ACT.Copy).then_inc(w_hi, 1)
            act.dma_start(early[:, :], A["early_c"]).then_inc(early_loaded, 16)
            act.wait_ge(prepared, 1)
            act.dma_start(*gain_load).then_inc(gain_loaded, 16)
            high(0)
            def load_cmp(i):
                kv, half = i // 2, i % 2
                src = A["nsa_cmp_w1"][0][kv].rearrange("(k p) n -> p k n", p=128)[:, 8 * half:8 * half + 8, :]
                act.dma_start(cmp_w[:, half, :, :], src).then_inc(cmp_loaded[half], 16)

            def preload_root():
                fn(scrap[:, :], eps_col[:, 0:1], ACT.Sqrt)

            def squares(i, T, src, ready, after=None):
                for c in range(8):
                    if c == (4 if i in (2, 4, 8) else 0):
                        preload_root()
                    act.wait_ge(*ready(c))
                    if c >= 4:
                        act.wait_ge(ss_step, 8 * i + c - 3)
                    if c % 2 and i in STREAMS and i > 0:
                        line.put(fn(xh[:, c, 0:T], src[:, c, 0:T], ACT.Copy, scale=vec("g", 8 * i + c)), xh_odd)
                    line.put(fn(sq[:, c % 4, 0:T], src[:, c, 0:T], ACT.Square), sq_ready)
                    if after is not None:
                        after(c)
                act.wait_ge(ss_step, 8 * i + 8)
                line.put(fn(root[:, 0:T], bank[7][:, 0:T], ACT.Sqrt, bias=eps_col[:, 0:1]), root_ready)

            def taken(n0):
                return lambda c: (proj_taken, n0 + c + 1)

            act.wait_ge(turn_taken, 5)
            for c in range(1, 8, 2):
                line.put(fn(xh[:, c, 0:T1], xT[:, c, 0:T1], ACT.Copy, scale=vec("g", c)), xh_odd)
            high(1)
            squares(0, T1, xT, lambda c: (turn_taken, 5))
            w2 = [A["nsa_cmp_w2"][0][kv].rearrange("(c p) d -> p c d", p=128) for kv in range(2)]
            for dst, src in ((w2k_sb[:, :, 0:64], w2[0]), (w2k_sb[:, :, 64:128], w2[0]), (w2v_sb, w2[1])):
                act.dma_start(dst, src).then_inc(small_loaded, 16)
            act.dma_start(sinks, A["swa_sinks"][0].unsqueeze(0).broadcast_to([128, 16])).then_inc(small_loaded, 16)
            for m in range(2, 9):
                high(m)
                if m in (3, 5):
                    load_cmp((m - 3) // 2)
            for w in range(2):
                act.wait_ge(vt_done, w + 1)
                line.put(fn(vtok[:, w, :, :].rearrange("p a b -> p (a b)"), bank[6 + w][:, :], ACT.Copy), vt_taken)
            high(9)
            act.wait_ge(cmp_hid, 1)
            load_cmp(2)
            act.wait_ge(vt_done, 3)
            line.put(fn(egate.rearrange("p a b -> p (a b)"), bank[6][:, 0:96], ACT.Exp, scale=-1.0), vt_taken)
            high(10)

            def cmp_hidden(kv):
                act.wait_ge(cmp_hid, 2 * kv + 2)
                line.put(fn(hidT[:, kv, :, :].rearrange("p b c -> p (b c)"), bank[7 - kv][:, 0:120], ACT.Gelu_apprx_tanh), cmp_act)

            act.wait_ge(cmp_hid, 2)
            load_cmp(3)
            cmp_hidden(0)
            act.wait_ge(cmp_kv, 1)
            act.wait_ge(prepared, 5)
            for a in range(2):
                half = slice(64 * a, 64 * a + 64)
                line.put(fn(kcT[half, a, :], bank[7][half, 0:60], ACT.Copy), cmp_kv_taken)
            high(11)
            cmp_hidden(1)
            fn(scrap, eps_col[:, 0:1], ACT.Exp)
            act.wait_ge(cmp_kv, 2)
            for r in range(4):
                line.put(fn(vc_rep[32 * r:32 * r + NCMP, :], bank[7][0:NCMP, 0:256], ACT.Copy), cmp_kv_taken)

            def attention(units, v0, nsa, c0):
                for i in range(len(units) + 4):
                    if i < len(units):
                        v = v0 + i
                        first = units[i][1] == "first"
                        act.wait_ge(at_neg, v + 1)
                        if v >= 3:
                            act.wait_ge(at_turned, v - 2)
                        n, w = (4 if nsa else 2, 128) if first else (2, 256)
                        for k in range(n):
                            ins = fn(S_p[:, v % 3, w * k:w * k + w], bank[4 + v % 2][:, w * k:w * k + w], ACT.Exp,
                                     scale=SCALE, bias=st_neg[:, v % 3, k:k + 1], accum_out=st_den[:, v % 3, k:k + 1])
                        line.put(ins, at_exp)
                        if not nsa:
                            act.wait_ge(at_sink, v - v0 + 1)
                            line.put(fn(st_es[:, v % 3, 0:2], st_es[:, v % 3, 0:2], ACT.Exp), at_sinkexp)
                    if nsa and i == 0:
                        act.wait_ge(cmp_centered, 1)
                        line.put(fn(c_e, c_s, ACT.Exp, scale=SCALE), cmp_exp)
                    if nsa and i == 6:
                        high(12)
                    if nsa and i == 1:
                        for qb in range(2):
                            act.wait_ge(cmp_turned, qb + 1)
                            line.put(fn(c_pt[:, qb, :, :].rearrange("p a b -> p (a b)"), bank[6 + qb][:, :], ACT.Copy), cmp_pt)
                    j = i - 4
                    if j >= 0 and units[j][1] in ("second", "second1"):
                        act.wait_ge(at_pv, v0 + j + 1)
                        ci = units[j][0]
                        line.put(fn(at_h[:, ci, :], bank[out_bank(ci, nsa)][:, 0:256], ACT.Copy), at_high)

            attention(NSA_UNITS, 0, True, 0)
            squares(1, T1, xT, taken(N_NSA_O), lambda c: high(13 + c // 2) if c % 2 else None)

            def ffn(l, T, func):
                n0, m0 = ffn_at[l]

                def step(k, n, p, w0, b, slab, target, m, first):
                    act.wait_ge(proj_taken, n + 1)
                    if not first:
                        act.wait_ge(conv_mid, k - 1)
                    fn(f_c1[:, p, 0:T], f_a[:, p, 0:T], ACT.Identity, scale=w0, bias=b).then_inc(c1_ready, 1)
                    act.wait_ge(raw_loaded[slab], target)
                    act.wait_ge(proj_done, n + 2)
                    fn(w_h[:, m, :], raw[:, slab, :], ACT.Copy).then_inc(w_hi, 1)
                    act.wait_ge(conv_ready, k + 1)
                    if not first:
                        act.wait_ge(hid_full, k - 1)
                    fn(f_s[:, p, 0:T], f_c3[:, p, 0:T], func).then_inc(act_ready, 1)

                def tap(name, f):
                    at = vcolc[name][0]
                    if isinstance(f, int):
                        return vecs[:, 1 + l, at + f:at + f + 1]
                    return vecs[:, 1 + l, bass.ds(f + at, 1)]

                for f in range(2):
                    step(FC * l + f, N_FFN[l] + 2 * f, f, tap("w0", f), tap("b", f), (n0 + f) % 2, loaded[n0 + f + 2],
                         (m0 + f) % 2, l == 0)
                with act.Fori(0, (FC - 2) // 2) as i:
                    for j in range(2):
                        step(i * 2 + (FC * l + 2 + j), i * 4 + (N_FFN[l] + 4 + 2 * j), j, tap("w0", i * 2 + (2 + j)),
                             tap("b", i * 2 + (2 + j)), (n0 + j) % 2, i * 32 + loaded[n0 + 4 + j], (m0 + j) % 2, False)

            def down(l, i, T):
                m = ffn_at[l][1] + FC
                highs = lambda a, b: [high(m + x) for x in range(a, b) if m + x < len(split_at)]
                highs(2, 8)
                squares(i, T, xT, taken(N_FFN[l] + 44), lambda c: highs(8, 13) if c == 3 else None)
                highs(13, 14)

            act.dma_start(late_in, A["late_c"]).then_inc(late_loaded, 16)
            ffn(0, T1, ACT.Silu)
            down(0, 2, T1)
            rope = 0
            for n in range(10):
                place, r = SWA[n][0], is_roped(SWA[n])
                act.wait_ge(proj_taken, N_SWA + n + 1)
                t = xs[:, (NSA_ROPED + rope) % 2, :] if r else big1[:, place, :]
                line.put(fn(t, t, ACT.Identity, bias=vec("bqkv", 8 if n == 0 else 9 if n == 1 else n - 2)), biased)
                rope += r
                if n % 2:
                    high(M_SWA + 2 + n // 2)
                if n == 3:
                    act.wait_ge(vt_done, 4)
                    line.put(fn(vtok[:, 0, :, 0:128], bank[6][:, 0:256].rearrange("p (a b) -> p a b", a=2), ACT.Copy),
                             vt_taken)
            attention(SWA_UNITS, V_SWA, False, 8)
            squares(3, T1, xT, taken(N_SWA_O), lambda c: high(M_SWA + 7 + c // 2) if c % 2 else None)
            ffn(1, T1, ACT.Silu)
            down(1, 4, T1)
            squares(5, T2, h2, lambda c: (h2_ready, c + 1))
            for m in range(M_IN2 + 2, M_IN2 + 8):
                high(m)
            for tb in range(3):
                w = min(128, T2 - 128 * tb)
                act.wait_ge(vt_done, 5 + tb)
                line.put(fn(sv_tok[0:w, tb, :], bank[4 + tb][0:w, :], ACT.Copy), vt_taken)
            Z = bank[4:8]

            def z_final(i):
                act.wait_ge(z_tri, i + 1)
                if i >= 2:
                    act.wait_ge(z_pv, i - 1)
                line.put(fn(z_w[:, i % 2, :], Z[i % 4][:, 0:ZW], ACT.Exp, scale=SCALE), z_weights)

            def z_evac(i):
                if i % 2:
                    act.wait_ge(z_pv, i + 1)
                    line.put(fn(z_h[:, i // 2, :], bank[2 + (i // 2) % 2][:, 0:T2], ACT.Copy), z_high)

            for i in range(8):
                act.wait_ge(z_abs, i + 1)
                if i >= 2:
                    act.wait_ge(z_soft, i - 1)
                line.put(fn(z_l[:, i % 2, :], z_a[:, i % 2, :], ACT.Exp, scale=-SCALE))
                line.settle()
                line.put(fn(z_l[:, i % 2, :], z_l[:, i % 2, :], ACT.Ln, bias=1.0), z_ln)
                if i >= 1:
                    z_final(i - 1)
                if i >= 2:
                    z_evac(i - 2)
                high(M_IN2 + 8 + i)
            z_final(7)
            high(M_IN2 + 16)
            high(M_IN2 + 17)
            z_evac(7)
            act.wait_ge(g_abs, 1)
            ga = g_d[:, 1, :]
            line.put(fn(ga, ga, ACT.Exp, scale=-1.0))
            line.settle()
            line.put(fn(ga, ga, ACT.Ln, bias=1.0), g_ln)
            for i in range(6):
                tb, half = i // 2, i % 2
                if i == 2:
                    high(M_IN2 + 18)
                w = min(128, T2 - 128 * tb)
                act.wait_ge(vt_done, 8 + i)
                line.put(fn(gv_tok[0:w, tb, 512 * half:512 * half + 512], bank[6 + i % 2][0:w, :], ACT.Copy), vt_taken)
            for lv in range(1, LEVELS + 1):
                act.wait_ge(g_dist, lv)
                line.put(fn(g_d[:, lv % 2, :], g_d[:, lv % 2, :], ACT.Exp, scale=-1.0 / 16), g_decay)
                high(M_IN2 + 18 + lv)
            act.wait_ge(k_dist, 1)
            line.put(fn(g_d[:, 0, :], g_d[:, 0, :], ACT.Exp, scale=-1.0 / 16), k_decay)
            line.put(fn(cum, cum, ACT.Exp, scale=-1.0 / 16), q_decay)
            for ck in range(2):
                act.wait_ge(k_turned, ck + 1)
                line.put(fn(kdT[:, ck, :], bank[6 + ck][:, :], ACT.Copy), k_tok)
            high(M_IN2 + 26)
            act.wait_ge(s_done, 1)
            for half in range(2):
                ins = fn(s1[:, 2 * half:2 * half + 2, :].rearrange("p a b -> p (a b)"), bank[2 + half][:, :], ACT.Copy)
                if half:
                    line.put(ins, s_taken)
            act.wait_ge(proj_taken, N_IN2 + 37)
            t = big2[:, 28:36, :]
            line.put(fn(t, t, ACT.Silu), gate_ready)
            act.wait_ge(proj_taken, N_IN2 + 45)
            t = big2[:, 36:44, :]
            line.put(fn(t, t, ACT.Sigmoid), gate_ready)
            for o in range(8):
                act.wait_ge(go_taken, o + 1)
                if o == 4:
                    high(M_IN2 + 27)
                    preload_root()
                if o >= 4:
                    act.wait_ge(go_ss, o - 3)
                line.put(fn(sq[:, o % 4, :], g_o[:, o, :], ACT.Square), go_sq)
            rs = g_d[:, 1, :].rearrange("p (n t) -> p n t", n=GN)
            for n in range(GN):
                act.wait_ge(go_ss, 2 * n + 2)
                line.put(fn(rs[:, n, :], bank[GO_NORM[n]][:, 0:T2], ACT.Sqrt, scale=float(D // 256), bias=eps_col[:, 0:1]), go_root)

            def go_highs(a, b):
                for o in range(a, b):
                    act.wait_ge(go_full, o + 1)
                    line.put(fn(go_h[:, o, :], g_o[:, o, :], ACT.Copy), go_high)

            high(M_IN2 + 28)
            go_highs(0, 6)
            high(M_GLO)
            go_highs(6, 8)
            high(M_GLO + 1)
            act.wait_ge(proj_taken, N_IN2 + 53)
            t = big2[:, 44:52, :]
            line.put(fn(t, t, ACT.Sigmoid), gate_ready)
            for c in range(8):
                act.wait_ge(mix_full, c + 1)
                line.put(fn(xh[:, c, :], big2[:, 36 + c, :], ACT.Copy), mix_high)
                if c % 2:
                    high(M_GLO + 2 + c // 2)
            squares(6, T2, xT, taken(N_WO2), lambda c: high(M_GLO + 6 + c // 2) if c in (1, 3, 5) else None)
            high(M_GLO + 9)
            squares(7, T2, h2, lambda c: (h2_odd if c % 2 else h2_even, c // 2 + 1))
            ffn(2, T2, ACT.Gelu_apprx_tanh)
            down(2, 8, T2)
            o_sb = big[:, 0:2048].rearrange("p (b n) -> p b n", b=2)
            for k, i in enumerate((0, 2, 1, 3)):
                act.wait_ge(y_turned, k + 1)
                line.put(fn(o_sb[:, i // 2, 512 * (i % 2):512 * (i % 2) + 512], bank[i][:, :], ACT.Copy), y_taken)

        @block.vector
        def _(dve):
            line = Line(dve, dve_step)
            V = nc.vector

            def factor(i, T):
                dve.wait_ge(root_ready, i + 1)
                line.put(V.reciprocal(rstd[:, 0:T], root[:, 0:T]))
                line.settle()

            def low(m):
                n = split_at[m]
                size = sizes[n][0] * sizes[n][1]
                dve.wait_ge(w_hi, m + 1)
                V.tensor_tensor(w_l[:, m % 2, 0:size], raw[:, n % 2, 0:size], w_h[:, m % 2, 0:size].bitcast(F32), ALU.subtract)\
                    .then_inc(w_lo, 1)

            def stream_low(i, T, src, c):
                dve.wait_ge(xh_odd if c % 2 else xh_even, 4 * STREAMS[i] + c // 2 + 1)
                line.put(V.scalar_tensor_tensor(out=xl[:, c, 0:T], in0=src[:, c, 0:T], scalar=vec("g", 8 * i + c),
                                                in1=xh[:, c, 0:T].bitcast(F32), op0=ALU.mult, op1=ALU.subtract), xl_ready)

            def take(n, dst, M, T, signal=proj_taken):
                dve.wait_ge(proj_done, n + 1)
                line.put(V.tensor_tensor(dst, bank[bank_of(n)][0:M, 0:T], rstd[0:M, 0:T], ALU.mult), signal)

            for b in range(4):
                dve.wait_ge(turn_done, 1 + b)
                line.put(V.tensor_copy(xT[:, 2 * b:2 * b + 2, 0:T1], bank[b][:, :].rearrange("p (a b) -> p a b", a=2)),
                         turn_taken)
            dve.wait_ge(turn_done, 5)
            line.put(V.tensor_copy(vecs[:, 0, 0:KC], bank[4][:, 0:KC]), turn_taken)
            low(0)
            for c in range(8):
                stream_low(0, T1, xT, c)
            low(1)

            def small():
                dve.wait_ge(turn_done, 6)
                line.put(V.tensor_copy(vecs[:, 0, KC:128], bank[5][:, KC:128]), turn_taken)
                line.put(V.tensor_copy(vecs[:, 1:4, :], bank[5][:, 128:512].rearrange("p (a b) -> p a b", a=3)), turn_taken)
                dve.wait_ge(turn_done, 7)
                line.put(V.tensor_copy(pe_dup, bank[6][:, 0:64].rearrange("p (a b) -> p a b", a=2)), turn_taken)
                line.put(V.tensor_copy(h2[:, :, 0:META], bank[6][:, 128:256].rearrange("p (a b) -> p a b", a=8)), turn_taken)

            factor(0, T1)

            rope = {"k": 0}

            def rope_sin():
                k = rope["k"]
                dve.wait_ge(perm_done, k + 1)
                if k >= 2:
                    dve.wait_ge(roped, k - 1)
                line.put(V.tensor_tensor(tsin[:, k % 2, :], bank[4 + k % 2][:, 0:T1], E("sin"), ALU.mult), sin_done)
                rope["k"] += 1

            def projections(n0, table, each_after):
                k0 = rope["k"]
                seen = 0
                for i, entry in enumerate(table):
                    place, r = entry[0], is_roped(entry)
                    if r:
                        k = k0 + seen
                        if k >= 2:
                            dve.wait_ge(perm_done, k - 1)
                            dve.wait_ge(cos_done, k - 1)
                        dst, seen = xs[:, k % 2, :], seen + 1
                    else:
                        dst = big1[:, place, :]
                    if n0 == 0 and i == 12:
                        take(n0 + i, dst[0:48], 48, T1)
                    else:
                        take(n0 + i, dst, 128, T1)
                    if i >= 1 and is_roped(table[i - 1]):
                        rope_sin()
                    each_after(i)
                rope_sin()

            def nsa_extra(i):
                if i == 0:
                    small()
                if i < 12 and i % 2 or i >= 12 and i % 2 == 0:
                    m = i // 2 if i < 12 else 6 + (i - 12) // 2
                    if m + 2 <= 10:
                        low(m + 2)
                if i == 12:
                    line.settle()
                    line.put(V.tensor_scalar(big1[0:48, 16, :], big1[0:48, 16, :],
                                             vecs[0:48, 0, vcol0["gb"][0]:vcol0["gb"][0] + 1], None, ALU.add), gate_moved)
                if i in (8, 10):
                    kv = (i - 8) // 2
                    dve.wait_ge(roped, 2)
                    for a in range(2):
                        for par in range(2):
                            for lh in range(2):
                                src = big1[64 * a:64 * a + 64, 8 + 2 * kv:10 + 2 * kv, :]\
                                    .rearrange("p j (c l s) -> p j c l s", l=8, s=2)[:, :, lh:lh + NCMP, :, par]
                                dst = blkT[64 * par:64 * par + 64, kv, 8 * lh:8 * lh + 8, :]\
                                    .rearrange("p l (j a c) -> p a j c l", j=2, a=2)[:, a]
                                pos = pe_dup[64 * a:64 * a + 64, kv, 16 * lh:16 * lh + 16]\
                                    .rearrange("p (l s) -> p l s", s=2)[:, :, par]
                                pos = each(each(pos, NCMP), 2)
                                line.put(V.tensor_tensor(dst, src, pos, ALU.add), blk_ready)
                if i == 18:
                    dve.wait_ge(vt_taken, 3)
                    e = egate.rearrange("p a b -> p (a b)")
                    line.put(V.tensor_scalar(e, e, 1.0, None, ALU.add))
                    line.settle()
                    line.put(V.reciprocal(gates.rearrange("p a b -> p (a b)"), e), gates_ready)

            projections(0, NSA, nsa_extra)

            gate_of = gates.rearrange("p q (c a b) -> p q c a b", c=8, a=2)

            def cmp_softmax():
                dve.wait_ge(cmp_scores, 1)
                neg = E("cmpneg").rearrange("p (q c) -> p q c", q=2)
                line.put(V.tensor_tensor(c_s.rearrange("p (q h) c -> p q h c", q=2),
                                         bank[2][:, 0:480].rearrange("p (q h c) -> p q h c", q=2, h=16),
                                         each(neg, 16, axis=2), ALU.add))
                line.settle()
                line.put(V.tensor_reduce(c_mx, c_s, AX.X, ALU.max))
                line.settle()
                line.put(V.tensor_scalar(c_mx, c_mx, -1e20, None, ALU.max))
                line.settle()
                line.put(V.tensor_tensor(c_s, c_s, each(c_mx, NCMP, axis=2), ALU.subtract), cmp_centered)

            def cmp_norm():
                dve.wait_ge(cmp_exp, 1)
                dve.wait_ge(prepared, 3)
                line.put(V.tensor_reduce(c_den, c_e, AX.X, ALU.add))
                line.settle()
                line.put(V.tensor_scalar(c_den, c_den, 1e-6, None, ALU.max))
                line.settle()
                line.put(V.reciprocal(c_mx, c_den))
                line.settle()
                line.put(V.tensor_tensor(c_den.rearrange("p (q h) -> p q h", q=2), c_mx.rearrange("p (q h) -> p q h", q=2),
                                         gates.rearrange("p q (h b) -> p q h b", b=3)[:, :, :, 0], ALU.mult))
                line.settle()
                line.put(V.tensor_tensor(c_p[:, :, 0:NCMP], c_e, each(c_den, NCMP, axis=2), ALU.mult), cmp_probs)

            def attention_low(ci, c0, nsa):
                dve.wait_ge(at_high, c0 + ci + 1)
                line.put(V.tensor_tensor(at_l[:, ci, :], bank[out_bank(ci, nsa)][:, 0:T1], at_h[:, ci, :].bitcast(F32), ALU.subtract),
                         at_out)

            def attention(units, v0, nsa, c0):
                def factors(i):
                    if 1 <= i <= len(units):
                        v = v0 + i - 1
                        ci, kind = units[i - 1]
                        n = 4 if nsa and kind == "first" else 2
                        dve.wait_ge(at_exp, v + 1)
                        if v >= 3:
                            dve.wait_ge(at_probs, v - 2)
                        den, r = st_den[:, v % 3, 0:n], st_r[:, v % 3, 0:n]
                        if nsa:
                            line.put(V.reciprocal(r, den))
                            line.settle()
                            g = gate_of[:, 0 if kind == "first" else 1, ci]
                            if kind == "first":
                                line.put(V.tensor_tensor(r.rearrange("p (a b) -> p a b", a=2), r.rearrange("p (a b) -> p a b", a=2),
                                                         g[:, :, 1:3], ALU.mult), at_r)
                            else:
                                line.put(V.tensor_tensor(r, r, g[:, int(kind[-1]), 1:3], ALU.mult), at_r)
                        else:
                            dve.wait_ge(at_sinkexp, v - v0 + 1)
                            line.put(V.tensor_tensor(den, den, st_es[:, v % 3, 0:2], ALU.add))
                            line.settle()
                            line.put(V.reciprocal(r, den), at_r)

                for i in range(len(units) + 5):
                    if 3 <= i < len(units) + 3:
                        v = v0 + i - 3
                        n = 256 if not nsa and units[i - 3][1] == "first" else 512
                        dve.wait_ge(at_turned, v + 1)
                        if v >= 2:
                            dve.wait_ge(at_pv, v - 1)
                        line.put(V.tensor_copy(S_pt[:, v % 2, 0:n], bank[6 + v % 2][:, 0:n]), at_pt)
                    if nsa:
                        factors(i)
                    if i < len(units):
                        v = v0 + i
                        ci, kind = units[i]
                        n, w = (4 if nsa else 2, 128) if kind == "first" else (2, 256)
                        dve.wait_ge(at_scores, v + 1)
                        line.put(V.tensor_reduce(st_mx[:, v % 3, 0:n], bank[4 + v % 2][:, 0:n * w].rearrange("p (n w) -> p n w", n=n),
                                                 AX.X, ALU.max))
                        line.settle()
                        if nsa:
                            line.put(V.tensor_scalar(st_neg[:, v % 3, 0:n], st_mx[:, v % 3, 0:n], -SCALE, None, ALU.mult), at_neg)
                        else:
                            ns = nsinks.rearrange("p (c a) -> p c a", a=2)[:, ci, :]
                            line.put(V.scalar_tensor_tensor(out=st_neg[:, v % 3, 0:2], in0=st_mx[:, v % 3, 0:2], scalar=-SCALE,
                                                            in1=ns, op0=ALU.mult, op1=ALU.min), at_neg)
                            line.settle()
                            line.put(V.tensor_tensor(st_es[:, v % 3, 0:2], st_neg[:, v % 3, 0:2], ns, ALU.subtract), at_sink)
                    if nsa and i == 0:
                        cmp_softmax()
                        cmp_norm()
                    if nsa and i == 8:
                        low(12)
                    if not nsa:
                        factors(i)
                    if i >= 5 and units[i - 5][1] in ("second", "second1"):
                        attention_low(units[i - 5][0], c0, nsa)

            low(11)
            attention(NSA_UNITS, 0, True, 0)

            def add_chunk(n0, c, bias=None):
                n = n0 + c
                dve.wait_ge(proj_done, n + 1)
                if bias is None:
                    line.put(V.tensor_tensor(xT[:, c, 0:T1], bank[bank_of(n)][:, 0:T1], xT[:, c, 0:T1], ALU.add), proj_taken)
                else:
                    line.put(V.scalar_tensor_tensor(out=xT[:, c, 0:T1], in0=bank[bank_of(n)][:, 0:T1], scalar=vec(bias, c),
                                                    in1=xT[:, c, 0:T1], op0=ALU.add, op1=ALU.add), proj_taken)

            def add_residual(n0, bias, norm, after):
                for c in range(8):
                    add_chunk(n0, c, bias)
                    if c >= 1:
                        stream_low(norm, T1, xT, c - 1)
                    if c < 7:
                        after(c)
                stream_low(norm, T1, xT, 7)
                after(7)

            add_residual(N_NSA_O, None, 1, lambda c: low(13 + c // 2) if c % 2 else None)
            factor(1, T1)

            def ffn(l, T):
                def tap(name, f):
                    at = vcolc[name][0]
                    if isinstance(f, int):
                        return vecs[:, 1 + l, at + f:at + f + 1]
                    return vecs[:, 1 + l, bass.ds(f + at, 1)]

                n0, m0 = ffn_at[l]

                def step(k, n, b, p, f, slab, m, mb, first):
                    dve.wait_ge(proj_done, n + 1)
                    if not first:
                        dve.wait_ge(c1_ready, k - 1)
                    V.tensor_tensor(f_a[:, p, 2:2 + T], bank[b][:, 0:T], rstd[:, 0:T], ALU.mult).then_inc(proj_taken, 1)
                    dve.wait_ge(proj_done, n + 2)
                    if not first:
                        dve.wait_ge(hid_full, k - 1)
                    V.tensor_tensor(f_u[:, p, 0:T], bank[b + 1][:, 0:T], rstd[:, 0:T], ALU.mult).then_inc(proj_taken, 1)
                    dve.wait_ge(proj_taken, n + 2)
                    dve.wait_ge(c1_ready, k + 1)
                    V.scalar_tensor_tensor(out=f_c2[:, p, 0:T], in0=f_a[:, p, 1:1 + T], scalar=tap("w1", f),
                                           in1=f_c1[:, p, 0:T], op0=ALU.mult, op1=ALU.add).then_inc(conv_mid, 1)
                    dve.wait_ge(conv_mid, k + 1)
                    if not first:
                        dve.wait_ge(act_ready, k - 1)
                    V.scalar_tensor_tensor(out=f_c3[:, p, 0:T], in0=f_a[:, p, 2:2 + T], scalar=tap("w2", f),
                                           in1=f_c2[:, p, 0:T], op0=ALU.mult, op1=ALU.add).then_inc(conv_ready, 1)
                    dve.wait_ge(w_hi, m + 1)
                    V.tensor_tensor(w_l[:, mb, :], raw[:, slab, :], w_h[:, mb, :].bitcast(F32), ALU.subtract).then_inc(w_lo, 1)

                for f in range(2):
                    step(FC * l + f, N_FFN[l] + 2 * f, 2 * f, f, f, (n0 + f) % 2, m0 + f + 2, (m0 + f) % 2, l == 0)
                with dve.Fori(0, (FC - 2) // 2) as i:
                    for j in range(2):
                        step(i * 2 + (FC * l + 2 + j), i * 4 + (N_FFN[l] + 4 + 2 * j), 2 * j, j, i * 2 + (2 + j),
                             (n0 + j) % 2, i * 2 + (m0 + 4 + j), (m0 + j) % 2, False)
                line.skip(proj_taken, 2 * FC)
                line.skip(conv_ready, FC)

            def down(l, put, norm=None):
                m0 = ffn_at[l][1]
                def lows(a, b):
                    for m in range(m0 + FC + a, min(m0 + FC + b, len(split_at))):
                        low(m)

                lows(2, 7)
                for c in range(4):
                    put(c)
                lows(7, 8)
                if norm is not None:
                    for c in range(4):
                        stream_low(norm, T1, xT, c)
                lows(8, 13)
                for c in range(4, 8):
                    put(c)
                    if norm is not None and c > 4:
                        stream_low(norm, T1, xT, c - 1)
                if norm is not None:
                    stream_low(norm, T1, xT, 7)
                    lows(13, 14)

            V.memset(f_a[:, :, 0:2], 0.0)
            ffn(0, T1)
            down(0, lambda c: add_chunk(N_FFN[0] + 44, c), 2)
            factor(2, T1)
            projections(N_SWA, SWA, lambda i: low(M_SWA + 2 + i // 2) if i % 2 else None)
            dve.wait_ge(small_loaded, 16 * SMALL_DMAS)
            line.put(V.tensor_scalar(nsinks, sinks, -1.0, None, ALU.mult))
            line.settle()
            attention(SWA_UNITS, V_SWA, False, 8)
            add_residual(N_SWA_O, "bo", 3, lambda c: low(M_SWA + 7 + c // 2) if c % 2 else None)
            factor(3, T1)
            V.memset(f_a[:, :, 0:2], 0.0)
            ffn(1, T1)
            down(1, lambda c: add_chunk(N_FFN[1] + 44, c))
            factor(4, T1)
            for c in range(8):
                line.put(V.scalar_tensor_tensor(out=h2[:, c, META:T2], in0=xT[:, c, 0:T1], scalar=vec("g", 8 * 4 + c),
                                                in1=rstd[:, 0:T1], op0=ALU.mult, op1=ALU.mult), h2_ready)
                if c >= 1:
                    stream_low(5, T2, h2, c - 1)
            stream_low(5, T2, h2, 7)
            low(M_IN2 + 1)
            factor(5, T2)

            def take2(c0, c1, split=True):
                for c in range(c0, c1):
                    n = N_IN2 + c
                    if c == 28:
                        take(n, glr[0:16, :], 16, T2)
                    elif 12 <= c < 16:
                        dve.wait_ge(proj_done, n + 1)
                        line.put(V.scalar_tensor_tensor(out=big2[:, c, :], in0=bank[bank_of(n)][:, 0:T2], scalar=GDK ** -0.5,
                                                        in1=rstd[:, :], op0=ALU.mult, op1=ALU.mult), proj_taken)
                    else:
                        take(n, big2[:, place2(c), :], 128, T2)
                    if split and PAIR[c] != PAIR.get(c + 1):
                        low(M_IN2 + 2 + PAIR[c])

            take2(0, 12)

            def z_low(c):
                dve.wait_ge(z_high, c + 1)
                line.put(V.tensor_tensor(z_lo[:, c, :], bank[2 + c % 2][:, 0:T2], z_h[:, c, :].bitcast(F32), ALU.subtract), z_out)

            Z = bank[4:8]
            for i in range(8):
                dve.wait_ge(z_scores, i + 1)
                if i >= 2:
                    dve.wait_ge(z_ln, i - 1)
                    dve.wait_ge(z_soft, i - 1)
                z = Z[i % 4][:, 0:ZW]
                line.put(V.tensor_scalar(z_r[:, i % 2, :], z, 0.0, SCALE, ALU.max, ALU.mult), z_relu)
                line.settle()
                line.put(V.scalar_tensor_tensor(out=z_a[:, i % 2, :], in0=z_r[:, i % 2, :], scalar=2.0 / SCALE, in1=z,
                                                op0=ALU.mult, op1=ALU.subtract), z_abs)
                if i:
                    low(M_IN2 + 7 + i)
                take2(12 + 2 * i, 14 + 2 * i, split=False)
                if i >= 3 and i % 2:
                    z_low(i // 2 - 1)
            low(M_IN2 + 15)
            take2(28, 31)
            z_low(3)
            dve.wait_ge(g_log, 1)
            gx = g_q[:, 0, :].rearrange("p (n t) -> p n t", n=GN)
            dve.wait_ge(z_pv, 8)
            for n in range(GN):
                line.put(V.tensor_scalar(gx[:, n, :], bank[4 + n][:, 0:T2], vec("bgk", n), None, ALU.add), g_x)
            line.settle()
            line.put(V.tensor_scalar(g_q[:, 1, :], g_q[:, 0, :], -1.0, 0.0, ALU.mult, ALU.max))
            line.settle()
            line.put(V.scalar_tensor_tensor(out=g_d[:, 1, :], in0=g_q[:, 1, :], scalar=2.0, in1=g_q[:, 0, :],
                                            op0=ALU.mult, op1=ALU.add), g_abs)
            take2(31, 33, split=False)
            dve.wait_ge(g_ln, 1)
            line.put(V.tensor_tensor(g_q[:, 0, :], g_q[:, 1, :], g_d[:, 1, :], ALU.add))
            dve.wait_ge(prepared, 7)
            line.settle()
            line.put(V.tensor_tensor_scan(cum.rearrange("p n t -> p (n t)"), g_k[:, 0, :], g_q[:, 0, :], 0.0, ALU.mult, ALU.add),
                     g_cum)
            line.settle()
            low(M_IN2 + 18)

            def distance(lv):
                b = 1 << (lv - 1)
                if lv >= 3:
                    dve.wait_ge(g_qk, lv - 2)
                d = g_d[:, lv % 2, :].rearrange("p (n t) -> p n t", n=GN)
                if b <= 8:
                    cf = cum.rearrange("p n t -> p (n t)").rearrange("p (q h b) -> p q h b", h=2, b=b)
                    df = g_d[:, lv % 2, :].rearrange("p (q h b) -> p q h b", h=2, b=b)
                    pairs = [(df, cf)]
                else:
                    pairs = [(d[:, n, 0:256].rearrange("p (q h b) -> p q h b", h=2, b=b),
                              cum[:, n, 0:256].rearrange("p (q h b) -> p q h b", h=2, b=b)) for n in range(GN)]
                for x, (dd, cc) in enumerate(pairs):
                    border = cc[:, :, 0, b - 1:b]
                    border = border.broadcast_to([128, border.shape[1], b])
                    line.put(V.tensor_tensor(dd[:, :, 1, :], cc[:, :, 1, :], border, ALU.subtract))
                    line.put(V.tensor_tensor(dd[:, :, 0, :], border, cc[:, :, 0, :], ALU.subtract),
                             g_dist if x == len(pairs) - 1 else None)

            def select(lv):
                dve.wait_ge(g_att, lv + 1)
                m = L("gla")[:, 128 * lv:128 * lv + 128]
                tiles = [(att[:, ck, :, :], bank[2 + 2 * (lv % 2) + ck][:, :].rearrange("p (n t) -> p n t", n=GN), m, 128)
                         for ck in range(2)]
                if lv <= 4:
                    tiles.append((att2[0:16, :, :], bank[6 + lv % 2][0:16, 0:64].rearrange("p (n t) -> p n t", n=GN),
                                  m[0:16, 0:16], 16))
                line.settle()
                for x, (dst, src, mask, w) in enumerate(tiles):
                    sig = g_sel if x == len(tiles) - 1 else None
                    if lv == 0:
                        line.put(V.tensor_tensor(dst, src, each(mask, GN), ALU.mult), sig)
                    else:
                        line.put(V.copy_predicated(dst, each(mask.bitcast(U16), GN), src), sig)

            line.settle()
            dve.wait_ge(late_loaded, 16)
            for lv in range(LEVELS + 1):
                if lv < LEVELS:
                    distance(lv + 1)
                if lv >= 1:
                    low(M_IN2 + 18 + lv)
                select(lv)
                if lv < LEVELS:
                    take2(33 + 2 * lv, 35 + 2 * lv, split=False)
            d = g_d[:, 0, :].rearrange("p (n t) -> p n t", n=GN)
            dve.wait_ge(g_qk, LEVELS)
            for ck in range(2):
                end = cum[:, :, 128 * ck + 127:128 * ck + 128].broadcast_to([128, GN, 128])
                line.put(V.tensor_tensor(d[:, :, 128 * ck:128 * ck + 128], end, cum[:, :, 128 * ck:128 * ck + 128], ALU.subtract),
                         k_dist if ck else None)
            take2(47, 49)
            dve.wait_ge(s_taken, 1)
            dve.wait_ge(q_decay, 1)
            dve.wait_ge(s_done, 2)
            for n in range(GN):
                line.put(V.scalar_tensor_tensor(out=s2[:, n, :], in0=s1[:, n, :], scalar=cum[:, n, 255:256],
                                                in1=bank[4 + n // 2][:, 256 * (n % 2):256 * (n % 2) + 256],
                                                op0=ALU.mult, op1=ALU.add), state2)
            for o in range(8):
                dve.wait_ge(go_done, o + 1)
                line.put(V.tensor_copy(g_o[:, o, :], bank[2 + o % 4][:, 0:T2]), go_taken)
            take2(49, 51)
            rs = g_d[:, 1, :].rearrange("p (n t) -> p n t", n=GN)

            def sb_gate(c0, c1):
                for c in range(c0, c1):
                    n = N_SBO + c
                    dve.wait_ge(proj_done, n + 1)
                    t = big2[:, 36 + c, :]
                    line.put(V.tensor_tensor(t, bank[bank_of(n)][:, 0:T2], t, ALU.mult), proj_taken)

            for n in range(GN):
                dve.wait_ge(go_root, n + 1)
                line.put(V.reciprocal(rs[:, n, :], rs[:, n, :]))
                line.settle()
                for dv in range(2):
                    o = g_o[:, 2 * n + dv, :]
                    line.put(V.scalar_tensor_tensor(out=o, in0=o, scalar=vec("hn", dv), in1=rs[:, n, :], op0=ALU.mult, op1=ALU.mult),
                             go_normed)
                if n == 1:
                    take2(51, 53, split=False)
                    dve.wait_ge(gate_ready, 2)
                elif n == 2:
                    sb_gate(0, 2)
                    low(M_IN2 + 28)
                    sb_gate(2, 4)
            sb_gate(4, 6)
            low(M_GLO)
            sb_gate(6, 8)
            low(M_GLO + 1)
            dve.wait_ge(gate_ready, 3)

            def mix_low(c):
                dve.wait_ge(mix_high, c + 1)
                line.put(V.tensor_tensor(xl[:, c, :], big2[:, 36 + c, :], xh[:, c, :].bitcast(F32), ALU.subtract), mix_ready)

            for c in range(8):
                n = N_GLO + c
                dve.wait_ge(proj_done, n + 1)
                line.put(V.tensor_tensor(g_tmp[:, c % 2, :], bank[bank_of(n)][:, 0:T2], big2[:, 44 + c, :], ALU.mult), proj_taken)
                line.settle()
                line.put(V.tensor_tensor(big2[:, 36 + c, :], big2[:, 36 + c, :], g_tmp[:, c % 2, :], ALU.add), mix_full)
                if c:
                    mix_low(c - 1)
                if c in (1, 3, 5):
                    low(M_GLO + 2 + c // 2)
            mix_low(7)
            low(M_GLO + 5)

            def copy_chunk(n0, c):
                n = n0 + c
                dve.wait_ge(proj_done, n + 1)
                line.put(V.tensor_copy(xT[:, c, :], bank[bank_of(n)][:, 0:T2]), proj_taken)

            def add_normed(i, norm=None):
                factor(i, T2)
                done = 4 * (i == 8)
                for c in range(8):
                    if c >= 4 and c % 2 == 0:
                        dve.wait_ge(h2_even, done + c // 2 - 1)
                    line.put(V.scalar_tensor_tensor(out=g_tmp[:, c % 4, :], in0=xT[:, c, :], scalar=vec("g", 8 * i + c),
                                                    in1=rstd[:, :], op0=ALU.mult, op1=ALU.mult), normed)
                    if c % 2:
                        line.settle()
                        line.put(V.tensor_tensor(h2[:, c, :], h2[:, c, :], g_tmp[:, c % 4, :], ALU.add), h2_odd)
                    if norm is not None and c >= 2:
                        stream_low(norm, T2, h2, c - 2)
                if norm is not None:
                    stream_low(norm, T2, h2, 6)
                    stream_low(norm, T2, h2, 7)

            for c in range(8):
                copy_chunk(N_WO2, c)
                if c in (1, 3, 5):
                    low(M_GLO + 6 + c // 2)
            add_normed(6, 7)
            low(M_GLO + 9)
            V.memset(f_a[:, :, 0:2], 0.0)
            factor(7, T2)
            ffn(2, T2)
            down(2, lambda c: copy_chunk(N_FFN[2] + 44, c))
            add_normed(8)

        @block.gpsimd
        def _(pool):
            line = Line(pool, pool_step)
            G = nc.gpsimd
            G.memset(eps_col[:, :], EPS)
            line.put(G.memset(vec_in, 0.0), prepared)
            pool.wait_ge(early_loaded, 16)
            G.tensor_copy(ident_b[:, :], ident)
            G.tensor_copy(mask_b[:, 0:128], E("before"))
            line.put(G.tensor_copy(mask_b[:, 128:256], E("causal")), prepared)

            def gains(i, T, src, ready):
                for c in range(0, 8, 2):
                    pool.wait_ge(*ready(c))
                    line.put(G.tensor_scalar(xh[:, c, 0:T], src[:, c, 0:T], vec("g", 8 * i + c), None, ALU.mult), xh_even)

            def taken(n0):
                return lambda c: (proj_taken, n0 + c + 1)

            gains(0, T1, xT, lambda c: (turn_taken, 5))
            rope = {"k": 0}

            def ropes(table, ready):
                for i, (place, r) in enumerate(table):
                    if not r and place != "k":
                        continue
                    k = rope["k"]
                    pool.wait_ge(*ready(i))
                    line.put(G.tensor_tensor(tcos[:, k % 2, :], xs[:, k % 2, :], E("cos"), ALU.mult), cos_done)
                    pool.wait_ge(sin_done, k + 1)
                    line.settle()
                    if place != "k":
                        line.put(G.tensor_tensor(big1[:, place, :], tcos[:, k % 2, :], tsin[:, k % 2, :], ALU.add), roped)
                    else:
                        for g in range(2):
                            for a in range(2):
                                half = slice(64 * g, 64 * g + 64)
                                line.put(G.tensor_tensor(big1[64 * a:64 * a + 64, K_AT + 2 * (r + g) + a, :],
                                                         tcos[half, k % 2, :], tsin[half, k % 2, :], ALU.add),
                                         roped if g and a else None)
                                line.settle()
                    rope["k"] += 1

            line.put(G.memset(c_p, 0.0), prepared)
            line.put(G.memset(big1[:, K_AT:K_AT + 16, :], 0.0), prepared)
            line.put(G.memset(kcT, 0.0), prepared)
            line.settle()
            ropes(NSA, lambda i: (proj_taken, i + 1))

            def attention(units, v0, nsa):
                for i, (ci, kind) in enumerate(units):
                    v = v0 + i
                    n, w = (4 if nsa else 2, 128) if kind == "first" else (2, 256)
                    pool.wait_ge(at_r, v + 1)
                    p = S_p[:, v % 3, 0:n * w].rearrange("p (n w) -> p n w", n=n)
                    r = st_r[:, v % 3, 0:n].unsqueeze(2).broadcast_to([128, n, w])
                    line.put(G.tensor_tensor(p, p, r, ALU.mult), at_probs)

            attention(NSA_UNITS, 0, True)
            gains(1, T1, xT, taken(N_NSA_O))

            def ffn(l, T):
                hh, hl = (hidden(v, T).rearrange("p f t -> p (f t)") for v in (hid_h, hid_l))

                def step(k, n, p, at):
                    pool.wait_ge(proj_taken, n + 2)
                    pool.wait_ge(act_ready, k + 1)
                    G.tensor_tensor(f_h[:, p, 0:T], f_s[:, p, 0:T], f_u[:, p, 0:T], ALU.mult).then_inc(hid_full, 1)
                    pool.wait_ge(hid_full, k + 1)
                    G.tensor_copy(hh[:, at], f_h[:, p, 0:T]).then_inc(hid_high, 1)
                    pool.wait_ge(hid_high, k + 1)
                    G.tensor_tensor(hl[:, at], f_h[:, p, 0:T], hh[:, at].bitcast(F32), ALU.subtract).then_inc(hidden_ready, 1)

                for f in range(2):
                    step(FC * l + f, N_FFN[l] + 2 * f, f, slice(f * T, f * T + T))
                with pool.Fori(0, (FC - 2) // 2) as i:
                    for j in range(2):
                        step(i * 2 + (FC * l + 2 + j), i * 4 + (N_FFN[l] + 4 + 2 * j), j, bass.ds(i * (2 * T) + (2 + j) * T, T))
                line.skip(hidden_ready, FC)

            ffn(0, T1)
            gains(2, T1, xT, taken(N_FFN[0] + 44))
            pool.wait_ge(late_loaded, 16)
            G.tensor_copy(tri_all[:, :], late_in[:, 0:256])
            line.put(G.tensor_copy(late_b[:, :], late_in[:, 256:ln]), prepared)
            pool.wait_ge(proj_done, N_FFN[0] + 52)
            line.put(G.memset(big1[:, K_AT:K_AT + 4, :], 0.0))
            line.settle()
            ropes(SWA, lambda i: (biased, i + 1))
            attention(SWA_UNITS, V_SWA, False)
            gains(3, T1, xT, taken(N_SWA_O))
            ffn(1, T1)
            gains(5, T2, h2, lambda c: (h2_ready, c + 1))
            pool.wait_ge(proj_taken, N_IN2 + 8)
            G.dma_start(up_sb[0:16, :], A["w_gk_up_2"][0]).then_inc(up_loaded, 16)
            line.put(G.memset(kpad, 0.0))
            line.settle()
            line.put(G.tensor_copy(kpad[:, :, 0:16], big2[:, 4:8, 256:T2]), kpad_ready)
            for i in range(8):
                pool.wait_ge(z_ln, i + 1)
                pool.wait_ge(z_relu, i + 1)
                if i >= 2:
                    pool.wait_ge(z_tri, i - 1)
                line.put(G.tensor_tensor(z_u[:, i % 2, :], z_l[:, i % 2, :], z_r[:, i % 2, :], ALU.add))
                line.settle()
                line.put(G.tensor_tensor(z_u[:, i % 2, :], z_u[:, i % 2, :], L("sbvalid"), ALU.mult), z_soft)
            pool.wait_ge(z_pv, 8)
            line.put(G.memset(g_k[:, 0, :], 1.0))
            line.settle()
            line.put(G.memset(g_k[:, 0, :].rearrange("p (n t) -> p n t", n=GN)[:, :, 0:T2:128], 0.0), prepared)
            pool.wait_ge(g_cum, 1)
            for v in (g_q, g_k):
                line.put(G.memset(v, 0.0))
            line.settle()
            for lv in range(1, LEVELS + 1):
                b = 1 << (lv - 1)
                pool.wait_ge(g_decay, lv)
                if lv >= 2:
                    pool.wait_ge(g_att, lv - 1)

                def split(v, n=None):
                    v = v if n is None else v[:, T2 * n:T2 * n + 256]
                    return v.rearrange("p (q h b) -> p q h b", h=2, b=b)

                d = g_d[:, lv % 2, :]
                q, k = big2[:, 12:16, :].rearrange("p n t -> p (n t)"), big2[:, 16:20, :].rearrange("p n t -> p (n t)")
                for n in ([None] if b <= 8 else range(GN)):
                    line.put(G.tensor_tensor(split(g_q[:, lv % 2, :], n)[:, :, 1, :], split(q, n)[:, :, 1, :],
                                             split(d, n)[:, :, 1, :], ALU.mult))
                    line.put(G.tensor_tensor(split(g_k[:, lv % 2, :], n)[:, :, 0, :], split(k, n)[:, :, 0, :],
                                             split(d, n)[:, :, 0, :], ALU.mult), g_qk if n in (None, GN - 1) else None)

            def by_head(v):
                return v.rearrange("p (n t) -> p n t", n=GN)

            pool.wait_ge(k_decay, 1)
            pool.wait_ge(g_att, LEVELS)
            line.put(G.tensor_tensor(by_head(g_k[:, 0, :])[:, :, 0:256], big2[:, 16:20, 0:256], by_head(g_d[:, 0, :])[:, :, 0:256],
                                     ALU.mult), k_dec)
            pool.wait_ge(q_decay, 1)
            line.put(G.tensor_tensor(by_head(g_q[:, 0, :])[:, :, 128:T2], big2[:, 12:16, 128:T2], cum[:, :, 128:T2], ALU.mult),
                     q_dec)
            def go_low(o):
                pool.wait_ge(go_high, o + 1)
                line.put(G.tensor_tensor(go_l[:, o, :], g_o[:, o, :], go_h[:, o, :].bitcast(F32), ALU.subtract), go_ready)

            pool.wait_ge(gate_ready, 1)
            for o in range(8):
                pool.wait_ge(go_normed, o + 1)
                line.put(G.tensor_tensor(g_o[:, o, :], g_o[:, o, :], big2[:, 28 + o, :], ALU.mult), go_full)
                if o:
                    go_low(o - 1)
            go_low(7)

            def add_even(i, c):
                pool.wait_ge(normed, 8 * (i == 8) + c + 1)
                line.put(G.tensor_tensor(h2[:, c, :], h2[:, c, :], g_tmp[:, c % 4, :], ALU.add), h2_even)
                return h2_even, 4 * (i == 8) + c // 2 + 1

            gains(7, T2, h2, lambda c: add_even(6, c))
            ffn(2, T2)
            for c in range(0, 8, 2):
                add_even(8, c)
    return nc


_INS = ["x", "nsa_w_in", "nsa_cmp_pe", "nsa_cmp_w1", "nsa_cmp_w2", "nsa_gate_b", "nsa_w_o", "swa_w_qkv", "swa_b_qkv",
        "swa_sinks", "swa_w_o", "swa_b_o", "ffn_w_gu", "ffn_conv_w", "ffn_conv_b", "ffn_w_down", "norm_mix", "norm_ffn",
        "norm_final", "meta_tokens_2", "norm_mix_pre_2", "w_in_2", "w_gk_up_2", "b_gk_2", "gla_head_norm_2", "w_sb_out_2",
        "w_gla_out_2", "w_o_2", "norm_mix_post_2", "norm_ffn_pre_2", "w_ffn_up_2", "w_ffn_gate_2", "conv_w_2", "conv_b_2",
        "w_ffn_down_2", "norm_ffn_post_2"]


def kernel(**inputs):
    import numpy as _np
    import concourse.bacc as _bacc
    from concourse import mybir as _mybir
    from concourse.bass_utils import run_bass_kernel_spmd as _run

    nc = _bacc.Bacc("TRN2", target_bir_lowering=False, num_devices=1)
    arrays, aps = {}, {}
    e, l = constants()
    for name, a in [(n, inputs[n]) for n in _INS] + [("early_c", e), ("late_c", l)]:
        a = _np.ascontiguousarray(a)
        arrays[f"in_{name}"] = a
        aps[name] = nc.dram_tensor(f"in_{name}", a.shape, _mybir.dt.from_np(a.dtype), kind="ExternalInput").ap()
    out = nc.dram_tensor("out_0", (1, SEQ, D), _mybir.dt.float32, kind="ExternalOutput").ap()
    build(nc, aps, out)
    r = _run(nc, [arrays], core_ids=[0])
    return r.results[0]["out_0"]
```
